# Optimizing a Trainium2 kernel written in Bass

```python
import math
import jax, jax.numpy as jnp
from jax import lax
import numpy as np

D_MODEL = 4096
BATCH = 1
SEQ = 256
DEPTH = 1

HEAD_DIM = 128
ATTN_HEADS = D_MODEL // (2 * HEAD_DIM)
DN_HEADS = D_MODEL // (2 * HEAD_DIM)
ATTN_WIDTH = ATTN_HEADS * HEAD_DIM
DN_WIDTH = DN_HEADS * HEAD_DIM
MIX_WIDTH = ATTN_WIDTH + DN_WIDTH
DILATED_PATTERNS = ((128, 1), (512, 4), (2048, 16))
ATTN_BLOCK = 128
CONV_WIDTH = 4
DN_CHUNK = 64
NORM_EPS = 1e-6
L2_EPS = 1e-6
IN_SPLITS = tuple(int(c) for c in np.cumsum([ATTN_WIDTH] * 4 + [DN_WIDTH] * 4 + [DN_HEADS]))
IN_WIDTH = 4 * ATTN_WIDTH + 4 * DN_WIDTH + 2 * DN_HEADS

kernel_name = "hybrid_dilated_attn_gated_deltanet_layer"

def rms_norm(x, g):
    xf = x.astype(jnp.float32)
    y = xf * lax.rsqrt(jnp.mean(xf * xf, axis=-1, keepdims=True) + NORM_EPS)
    return (y * g.astype(jnp.float32)).astype(x.dtype)

def alibi_slopes(n_heads):
    start = 2.0 ** (-8.0 / n_heads)
    return jnp.asarray(np.array([start ** (i + 1) for i in range(n_heads)], dtype=np.float32))

def dilated_window_attention(q, k, v, slopes, window, dilation):
    B, S, H, Dh = q.shape
    L = ATTN_BLOCK
    reach = window // dilation
    M = S // dilation
    nb = -(-M // L)
    Mp = nb * L

    def to_blocks(t):
        t = t.reshape(B, M, dilation, H, Dh)
        t = jnp.pad(t, ((0, 0), (0, Mp - M), (0, 0), (0, 0), (0, 0)))
        return t.reshape(B, nb, L, dilation, H, Dh)

    def with_prev(t):
        prev = jnp.pad(t, ((0, 0), (1, 0), (0, 0), (0, 0), (0, 0), (0, 0)))[:, :-1]
        return jnp.concatenate([prev, t], axis=2)

    qb = to_blocks(q)
    kk = with_prev(to_blocks(k))
    vv = with_prev(to_blocks(v))
    scores = jnp.einsum('bnqrhd,bnkrhd->bnrhqk', qb, kk,
                        preferred_element_type=jnp.float32) * (Dh ** -0.5)
    qi = jnp.arange(L)[:, None]
    kj = jnp.arange(2 * L)[None, :]
    dist = qi + L - kj
    key_pos = (jnp.arange(nb)[:, None, None] - 1) * L + kj[None]
    valid = (dist >= 0)[None] & (dist <= reach)[None] & (key_pos >= 0)
    bias = -slopes[:, None, None] * (dist * dilation).astype(jnp.float32)[None]
    scores = jnp.where(valid[None, :, None, None], scores + bias, -jnp.inf)
    lse = jax.nn.logsumexp(scores, axis=-1)
    p = jnp.exp(scores - lse[..., None])
    out = jnp.einsum('bnrhqk,bnkrhd->bnqrhd', p.astype(v.dtype), vv)
    out = out.reshape(B, Mp, dilation, H, Dh)[:, :M].reshape(B, S, H, Dh)
    lse = jnp.transpose(lse, (0, 1, 4, 2, 3)).reshape(B, Mp, dilation, H)[:, :M].reshape(B, S, H)
    return out, lse

def causal_short_conv(x, w):
    K = w.shape[0]
    S = x.shape[1]
    xp = jnp.pad(x, ((0, 0), (K - 1, 0), (0, 0)))
    return sum(xp[:, j:j + S] * w[j] for j in range(K))

def l2_normalize(x):
    return x * lax.rsqrt(jnp.sum(x * x, axis=-1, keepdims=True) + L2_EPS)

def gated_delta_rule(q, k, v, beta, g):
    B, S, H, Dk = q.shape
    Dv = v.shape[-1]
    C = DN_CHUNK
    N = S // C
    q = q * (Dk ** -0.5)

    def chunks(t):
        t = jnp.moveaxis(t, 2, 1)
        return t.reshape((B, H, N, C) + t.shape[3:])

    q, k, v, beta, g = chunks(q), chunks(k), chunks(v), chunks(beta), chunks(g)
    gc = jnp.cumsum(g, axis=-1)
    incl = jnp.tril(jnp.ones((C, C), dtype=bool))
    strict = jnp.tril(jnp.ones((C, C), dtype=bool), k=-1)
    decay = jnp.exp(jnp.where(incl, gc[..., :, None] - gc[..., None, :], -jnp.inf))
    kb = k * beta[..., None]
    a_strict = jnp.where(strict, jnp.einsum('bhnid,bhnjd->bhnij', kb, k) * decay, 0.0)
    eye = jnp.eye(C, dtype=jnp.float32)
    rhs = jnp.concatenate([v * beta[..., None], kb * jnp.exp(gc)[..., None]], axis=-1)
    sol = lax.linalg.triangular_solve(a_strict + eye, rhs, left_side=True, lower=True,
                                      unit_diagonal=True)
    u, w = sol[..., :Dv], sol[..., Dv:]
    attn_intra = jnp.einsum('bhnid,bhnjd->bhnij', q, k) * decay
    q_dec = q * jnp.exp(gc)[..., None]
    k_tail = k * jnp.exp(gc[..., -1:] - gc)[..., None]
    chunk_decay = jnp.exp(gc[..., -1])

    def step(state, xs):
        w_c, u_c, q_c, k_c, a_c, d_c = xs
        v_new = u_c - jnp.einsum('bhcd,bhde->bhce', w_c, state)
        o_c = jnp.einsum('bhcd,bhde->bhce', q_c, state) + jnp.einsum('bhij,bhje->bhie', a_c, v_new)
        state = state * d_c[..., None, None] + jnp.einsum('bhcd,bhce->bhde', k_c, v_new)
        return state, o_c

    xs = tuple(jnp.moveaxis(t, 2, 0) for t in (w, u, q_dec, k_tail, attn_intra, chunk_decay))
    state0 = jnp.zeros((B, H, Dk, Dv), dtype=jnp.float32)
    _, o = lax.scan(step, state0, xs)
    o = jnp.moveaxis(o, 0, 2).reshape(B, H, S, Dv)
    return jnp.moveaxis(o, 1, 2)

def setup_inputs(seed: int = 0) -> dict:
    key = jax.random.key(seed)
    ks = jax.random.split(key, 10)
    x = jax.random.normal(ks[0], (BATCH, SEQ, D_MODEL), dtype=jnp.float32)
    norm_g = 1.0 + 0.02 * jax.random.normal(ks[1], (DEPTH, D_MODEL), dtype=jnp.float32)
    w_in = jax.random.normal(ks[2], (DEPTH, D_MODEL, IN_WIDTH), dtype=jnp.float32) * D_MODEL ** -0.5
    conv_w = jax.random.normal(ks[3], (DEPTH, CONV_WIDTH, 3 * DN_WIDTH), dtype=jnp.float32) * CONV_WIDTH ** -0.5
    a_log = jnp.log(jax.random.uniform(ks[4], (DEPTH, DN_HEADS), minval=1.0, maxval=16.0))
    dt = jnp.exp(jax.random.uniform(ks[5], (DEPTH, DN_HEADS), minval=math.log(1e-3), maxval=math.log(1e-1)))
    dt_bias = dt + jnp.log(-jnp.expm1(-dt))
    dn_norm_g = 1.0 + 0.02 * jax.random.normal(ks[6], (DEPTH, HEAD_DIM), dtype=jnp.float32)
    w_out = jax.random.normal(ks[7], (DEPTH, MIX_WIDTH, D_MODEL), dtype=jnp.float32) * MIX_WIDTH ** -0.5
    final_norm_g = 1.0 + 0.02 * jax.random.normal(ks[8], (D_MODEL,), dtype=jnp.float32)
    return {"x": x, "norm_g": norm_g, "w_in": w_in, "conv_w": conv_w, "a_log": a_log,
            "dt_bias": dt_bias, "dn_norm_g": dn_norm_g, "w_out": w_out,
            "final_norm_g": final_norm_g}

def reference(x, norm_g, w_in, conv_w, a_log, dt_bias, dn_norm_g, w_out, final_norm_g):
    B, S, _ = x.shape
    slopes = alibi_slopes(ATTN_HEADS)
    h = x
    for layer in range(DEPTH):
        u = rms_norm(h, norm_g[layer])
        proj = u @ w_in[layer]
        aq, ak, av, ag, dq, dk, dv, dg, b_logit, a_logit = jnp.split(proj, IN_SPLITS, axis=-1)

        to_heads = lambda t: t.reshape(B, S, ATTN_HEADS, HEAD_DIM)
        qh, kh, vh = to_heads(aq), to_heads(ak), to_heads(av)
        outs, lses = [], []
        for window, dilation in DILATED_PATTERNS:
            o_p, lse_p = dilated_window_attention(qh, kh, vh, slopes, window, dilation)
            outs.append(o_p)
            lses.append(lse_p)
        mix_w = jax.nn.softmax(jnp.stack(lses, axis=0), axis=0)
        attn = jnp.einsum('pbsh,pbshd->bshd', mix_w, jnp.stack(outs, axis=0).astype(jnp.float32))
        attn = attn.reshape(B, S, ATTN_WIDTH).astype(x.dtype) * jax.nn.silu(ag)

        qkv = jax.nn.silu(causal_short_conv(jnp.concatenate([dq, dk, dv], axis=-1), conv_w[layer]))
        cq, ck, cv = jnp.split(qkv.astype(jnp.float32), 3, axis=-1)
        to_dn = lambda t: t.reshape(B, S, DN_HEADS, HEAD_DIM)
        q_dn = l2_normalize(to_dn(cq))
        k_dn = l2_normalize(to_dn(ck))
        v_dn = to_dn(cv)
        beta = jax.nn.sigmoid(b_logit.astype(jnp.float32))
        g = -jnp.exp(a_log[layer]) * jax.nn.softplus(a_logit.astype(jnp.float32) + dt_bias[layer])
        o_dn = gated_delta_rule(q_dn, k_dn, v_dn, beta, g)
        o_dn = rms_norm(o_dn, dn_norm_g[layer]).reshape(B, S, DN_WIDTH).astype(x.dtype) * jax.nn.silu(dg)

        mixed = jnp.concatenate([attn, o_dn], axis=-1)
        h = h + mixed @ w_out[layer]
    return rms_norm(h, final_norm_g)


_drawn_inputs = setup_inputs


def setup_inputs(seed=0):
    import zlib

    import numpy as np

    out = dict(_drawn_inputs(seed))
    spreads = {}
    factors = {'norm_g': 4.044, 'dn_norm_g': 56.769, 'final_norm_g': 22.569}
    for name, (base, spread) in spreads.items():
        noise = np.random.default_rng([zlib.crc32(name.encode()), seed]).standard_normal(out[name].shape)
        drawn = base * np.exp(spread * noise) if base else spread * noise
        out[name] = __import__('jax').numpy.asarray(drawn.astype(out[name].dtype))
    for name, factor in factors.items():
        out[name] = (out[name] * factor).astype(out[name].dtype)
    return out
```

```python
from contextlib import ExitStack

import numpy as np

import concourse.bass as bass
from concourse import mybir

F32 = mybir.dt.float32
F32R = mybir.dt.float32r
ACT = mybir.ActivationFunctionType
ALU = mybir.AluOpType
AX = mybir.AxisListType

P = 128
SEQ = 256
T = SEQ // P
D = 4096
KT = D // P
HEADS = 16
WIDTH = HEADS * P
QH = 4
GC = QH * P
QUADS = HEADS // QH
COL = {"aq": 0, "ak": WIDTH, "av": 2 * WIDTH, "ag": 3 * WIDTH,
       "dq": 4 * WIDTH, "dk": 5 * WIDTH, "dv": 6 * WIDTH, "dg": 7 * WIDTH}
LOGITS = 8 * WIDTH
TAPS = 4
LEVELS = 7
SMALL = 5
EPS = 1e-6
NEG = -1.0e30
BODY = 4 * KT
RAW = 4
RING = 4
AHEAD = 3
NG = D // GC
XCUT = (0, 256, 1024, 2048, D)
M_AT = (0, 1) + tuple(range(QH, KT, QH))

C_ID, C_TRI, C_CAUSAL, C_YM = 0, 128, 256, 384
C_DIST = C_YM + LEVELS * 64
C_LOGN = C_DIST + 384
C_SLOPE = C_LOGN + 384
C_ALL = C_SLOPE + HEADS


def constant_table():
    c = np.zeros((P, C_ALL), np.float32)
    p = np.arange(P)[:, None]
    f = np.arange(P)[None, :]
    c[:, C_ID:C_ID + P] = p == f
    c[:, C_TRI:C_TRI + P] = p <= f
    c[:, C_CAUSAL:C_CAUSAL + P] = np.where(p <= f, 0.0, NEG)
    n = np.arange(64)[None, :]
    for lv in range(LEVELS):
        s = 1 << lv
        c[:, C_YM + 64 * lv:C_YM + 64 * lv + 64] = (p // (2 * s) == n // s) & (p % (2 * s) >= s)
    dist = np.concatenate([p - f, P + p - np.arange(SEQ)[None, :]], axis=1)
    count = np.zeros(dist.shape)
    for window, dilation in ((128, 1), (512, 4), (2048, 16)):
        count += (dist >= 0) & (dist <= window) & (dist % dilation == 0)
    c[:, C_DIST:C_DIST + 384] = -np.where(count > 0, dist, 0)
    c[:, C_LOGN:C_LOGN + 384] = np.where(count > 0, np.log(np.maximum(count, 1)), NEG)
    start = 2.0 ** (-8.0 / HEADS)
    c[:, C_SLOPE:] = np.array([start ** (i + 1) for i in range(HEADS)], np.float32)
    return c


def hybrid_layer(nc, x, norm_g, w_in, conv_w, a_log, dt_bias, dn_norm_g, w_out, final_norm_g,
                 consts, out):
    with ExitStack() as ctx:
        def sb(name, shape, dt=F32):
            return ctx.enter_context(nc.sbuf_tensor(name, shape, dt))

        def sem(name):
            return ctx.enter_context(nc.semaphore(name))

        u_hi = sb("u_hi", [P, KT, SEQ], F32R)
        u_lo = sb("u_lo", [P, KT, SEQ], F32R)
        mixedT = sb("mixedT", [P, KT, SEQ])
        w_raw = sb("w_raw", [P, RAW, 2, GC])
        w_hi = sb("w_hi", [P, RING, GC], F32R)
        w_lo = sb("w_lo", [P, RING, GC], F32R)
        cst = sb("cst", [P, C_ALL])
        mix = sb("mix", [P, 17920])
        quad_all = sb("quad_all", [P, QUADS, 32])
        conv_all = sb("conv_all", [P, QUADS, 48])
        qp = sb("qp", [P, 32])
        cw = sb("cw", [P, 48])
        ngT = sb("ngT", [P, KT + 1])
        rstd = sb("rstd", [P, 2])
        half = sb("half", [P, 32])
        stat = sb("stat", [P, 16])
        fac = sb("fac", [P, 16])
        negmax = sb("negmax", [P, 8])
        esum = sb("esum", [P, 8])
        rinv = sb("rinv", [P, 8])
        slope4 = sb("slope4", [P, QH])
        hsum = sb("hsum", [P, T, NG])

        ident = cst[:, C_ID:C_ID + P]
        tri = cst[:, C_TRI:C_TRI + P]
        causal = cst[:, C_CAUSAL:C_CAUSAL + P]

        def region(at, n):
            return mix[:, at:at + n]

        rawk, rawq, rawv, gate = (region(1024 * i, 1024) for i in range(4))
        f_k, f_q, f_v = (region(4096 + 1024 * i, 1024) for i in range(3))
        t_k, t_q, t_v = (region(7168 + 1024 * i, 1024) for i in range(3))
        XX = region(10240, 1024)
        XT = region(11264, 1024)
        decay = region(12288, 1024)
        Sst = region(13312, 512)
        Yb = region(13824, 512)
        yv = region(14336, 1024)
        Rb = region(15360, 512)
        QS = region(15872, 512)
        ktail = region(16384, 512)
        sq = region(16896, 1024)
        o_dn = t_q
        AT = f_v
        prob = region(10240, 1536)
        bias = region(7168, 1536)
        pT = region(12288, 1536)
        o_at = yv
        xin = region(0, 8192)
        wba = region(8192, 1024)
        junk = region(9216, 2048)
        cvr = region(11264, 256)
        ngr = region(11520, 128)
        lg = region(11648, 64)
        alog = region(11712, 16)
        dtb = region(11728, 16)
        zz = region(11744, 64)
        spa = region(11808, 32)
        spb = region(11840, 32)
        spc = region(11872, 32)
        ones = region(11904, 128)
        ssx = region(12032, 16)
        lgT = region(12288, SEQ)
        ba_hi = w_hi[:, 2:4, :].rearrange("p r n -> p (r n)")
        ba_lo = w_lo[:, 2:4, :].rearrange("p r n -> p (r n)")
        hbuf = region(0, 8192)
        gfin = region(8192, 4096)

        def by_h(ap, n=P):
            return ap.rearrange("p (h n) -> p h n", n=n)

        def pair(s):
            return lambda ap, half_: ap.rearrange("p h (b two s) -> p h b two s", two=2, s=s)[:, :, :, half_, :]

        proj = [[ctx.enter_context(nc.psum_tensor(f"proj{b}{t}", [P, GC], F32)) for t in range(T)]
                for b in range(2)]
        B = [ctx.enter_context(nc.psum_tensor(f"B{i}", [P, GC], F32)) for i in range(4)]

        ident_in, ng_in, consts_in, small_in, wba_in = (sem(n) for n in ("ident_in", "ng_in", "consts_in", "small_in", "wba_in"))
        x_in = [sem(f"x_in{i}") for i in range(len(XCUT) - 1)]
        w_in_ring = [sem(f"w_landed{i}") for i in range(RAW)]
        hi_ready, lo_ready, tile_used = sem("hi_ready"), sem("lo_ready"), sem("tile_used")
        chunks_asked = sem("chunks_asked")
        evac0, evac1 = sem("evac0"), sem("evac1")
        S = {n: sem(n) for n in (
            "pre_ng", "pre_ngc", "xT", "uhi", "ulo", "xsq", "xss", "rstd_ok", "half_ok", "cvT", "cv_ok",
            "lg_p", "ba_hi", "ba_lo", "lgT", "lg_t", "pre_v", "pre_a", "pre_p", "gc_p", "par_ok", "par_a",
            "fT", "bT", "kqT", "gcrow", "kk", "qk", "aT", "yp", "zp", "xtp", "y0p", "o0p", "ksp", "y1p", "o1p", "mT",
            "qp_ok", "tap3", "conv", "silu", "tok", "sqr", "red", "fac_ok", "scaled", "kq_ev", "v_ok",
            "ktail_ok", "gsub", "gmin", "gexp", "at_ok", "qkt_ok", "x_id", "y_ok", "x_ok", "xt_v", "xt_a", "y0_ok", "s_ok", "o0_ok",
            "r_mul", "r_ok", "qs_ok", "y1_ok", "o_ok", "silu_g", "gated", "osq", "ored", "ofac", "onorm", "mix_ok",
            "akT", "a_ev", "sl_ok", "bias_ok", "bias1", "sc", "logit", "amax", "aexp", "arin", "pTp", "pT_ok", "pv", "ao_ok",
            "a_silu", "agated", "amT", "amix_ok",
            "m_hi", "m_lo", "h_in", "gf_in", "h_add", "h_sq", "h_g", "h_fin_a", "h_fin_v", "y_out", "h_red", "h_mean", "h_rstd", "h_gl", "pow_in", "pow_k", "pool_waits")}

        tokens = x.rearrange("b (t p) d -> p (b t) d", p=P)
        out_tokens = out.rearrange("b (t p) d -> p (b t) d", p=P)
        w_in_r = w_in.rearrange("a (k p) n -> p (a k) n", p=P)
        w_out_r = w_out.rearrange("a (k p) n -> p (a k) n", p=P)

        block = ctx.enter_context(nc.Block())

        @block.sync
        def _(sp):
            def chunk(src, n, slot, first):
                if not first:
                    sp.wait_ge(lo_ready, 2 * n - 2 * RAW + 2)
                    sp.sem_inc(chunks_asked)
                sp.dma_start(w_raw[:, slot], src).then_inc(w_in_ring[slot], 16)

            def quad_groups(names, q, base):
                for i, name in enumerate(names):
                    col = COL[name] + q * GC if isinstance(q, int) else sp.snap(COL[name] + q * GC)
                    for c in range(KT // 2):
                        src = w_in_r[:, 2 * c:2 * c + 2, bass.ds(col, GC)]
                        first = isinstance(q, int) and i == 0 and c < RAW and base == 0
                        chunk(src, (q * 4 + i) * (KT // 2) + base + c, c % RAW, first)

            quad_groups(("dk", "dq", "dv", "dg"), 0, 0)
            with sp.Fori(1, QUADS) as q:
                quad_groups(("dk", "dq", "dv", "dg"), q, 0)
            with sp.Fori(0, QUADS) as q:
                quad_groups(("ak", "aq", "av", "ag"), q, QUADS * 4 * KT // 2)
            with sp.Fori(0, NG) as j:
                col = sp.snap(j * GC)
                for c in range(KT // 2):
                    tile = 2 * c + KT // 2 if c < KT // 4 else 2 * c - KT // 2
                    src = w_out_r[:, tile:tile + 2, bass.ds(col, GC)]
                    chunk(src, j * (KT // 2) + 2 * QUADS * 4 * KT // 2 + c, c % RAW, False)
            for t in range(T):
                for j in range(4):
                    sp.wait_ge(S["h_fin_v" if j > 1 else "h_fin_a"], 2 * t + j % 2 + 1)
                    sp.dma_start(out_tokens[:, t, 1024 * j:1024 * j + 1024],
                                 hbuf[:, 4096 * t + 1024 * j:4096 * t + 1024 * j + 1024]).then_inc(S["y_out"], 16)
            sp.wait_ge(S["y_out"], 16 * 4 * T)

        @block.tensor
        def _(pe):
            def bank_free(group):
                pe.wait_ge(evac0, group - 2)
                pe.wait_ge(evac1, group - 2)

            def run_step(n, k, bank):
                pe.wait_ge(lo_ready, n + 1)
                r = k % RING
                for t in range(T):
                    tk = slice(t * P, t * P + P)
                    o = proj[bank][t][:, :]
                    nc.tensor.matmul(o, u_hi[:, k, tk], w_hi[:, r], start=(k == 0), stop=False)
                    nc.tensor.matmul(o, u_hi[:, k, tk], w_lo[:, r], start=False, stop=False)
                    mm = nc.tensor.matmul(o, u_lo[:, k, tk], w_hi[:, r], start=False, stop=(k == KT - 1))
                mm.then_inc(tile_used, 1)

            def turn(dst, src):
                for h in range(QH):
                    mm = nc.tensor.transpose(dst[:, h * P:h * P + P], src(h), ident)
                return mm

            def to_features(src, banks):
                for h in range(QH):
                    for t in range(T):
                        mm = nc.tensor.transpose(B[banks + h // 2][:, (h % 2) * SEQ + t * P:(h % 2) * SEQ + t * P + P],
                                                 src[:, t * GC + h * P:t * GC + h * P + P], ident)
                return mm

            def to_tokens(src, banks):
                for t in range(T):
                    for h in range(QH):
                        mm = nc.tensor.transpose(B[banks + t][:, h * P:h * P + P],
                                                 src[:, h * SEQ + t * P:h * SEQ + t * P + P], ident)
                return mm

            def mms(dst, lhs, rhs, n=P):
                for h in range(QH):
                    mm = nc.tensor.matmul(dst[:, h * n:h * n + n], lhs(h), rhs(h), start=True, stop=True)
                return mm

            def hs(ap, c=0, n=P):
                return lambda h: ap[:, c + h * n:c + h * n + n]

            def fs(ap, t):
                return lambda h: ap[:, h * SEQ + t * P:h * SEQ + t * P + P]

            def turned(m, lv, c):
                if lv < SMALL:
                    pe.wait_ge(S["xt_v"], 2 * SMALL * m + 2 * lv + c + 1)
                else:
                    pe.wait_ge(S["xt_a"], 2 * (LEVELS - SMALL) * m + 2 * (lv - SMALL) + c + 1)

            def dn(m, s):
                if s == 0:
                    pe.wait_ge(evac0, 4 * m + 1)
                    pe.wait_ge(evac1, 4 * m + 1)
                    to_features(rawk, 0).then_inc(S["fT"], 1)
                if s == 4:
                    pe.wait_ge(evac0, 4 * m + 2)
                    pe.wait_ge(evac1, 4 * m + 2)
                    to_features(rawq, 2).then_inc(S["fT"], 1)
                if s == 10:
                    pe.wait_ge(S["silu"], 3 * m + 1)
                    to_tokens(f_k, 0).then_inc(S["bT"], 1)
                if s == 16:
                    pe.wait_ge(S["silu"], 3 * m + 2)
                    to_tokens(f_q, 2).then_inc(S["bT"], 1)
                if s == 20:
                    pe.wait_ge(S["scaled"], 2 * m + 1)
                    to_features(t_k, 0).then_inc(S["kqT"], 1)
                if s == 23:
                    pe.wait_ge(S["kq_ev"], 4 * m + 2)
                    pe.wait_ge(evac0, 4 * m + 3)
                    pe.wait_ge(evac1, 4 * m + 3)
                    to_features(rawv, 0).then_inc(S["fT"], 1)
                if s == 25:
                    pe.wait_ge(S["scaled"], 2 * m + 2)
                    to_features(t_q, 2).then_inc(S["kqT"], 1)
                if s == 28:
                    pe.wait_ge(S["kq_ev"], 4 * m + 4)
                    for c in range(T):
                        for h in range(QH):
                            g = qp[:, c * QH + h:c * QH + h + 1].to_broadcast([P, P])
                            mm = nc.tensor.matmul(B[2 + c][:, h * P:h * P + P], g, tri, start=True, stop=True)
                    mm.then_inc(S["gcrow"], 1)
                if s == 33:
                    pe.wait_ge(S["silu"], 3 * m + 3)
                    to_tokens(f_v, 0).then_inc(S["bT"], 1)
                if s == 36:
                    pe.wait_ge(S["v_ok"], 2 * m + 2)
                    for c in range(T):
                        mms(B[c], fs(f_k, c), fs(f_k, c)).then_inc(S["kk"], 1)
                if s == 38:
                    pe.wait_ge(S["gsub"], 2 * m + 2)
                    for c in range(T):
                        mms(B[2 + c], fs(f_k, c), fs(f_q, c)).then_inc(S["qk"], 1)
                for c in range(T):
                    at, xx, xt, yb = (r[:, c * n:c * n + n] for r, n in ((AT, GC), (XX, GC), (XT, GC), (Yb, 256)))
                    e = s - 48 - c
                    if e >= 0 and e < 6 * (LEVELS - 1) and e % 6 == 0:
                        lv = e // 6 + 1
                        turned(m, lv - 1, c)
                        cols = pair(1 << lv)
                        xc = cols(by_h(xx), 0)
                        for h in range(QH):
                            mm = nc.tensor.matmul(B[c][:, h * 64:h * 64 + 64], at[:, h * P:h * P + P], xc[:, h],
                                                  start=True, stop=True)
                        mm.then_inc(S["yp"], 1)
                    if e >= 0 and e < 6 * (LEVELS - 1) and e % 6 == 2:
                        lv = e // 6 + 1
                        pe.wait_ge(S["qkt_ok"], 2 * m + c + 1)
                        pe.wait_ge(S["y_ok"], 2 * LEVELS * m + 2 * lv + c + 1)
                        mms(B[2 + c], hs(xt), hs(yb, 0, 64), 64).then_inc(S["zp"], 1)
                    if e < 6 * (LEVELS - 1) and e % 6 == 4 and (e + 2) // 6 >= SMALL:
                        lv = (e + 2) // 6
                        pe.wait_ge(S["x_ok"], 2 * LEVELS * m + 2 * lv + c + 1)
                        turn(B[c], hs(xx)).then_inc(S["xtp"], 1)
                if s == 85:
                    turned(m, LEVELS - 1, 0)
                    mms(B[0], hs(XT), hs(t_v)).then_inc(S["y0p"], 1)
                if s == 87:
                    pe.wait_ge(S["y0_ok"], m + 1)
                    mms(B[2], hs(decay), hs(yv)).then_inc(S["o0p"], 1)
                    pe.wait_ge(S["ktail_ok"], m + 1)
                    mms(B[0], hs(ktail), hs(yv)).then_inc(S["o0p"], 1)
                if s == 90:
                    pe.wait_ge(S["s_ok"], m + 1)
                    turned(m, LEVELS - 1, 1)
                    mms(B[1], fs(f_k, 1), hs(Sst)).then_inc(S["ksp"], 1)
                    mms(B[3], fs(f_q, 1), hs(Sst)).then_inc(S["ksp"], 1)
                if s == 94:
                    pe.wait_ge(S["r_ok"], m + 1)
                    mms(B[1], hs(XT, GC), hs(Rb)).then_inc(S["y1p"], 1)
                if s == 96:
                    pe.wait_ge(S["y1_ok"], m + 1)
                    pe.wait_ge(S["qs_ok"], m + 1)
                    mms(B[3], hs(decay, GC), hs(yv, GC)).then_inc(S["o1p"], 1)
                if s == 109:
                    pe.wait_ge(S["onorm"], m + 1)
                    pe.wait_ge(S["o0_ok"], m + 1)
                    to_features(gate, 0).then_inc(S["mT"], 1)
                if s == 126:
                    pe.wait_ge(S["mix_ok"], 2 * m + 2)

            def attn(m, s):
                a = m - QUADS
                if s == 0:
                    pe.wait_ge(evac0, 4 * m + 1)
                    pe.wait_ge(evac1, 4 * m + 1)
                    to_features(rawk, 0).then_inc(S["akT"], 1)
                if s == 2:
                    pe.wait_ge(evac0, 4 * m + 2)
                    pe.wait_ge(evac1, 4 * m + 2)
                    to_features(rawq, 2).then_inc(S["akT"], 1)
                if s == 6 or s == 7:
                    if s == 6:
                        pe.wait_ge(S["a_ev"], 4 * a + 4)
                    for h in range(2 * (s - 6), 2 * (s - 6) + 2):
                        nc.tensor.matmul(B[h][:, 0:P], f_q[:, h * SEQ:h * SEQ + P],
                                         f_k[:, h * SEQ:h * SEQ + P], start=True, stop=True)
                        nc.tensor.matmul(B[h][:, P:3 * P], f_q[:, h * SEQ + P:h * SEQ + SEQ],
                                         f_k[:, h * SEQ:h * SEQ + SEQ], start=True, stop=True).then_inc(S["sc"], 1)
                if s == 20:
                    pe.wait_ge(S["aexp"], 8 * a + 8)
                    for b in range(3):
                        turn(B[b], lambda h: prob[:, h * 384 + b * P:h * 384 + b * P + P]).then_inc(S["pTp"], 1)
                if s == 25:
                    pe.wait_ge(S["pT_ok"], 3 * a + 3)
                    pe.wait_ge(evac0, 4 * m + 3)
                    pe.wait_ge(evac1, 4 * m + 3)
                    mms(B[3], hs(pT), hs(rawv)).then_inc(S["pv"], 1)
                if s == 26:
                    for h in range(QH):
                        nc.tensor.matmul(B[0][:, h * P:h * P + P], pT[:, GC + h * P:GC + h * P + P],
                                         rawv[:, h * P:h * P + P], start=True, stop=False)
                        mm = nc.tensor.matmul(B[0][:, h * P:h * P + P], pT[:, 2 * GC + h * P:2 * GC + h * P + P],
                                              rawv[:, GC + h * P:GC + h * P + P], start=False, stop=True)
                    mm.then_inc(S["pv"], 1)
                if s == 40:
                    pe.wait_ge(S["agated"], a + 1)
                    to_features(gate, 1).then_inc(S["amT"], 1)
                if s == 44:
                    pe.wait_ge(S["amix_ok"], 2 * a + 2)

            pe.wait_ge(ident_in, 16)
            pe.wait_ge(ng_in, 32)
            nc.tensor.transpose(B[0][:, 0:KT + 1], ngr[0:KT + 1, :], ident[0:KT + 1, 0:KT + 1]).then_inc(S["pre_ng"], 1)

            def x_tile(k):
                if k * P in XCUT:
                    pe.wait_ge(x_in[XCUT.index(k * P)], 16)
                if k >= 4:
                    pe.wait_ge(S["ulo"], k - 3)
                else:
                    pe.wait_ge(S["pre_ngc"], 1)
                for t in range(T):
                    mm = nc.tensor.transpose(B[k % 4][:, t * P:t * P + P],
                                             xin[:, t * D + k * P:t * D + k * P + P], ident)
                mm.then_inc(S["xT"], 1)

            for k in range(3):
                x_tile(k)
            for k in range(KT):
                if k + 3 < KT:
                    x_tile(k + 3)
                pe.wait_ge(S["ulo"], k + 1)
                run_step(k, k, 1)
            bank_pair = 0
            for k in range(2):
                run_step(KT + k, k, bank_pair)
            pe.wait_ge(S["ba_lo"], 1)
            for k in range(KT):
                for i, (w, u) in enumerate(((ba_hi, u_hi), (ba_hi, u_lo), (ba_lo, u_hi))):
                    mm = nc.tensor.matmul(B[0][0:2 * HEADS, 0:SEQ], w[:, k * 32:k * 32 + 32], u[:, k, :],
                                          start=(k == 0 and i == 0), stop=(k == KT - 1 and i == 2))
            mm.then_inc(S["lg_p"], 1)
            for k in range(2, KT):
                run_step(KT + k, k, bank_pair)
                if k == 6:
                    pe.wait_ge(S["lgT"], 1)
                    for t in range(T):
                        mm = nc.tensor.transpose(B[2][:, t * 32:t * 32 + 32], lgT[0:32, t * P:t * P + P], ident[0:32, 0:32])
                    mm.then_inc(S["lg_t"], 1)
                if k == 8:
                    pe.wait_ge(small_in, 16 * 3)
                    for i in range(2):
                        mm = nc.tensor.transpose(B[3][:, 96 * i:96 * i + 96], cvr[0:96, i * P:i * P + P], ident[0:96, 0:96])
                    mm.then_inc(S["cvT"], 1)
            bank_free(3)
            for k in range(KT):
                run_step(2 * KT + k, k, 1)
                if k == 4:
                    pe.wait_ge(S["pre_v"], 8)
                    pe.wait_ge(consts_in, 16)
                    nc.tensor.matmul(B[0][:, 0:32], tri, spc, start=True, stop=True)
                    nc.tensor.matmul(B[1][:, 0:32], ones, spc, start=True, stop=True).then_inc(S["gc_p"], 1)

            def body(m, mixer):
                for s in range(BODY):
                    g, k = s // KT, s % KT
                    if k == 0:
                        bank_free(4 * m + 4 + g)
                    run_step(m * BODY + 3 * KT + s, k, g % 2)
                    mixer(m, s)

            pe.wait_ge(S["par_ok"], 1)
            with pe.Fori(0, QUADS) as m:
                body(m, dn)
            with pe.Fori(QUADS, 2 * QUADS - 1) as m:
                body(m, attn)

            last = 2 * QUADS - 1
            first_out = last * BODY + 4 * KT
            bank_free(4 * last + 4)
            for s in range(2 * KT):
                if s == KT:
                    bank_free(4 * last + 5)
                if s - KT in M_AT:
                    pe.wait_ge(S["m_lo"], M_AT.index(s - KT) + 1)
                run_step(last * BODY + 3 * KT + s, s % KT, s // KT % 2)
                attn(last, s)

            def out_bank_free(j):
                pe.wait_ge(S["h_add"], 2 * (j - 1))

            bank_free(4 * last + 6)
            for k in range(KT):
                run_step(first_out + KT + k, k, 0)
            with pe.Fori(2, NG, 2) as j:
                for i in range(2):
                    out_bank_free(j + i)
                    for k in range(KT):
                        run_step(first_out + (j + i) * KT + k, k, (1 + i) % 2)

        def split_hi(act, n, k, first=False):
            if k % 2 == 0:
                act.wait_ge(w_in_ring[k // 2 % RAW], 16 * (n // (2 * RAW)) + 16 if isinstance(n, int) else n * 2 - (k % 8) * 2 + 16)
            if not first:
                act.wait_ge(tile_used, n - RING + 1)
            nc.scalar.copy(w_hi[:, k % RING], w_raw[:, k // 2 % RAW, k % 2]).then_inc(hi_ready, 1)

        def split_lo(dve, n, k):
            dve.wait_ge(hi_ready, n + 1)
            nc.vector.tensor_tensor(w_lo[:, k % RING], w_raw[:, k // 2 % RAW, k % 2],
                                    w_hi[:, k % RING].bitcast(F32), ALU.subtract).then_inc(lo_ready, 1)

        @block.scalar
        def _(act):
            def evac_t0(group, dst, bank):
                act.wait_ge(tile_used, KT * group)
                nc.scalar.mul(dst[:, 0:GC], proj[bank][0][:, :], rstd[:, 0:1]).then_inc(evac0, 1)

            def tap3(m, i, dst, banks, hh):
                if hh == 0:
                    act.wait_ge(S["fT"], 3 * m + i + 1)
                for h in range(2 * hh, 2 * hh + 2):
                    nc.scalar.mul(dst[:, h * SEQ:h * SEQ + SEQ],
                                  B[banks + h // 2][:, (h % 2) * SEQ:(h % 2) * SEQ + SEQ],
                                  cw[:, (i * QH + h) * TAPS + 3:(i * QH + h) * TAPS + 4]).then_inc(S["tap3"], 1)

            def silu(m, i, f):
                act.wait_ge(S["conv"], 36 * m + 12 * i + 12)
                nc.scalar.activation(f, f, ACT.Silu).then_inc(S["silu"], 1)

            def dn(m, s):
                if s == 1:
                    evac_t0(4 * m + 3, rawv, 1)
                    act.wait_ge(S["qp_ok"], 2 * m + 2)
                if s in (2, 3):
                    tap3(m, 0, f_k, 0, s - 2)
                if s in (5, 6):
                    tap3(m, 1, f_q, 2, s - 5)
                if s == 9:
                    silu(m, 0, f_k)
                if s in (11, 12):
                    if s == 11:
                        act.wait_ge(S["bT"], 3 * m + 1)
                    nc.scalar.copy(t_k[:, (s - 11) * GC:(s - 10) * GC], B[s - 11][:, :]).then_inc(S["tok"], 1)
                if s == 15:
                    silu(m, 1, f_q)
                if s in (17, 18):
                    if s == 17:
                        act.wait_ge(S["bT"], 3 * m + 2)
                    nc.scalar.copy(t_q[:, (s - 17) * GC:(s - 16) * GC], B[2 + s - 17][:, :]).then_inc(S["tok"], 1)
                if s in (21, 22):
                    if s == 21:
                        act.wait_ge(S["kqT"], 2 * m + 1)
                    nc.scalar.copy(f_k[:, (s - 21) * GC:(s - 20) * GC], B[s - 21][:, :]).then_inc(S["kq_ev"], 1)
                if s in (24, 25):
                    tap3(m, 2, f_v, 0, s - 24)
                if s in (26, 27):
                    if s == 26:
                        act.wait_ge(S["kqT"], 2 * m + 2)
                    nc.scalar.copy(f_q[:, (s - 26) * GC:(s - 25) * GC], B[2 + s - 26][:, :]).then_inc(S["kq_ev"], 1)
                if s == 32:
                    silu(m, 2, f_v)
                if s == 33:
                    evac_t0(4 * m + 4, gate, 0)
                if s == 36:
                    act.wait_ge(evac0, 4 * m + 4)
                    act.wait_ge(evac1, 4 * m + 4)
                    nc.scalar.activation(gate, gate, ACT.Silu).then_inc(S["silu_g"], 1)
                if s == 38:
                    act.wait_ge(S["gmin"], 2 * m + 2)
                    nc.scalar.activation(decay, decay, ACT.Exp).then_inc(S["gexp"], 1)
                for c in range(T):
                    e = s - 47 - c
                    if 6 * SMALL <= e < 6 * LEVELS and e % 6 == 0:
                        act.wait_ge(S["xtp"], 2 * (LEVELS - SMALL) * m + 2 * (e // 6 - SMALL) + c + 1)
                        nc.scalar.copy(XT[:, c * GC:c * GC + GC], B[c][:, :]).then_inc(S["xt_a"], 1)
                if s == 65:
                    evac_t0(4 * m + 5, rawk, 1)
                if s == 86:
                    act.wait_ge(S["y0p"], m + 1)
                    nc.scalar.copy(yv[:, 0:GC], B[0][:, :]).then_inc(S["y0_ok"], 1)
                if s == 88:
                    act.wait_ge(S["o0p"], 2 * m + 2)
                    nc.scalar.copy(Sst, B[0][:, :]).then_inc(S["s_ok"], 1)
                if s == 89:
                    nc.scalar.copy(o_dn[:, 0:GC], B[2][:, :]).then_inc(S["o0_ok"], 1)
                if s == 95:
                    act.wait_ge(S["y1p"], m + 1)
                    nc.scalar.copy(yv[:, GC:2 * GC], B[1][:, :]).then_inc(S["y1_ok"], 1)
                if s == 97:
                    evac_t0(4 * m + 6, rawq, 0)
                if s in (110, 111):
                    b = s - 110
                    if b == 0:
                        act.wait_ge(S["mT"], m + 1)
                    nc.scalar.mul(mixedT[:, bass.ds(m * QH + 2 * b, 2), :],
                                  B[b][:, :].rearrange("p (h n) -> p h n", h=2), ngT[:, KT:KT + 1]).then_inc(S["mix_ok"], 1)

            def attn(m, s):
                a = m - QUADS
                if s == 1:
                    evac_t0(4 * m + 3, rawv, 1)
                if s in (2, 3):
                    if s == 2:
                        act.wait_ge(S["akT"], 2 * a + 1)
                    nc.scalar.copy(f_k[:, (s - 2) * GC:(s - 1) * GC], B[s - 2][:, :]).then_inc(S["a_ev"], 1)
                if s in (4, 5):
                    if s == 4:
                        act.wait_ge(S["akT"], 2 * a + 2)
                    nc.scalar.copy(f_q[:, (s - 4) * GC:(s - 3) * GC], B[2 + s - 4][:, :]).then_inc(S["a_ev"], 1)
                if s in (15, 16, 17, 18):
                    h = s - 15
                    if h == 0:
                        act.wait_ge(S["amax"], 2 * a + 2)
                    for t, (lo, n) in enumerate(((0, P), (P, SEQ))):
                        pr = prob[:, h * 384 + lo:h * 384 + lo + n]
                        nc.scalar.activation(pr, pr, ACT.Exp, bias=negmax[:, t * QH + h:t * QH + h + 1],
                                             accum_out=esum[:, t * QH + h:t * QH + h + 1]).then_inc(S["aexp"], 1)
                if s in (21, 22, 23):
                    b = s - 21
                    act.wait_ge(S["pTp"], 3 * a + b + 1)
                    nc.scalar.copy(pT[:, b * GC:b * GC + GC], B[b][:, :]).then_inc(S["pT_ok"], 1)
                if s == 33:
                    evac_t0(4 * m + 4, gate, 0)
                if s == 35:
                    act.wait_ge(evac0, 4 * m + 4)
                    act.wait_ge(evac1, 4 * m + 4)
                    nc.scalar.activation(gate, gate, ACT.Silu).then_inc(S["a_silu"], 1)
                if s in (41, 42):
                    b = s - 41
                    if b == 0:
                        act.wait_ge(S["amT"], a + 1)
                    nc.scalar.copy(mixedT[:, bass.ds(m * QH + 2 * b, 2), :],
                                   B[1 + b][:, :].rearrange("p (h n) -> p h n", h=2)).then_inc(S["amix_ok"], 1)
                if s == 65:
                    evac_t0(4 * m + 5, rawk, 1)
                if s == 97:
                    evac_t0(4 * m + 6, rawq, 0)

            act.dma_start(ident, consts[:, C_ID:C_ID + P]).then_inc(ident_in, 16)
            act.dma_start(ngr[0:KT, :], norm_g.rearrange("a (k p) -> (a k) p", p=P)).then_inc(ng_in, 16)
            act.dma_start(ngr[KT:KT + 1, :], dn_norm_g).then_inc(ng_in, 16)
            for i, (lo, hi) in enumerate(zip(XCUT, XCUT[1:])):
                act.dma_start(xin.rearrange("p (t d) -> p t d", t=T)[:, :, lo:hi], tokens[:, :, lo:hi]).then_inc(x_in[i], 16)
                if i == 3:
                    act.dma_start(cst[:, P:C_ALL], consts[:, P:C_ALL]).then_inc(consts_in, 16)
                    act.dma_start(cvr.rearrange("p (i n) -> p i n", i=2)[0:96],
                                  conv_w.rearrange("a t (b n) -> (a t b) n", n=P).rearrange("(i r) n -> r i n", i=2)).then_inc(small_in, 16)
                    act.dma_start(alog, a_log.to_broadcast([P, HEADS])).then_inc(small_in, 16)
                    act.dma_start(dtb, dt_bias.to_broadcast([P, HEADS])).then_inc(small_in, 16)
            act.dma_start(wba.rearrange("p (k n) -> p k n", k=KT), w_in_r[:, :, LOGITS:LOGITS + 32]).then_inc(wba_in, 16)
            for n in range(3):
                split_hi(act, n, n, first=True)
            for k in range(KT):
                act.wait_ge(S["xT"], k + 1)
                nc.scalar.mul(u_hi[:, k], B[k % 4][:, 0:SEQ], ngT[:, k:k + 1]).then_inc(S["uhi"], 1)
                if k == KT - 1:
                    act.wait_ge(wba_in, 16)
                    act.wait_ge(tile_used, KT)
                    nc.scalar.copy(ba_hi, wba).then_inc(S["ba_hi"], 1)
                    act.wait_ge(S["lg_p"], 1)
                split_hi(act, k + 3, (k + 3) % KT, first=(k < 1))
            for part in x_in:
                act.wait_ge(part, 16)
            for k in range(KT):
                split_hi(act, KT + k + 3, (k + 3) % KT)
                if k == 0:
                    nc.scalar.copy(lgT[0:32, :], B[0][0:32, 0:SEQ]).then_inc(S["lgT"], 1)
                if k < 16:
                    if k >= 2:
                        act.wait_ge(S["xsq"], k - 1)
                    nc.scalar.activation(junk[:, (k % 2) * GC:(k % 2) * GC + GC], xin[:, GC * k:GC * k + GC], ACT.Square,
                                         accum_out=ssx[:, k:k + 1]).then_inc(S["xsq"], 1)
                if k == 20:
                    act.wait_ge(S["rstd_ok"], 1)
                    evac_t0(1, rawk, 1)
                if k == 23:
                    act.wait_ge(small_in, 16 * 3)
                    act.wait_ge(S["pre_v"], 5)
                    nc.scalar.activation(zz[:, 0:32], lg.rearrange("p (t n) -> p t n", t=T)[:, :, 0:HEADS], ACT.Exp,
                                         scale=-1.0).then_inc(S["pre_a"], 1)
                    nc.scalar.activation(spb, spb, ACT.Exp).then_inc(S["pre_a"], 1)
                if k == 24:
                    nc.scalar.activation(alog, alog, ACT.Exp).then_inc(S["pre_a"], 1)
                    act.wait_ge(S["pre_a"], 2)
                    nc.scalar.activation(spb, spb, ACT.Ln, bias=1.0).then_inc(S["pre_a"], 1)
            for k in range(KT):
                split_hi(act, 2 * KT + k + 3, (k + 3) % KT)
                if k == 1:
                    evac_t0(2, rawq, 0)
                if k == 8:
                    act.wait_ge(S["pre_v"], 11)
                    nc.scalar.activation(quad_all[:, :, 24:28], quad_all[:, :, 12:16], ACT.Exp).then_inc(S["par_a"], 1)
                    nc.scalar.activation(quad_all[:, :, 28:32], zz[:, 32:48].rearrange("p (q h) -> p q h", h=QH),
                                         ACT.Exp).then_inc(S["par_a"], 1)

            def body(m, mixer):
                for s in range(BODY):
                    split_hi(act, m * BODY + 3 * KT + s + 3, (s + 3) % KT)
                    mixer(m, s)

            with act.Fori(0, QUADS) as m:
                body(m, dn)
            with act.Fori(QUADS, 2 * QUADS - 1) as m:
                body(m, attn)

            last = 2 * QUADS - 1
            first_out = last * BODY + 4 * KT

            def m_hi(b):
                tiles = slice(M_AT[b], (M_AT + (KT,))[b + 1])
                nc.scalar.copy(u_hi[:, tiles], mixedT[:, tiles]).then_inc(S["m_hi"], 1)

            for s in range(2 * KT):
                split_hi(act, last * BODY + 3 * KT + s + 3, (s + 3) % KT)
                if s == KT:
                    act.wait_ge(tile_used, KT * (4 * last + 4))
                    act.wait_ge(S["mix_ok"], 2 * QUADS)
                    act.wait_ge(S["amix_ok"], 2 * QUADS - 2)
                attn(last, s)
                if s == KT:
                    m_hi(0)
                if KT <= s < KT + 7:
                    m_hi(s - KT + 1)
                if s == 43:
                    act.wait_ge(S["amix_ok"], 2 * QUADS)
                    m_hi(8)
                if s == 45:
                    act.wait_ge(S["amT"], QUADS)
                    act.wait_ge(S["m_lo"], len(M_AT))
                    act.dma_start(hbuf.rearrange("p (t d) -> p t d", t=T), tokens).then_inc(S["h_in"], 16)
                    act.dma_start(gfin, final_norm_g.rearrange("(a d) -> a d", a=1).to_broadcast([P, D])).then_inc(S["gf_in"], 16)

            def h_square(j, g):
                for t in range(T):
                    act.wait_ge(S["h_add"], 2 * g + t + 1)
                    nc.scalar.activation(w_sq, hbuf[:, bass.ds(j * GC + t * D, GC)], ACT.Square,
                                         accum_out=hsum[:, t, bass.ds(j, 1)]).then_inc(S["h_sq"], 1)
                    act.wait_ge(S["h_sq"], 2 * g + t + 1)

            w_sq = region(12288, GC)
            for i in range(1):
                for k in range(KT):
                    split_hi(act, first_out + KT + k + 3, (k + 3) % KT)
                    if k == 16:
                        h_square(0, 0)
            with act.Fori(2, NG - 1) as j:
                for k in range(KT):
                    split_hi(act, first_out + j * KT + k + 3, (k + 3) % KT)
                    if k == 16:
                        h_square(j - 1, j - 1)
            for k in range(KT):
                if k + 3 < KT:
                    split_hi(act, first_out + (NG - 1) * KT + k + 3, k + 3)
                if k == 16:
                    h_square(NG - 2, NG - 2)
            h_square(NG - 1, NG - 1)
            act.wait_ge(S["h_rstd"], 1)
            act.wait_ge(S["h_g"], 2 * (NG - 1))
            for t in range(T):
                for j in range(2):
                    part = hbuf[:, t * D + 1024 * j:t * D + 1024 * j + 1024]
                    nc.scalar.mul(part, part, rstd[:, t:t + 1]).then_inc(S["h_fin_a"], 1)

        @block.vector
        def _(dve):
            def evac_t1(group, dst, bank):
                dve.wait_ge(tile_used, KT * group)
                nc.vector.tensor_scalar(dst[:, GC:2 * GC], proj[bank][1][:, :], rstd[:, 1:2], None,
                                        ALU.mult).then_inc(evac1, 1)

            def over_h(ap, n=P):
                return ap.unsqueeze(2).to_broadcast([P, ap.shape[1], n])

            def each_h(ap, blocks=QH):
                return ap.unsqueeze(1).to_broadcast([P, blocks, ap.shape[1]])

            def taps(m, i, f, banks, part):
                for n in (2 * part, 2 * part + 1):
                    shift, h = n // QH + 1, n % QH
                    if n < QH:
                        dve.wait_ge(S["tap3"], 12 * m + QH * i + h + 1)
                    else:
                        dve.wait_ge(S["conv"], 36 * m + 12 * i + n - 3)
                    to = f[:, h * SEQ + shift:h * SEQ + SEQ]
                    at = (h % 2) * SEQ
                    w = (i * QH + h) * TAPS + 3 - shift
                    nc.vector.scalar_tensor_tensor(out=to, in0=B[banks + h // 2][:, at:at + SEQ - shift],
                                                   scalar=cw[:, w:w + 1], in1=to,
                                                   op0=ALU.mult, op1=ALU.add).then_inc(S["conv"], 1)

            def dn(m, s):
                if s == 0:
                    nc.vector.tensor_copy(qp[:, :], quad_all[:, bass.ds(m, 1), :].rearrange("p q n -> p (q n)")).then_inc(S["qp_ok"], 1)
                    nc.vector.tensor_copy(cw[:, :], conv_all[:, bass.ds(m, 1), :].rearrange("p q n -> p (q n)")).then_inc(S["qp_ok"], 1)
                if s == 1:
                    evac_t1(4 * m + 3, rawv, 1)
                    dve.wait_ge(S["qp_ok"], 2 * m + 2)
                if 3 <= s < 9:
                    taps(m, 0, f_k, 0, s - 3)
                if 9 <= s < 15:
                    taps(m, 1, f_q, 2, s - 9)
                if 26 <= s < 32:
                    taps(m, 2, f_v, 0, s - 26)
                for i, at in ((0, 15), (1, 21)):
                    if s == at:
                        dve.wait_ge(S["sqr"], 2 * m + i + 1)
                        nc.vector.tensor_reduce(stat[:, 8 * i:8 * i + 8], by_h(sq), AX.X, ALU.add).then_inc(S["red"], 1)
                for i, at, tk in ((0, 18, t_k), (1, 24, t_q)):
                    if s == at:
                        dve.wait_ge(S["fac_ok"], 2 * m + i + 1)
                        nc.vector.tensor_tensor(by_h(tk), by_h(tk), over_h(fac[:, 8 * i:8 * i + 8]), ALU.mult).then_inc(S["scaled"], 1)
                if s in (30, 32):
                    c = (s - 30) // 2
                    if c == 0:
                        dve.wait_ge(S["gcrow"], m + 1)
                    nc.vector.tensor_tensor(by_h(decay[:, c * GC:c * GC + GC]), by_h(B[2 + c][:, :]),
                                            over_h(qp[:, 8 + QH * c:8 + QH * c + QH]), ALU.subtract).then_inc(S["gsub"], 1)
                if s == 33:
                    evac_t1(4 * m + 4, gate, 0)
                if s in (34, 35):
                    t = s - 34
                    if t == 0:
                        dve.wait_ge(S["bT"], 3 * m + 3)
                    nc.vector.tensor_tensor(by_h(t_v[:, t * GC:t * GC + GC]), by_h(B[t][:, :]),
                                            over_h(qp[:, 16 + QH * t:16 + QH * t + QH]), ALU.mult).then_inc(S["v_ok"], 1)
                if s in (39, 40):
                    c = s - 39
                    if c == 0:
                        dve.wait_ge(S["gexp"], m + 1)
                    dve.wait_ge(S["kk"], 2 * m + c + 1)
                    cc = slice(c * GC, c * GC + GC)
                    nc.vector.tensor_tensor(AT[:, cc], B[c][:, :], decay[:, cc], ALU.mult).then_inc(S["at_ok"], 1)
                if s in (41, 42):
                    c = s - 41
                    dve.wait_ge(S["qk"], 2 * m + c + 1)
                    cc = slice(c * GC, c * GC + GC)
                    nc.vector.tensor_tensor(decay[:, cc], B[2 + c][:, :], decay[:, cc], ALU.mult).then_inc(S["qkt_ok"], 1)
                for c in range(T):
                    yb = by_h(Yb[:, c * 256:c * 256 + 256], 64)
                    xx = by_h(XX[:, c * GC:c * GC + GC])
                    e = s - 43 - c
                    if e == 0:
                        dve.wait_ge(S["at_ok"], 2 * m + c + 1)
                        nc.vector.transpose(XT[:, c * GC:c * GC + GC], AT[:, c * GC:c * GC + GC]).then_inc(S["aT"], 1)
                    lv = e // 6
                    if 0 <= lv < LEVELS and e == (1 if lv == 0 else 6 * lv):
                        mask = each_h(cst[:, C_YM + 64 * lv:C_YM + 64 * lv + 64])
                        if lv == 0:
                            dve.wait_ge(S["aT"], 2 * m + c + 1)
                            nc.vector.tensor_tensor(yb, by_h(XT[:, c * GC:c * GC + GC])[:, :, 0:P:2], mask, ALU.mult).then_inc(S["y_ok"], 1)
                        else:
                            dve.wait_ge(S["yp"], 2 * (LEVELS - 1) * m + 2 * (lv - 1) + c + 1)
                            nc.vector.tensor_tensor(yb, by_h(B[c][:, 0:256], 64), mask, ALU.mult).then_inc(S["y_ok"], 1)
                    if 0 <= lv < LEVELS and e == 6 * lv + 2:
                        xc = pair(1 << lv)(xx, 0)
                        if lv == 0:
                            dve.wait_ge(S["y_ok"], 2 * LEVELS * m + c + 1)
                            dve.wait_ge(S["x_id"], m + 1)
                            z = yb
                        else:
                            dve.wait_ge(S["zp"], 2 * (LEVELS - 1) * m + 2 * (lv - 1) + c + 1)
                            z = by_h(B[2 + c][:, 0:256], 64)
                        z = z.rearrange("p h (b s) -> p h b s", s=1 << lv)
                        nc.vector.tensor_tensor(xc, xc, z, ALU.subtract).then_inc(S["x_ok"], 1)
                    if 0 <= lv < SMALL and e == 6 * lv + 3:
                        dve.wait_ge(S["x_ok"], 2 * LEVELS * m + 2 * lv + c + 1)
                        nc.vector.transpose(XT[:, c * GC:c * GC + GC], XX[:, c * GC:c * GC + GC]).then_inc(S["xt_v"], 1)
                if s == 65:
                    evac_t1(4 * m + 5, rawk, 1)
                if s == 91:
                    dve.wait_ge(S["ksp"], 2 * m + 2)
                    nc.vector.tensor_tensor(by_h(Rb), by_h(B[1][:, :]), over_h(qp[:, 24:28]), ALU.mult).then_inc(S["r_mul"], 1)
                if s == 92:
                    dve.wait_ge(S["r_mul"], m + 1)
                    nc.vector.tensor_tensor(Rb, t_v[:, GC:2 * GC], Rb, ALU.subtract).then_inc(S["r_ok"], 1)
                if s == 93:
                    nc.vector.tensor_tensor(by_h(QS), by_h(B[3][:, :]), over_h(qp[:, 24:28]), ALU.mult).then_inc(S["qs_ok"], 1)
                if s == 97:
                    evac_t1(4 * m + 6, rawq, 0)
                if s == 98:
                    dve.wait_ge(S["o1p"], m + 1)
                    dve.wait_ge(S["qs_ok"], m + 1)
                    nc.vector.tensor_tensor(o_dn[:, GC:2 * GC], B[3][:, :], QS, ALU.add).then_inc(S["o_ok"], 1)
                if s == 102:
                    dve.wait_ge(S["osq"], m + 1)
                    nc.vector.tensor_reduce(stat[:, 0:8], by_h(sq), AX.X, ALU.add).then_inc(S["ored"], 1)
                if s == 107:
                    dve.wait_ge(S["ofac"], m + 1)
                    dve.wait_ge(S["gated"], m + 1)
                    nc.vector.tensor_tensor(by_h(gate), by_h(gate), over_h(fac[:, 0:8]), ALU.mult).then_inc(S["onorm"], 1)

            def attn(m, s):
                a = m - QUADS
                if s == 1:
                    evac_t1(4 * m + 3, rawv, 1)
                if 8 <= s < 12:
                    h = s - 8
                    if h == 0:
                        dve.wait_ge(S["bias_ok"], QH * a + QH)
                    dve.wait_ge(S["sc"], QH * a + h + 1)
                    cc = slice(h * 384, h * 384 + 384)
                    nc.vector.scalar_tensor_tensor(out=prob[:, cc], in0=B[h][:, 0:384], scalar=float(P) ** -0.5,
                                                   in1=bias[:, cc], op0=ALU.mult, op1=ALU.add).then_inc(S["logit"], 1)
                if s in (12, 13):
                    t = s - 12
                    if t == 0:
                        dve.wait_ge(S["logit"], QH * a + QH)
                    lo, n = ((0, P), (P, SEQ))[t]
                    nc.vector.tensor_reduce(negmax[:, t * QH:t * QH + QH], by_h(prob, 384)[:, :, lo:lo + n], AX.X, ALU.max,
                                            negate=True).then_inc(S["amax"], 1)
                if s == 20:
                    dve.wait_ge(S["aexp"], 8 * a + 8)
                    nc.vector.reciprocal(rinv[:, :], esum[:, :]).then_inc(S["arin"], 1)
                if s in (27, 28):
                    t = s - 27
                    dve.wait_ge(S["arin"], a + 1)
                    dve.wait_ge(S["pv"], 2 * a + t + 1)
                    nc.vector.tensor_tensor(by_h(o_at[:, t * GC:t * GC + GC]), by_h(B[3 - 3 * t][:, :]),
                                            over_h(rinv[:, t * QH:t * QH + QH]), ALU.mult).then_inc(S["ao_ok"], 1)
                if s == 33:
                    evac_t1(4 * m + 4, gate, 0)
                if s == 37:
                    dve.wait_ge(S["a_silu"], a + 1)
                    dve.wait_ge(S["ao_ok"], 2 * a + 2)
                    nc.vector.tensor_tensor(gate, gate, o_at, ALU.mult).then_inc(S["agated"], 1)
                if s == 65:
                    evac_t1(4 * m + 5, rawk, 1)
                if s == 97:
                    evac_t1(4 * m + 6, rawq, 0)

            nc.vector.memset(half[:, :], -0.5).then_inc(S["half_ok"], 1)
            nc.vector.memset(ones, 1.0).then_inc(S["half_ok"], 1)
            dve.wait_ge(S["pre_ng"], 1)
            nc.vector.tensor_copy(ngT[:, :], B[0][:, 0:KT + 1]).then_inc(S["pre_ngc"], 1)
            for n in range(3):
                split_lo(dve, n, n)
            dve.wait_ge(S["pre_ngc"], 1)
            for k in range(KT):
                dve.wait_ge(S["uhi"], k + 1)
                nc.vector.scalar_tensor_tensor(out=u_lo[:, k], in0=B[k % 4][:, 0:SEQ], scalar=ngT[:, k:k + 1],
                                               in1=u_hi[:, k].bitcast(F32), op0=ALU.mult,
                                               op1=ALU.subtract).then_inc(S["ulo"], 1)
                if k == KT - 1:
                    dve.wait_ge(S["ba_hi"], 1)
                    nc.vector.tensor_tensor(ba_lo, wba, ba_hi.bitcast(F32), ALU.subtract).then_inc(S["ba_lo"], 1)
                split_lo(dve, k + 3, (k + 3) % KT)
            dve.wait_ge(small_in, 16 * 3)
            lgt = lg.rearrange("p (t n) -> p t n", t=T)
            s2 = lambda r: r.rearrange("p (t n) -> p t n", t=T)
            by_quad = lambda r: r.rearrange("p (t q h) -> p q t h", t=T, h=QH)
            for k in range(KT):
                split_lo(dve, KT + k + 3, (k + 3) % KT)
                if k == 17:
                    dve.wait_ge(S["xsq"], 16)
                    nc.vector.tensor_reduce(stat[:, 0:2], ssx.rearrange("p (t n) -> p t n", t=T), AX.X, ALU.add).then_inc(S["xss"], 1)
                    dve.wait_ge(S["xss"], 1)
                    nc.vector.tensor_scalar(stat[:, 2:4], stat[:, 0:2], 1.0 / D, EPS, ALU.mult, ALU.add).then_inc(S["xss"], 1)
                if k == 20:
                    dve.wait_ge(S["rstd_ok"], 1)
                    evac_t1(1, rawk, 1)
                if k == 21:
                    dve.wait_ge(S["lg_t"], 1)
                    for t in range(T):
                        nc.vector.tensor_scalar(lgt[:, t], B[2][:, t * 32:t * 32 + 32], rstd[:, t:t + 1], None, ALU.mult).then_inc(S["pre_v"], 1)
                    dve.wait_ge(S["pre_v"], 2)
                    nc.vector.tensor_tensor(s2(spa), lgt[:, :, HEADS:2 * HEADS], each_h(dtb, T), ALU.add).then_inc(S["pre_v"], 1)
                    dve.wait_ge(S["pre_v"], 3)
                    nc.vector.tensor_scalar(zz[:, 32:64], spa, -1.0, None, ALU.mult).then_inc(S["pre_v"], 1)
                    dve.wait_ge(S["pre_v"], 4)
                    nc.vector.tensor_tensor(spb, spa, zz[:, 32:64], ALU.min).then_inc(S["pre_v"], 1)
                if k == 26:
                    dve.wait_ge(S["pre_a"], 4)
                    nc.vector.tensor_scalar(zz[:, 0:32], zz[:, 0:32], 1.0, None, ALU.add).then_inc(S["pre_v"], 1)
                    nc.vector.scalar_tensor_tensor(out=spc, in0=spa, scalar=0.0, in1=spb, op0=ALU.max, op1=ALU.add).then_inc(S["pre_v"], 1)
                    dve.wait_ge(S["pre_v"], 7)
                    nc.vector.scalar_tensor_tensor(out=s2(spc), in0=s2(spc), scalar=-1.0, in1=each_h(alog, T), op0=ALU.mult,
                                                   op1=ALU.mult).then_inc(S["pre_v"], 1)
                if k == 12:
                    dve.wait_ge(S["cvT"], 1)
                    for i in range(2):
                        for j, of in enumerate((1, 0, 2)):
                            to = conv_all[:, :, 16 * j:16 * j + 16].rearrange("p q (h c) -> p c q h", c=TAPS)[:, 2 * i:2 * i + 2]
                            fr = B[3][:, 96 * i:96 * i + 96].rearrange("p (c x q h) -> p x c q h", x=3, q=QUADS, h=QH)[:, of]
                            for c in range(2):
                                nc.vector.tensor_copy(to[:, c], fr[:, c]).then_inc(S["cv_ok"], 1)
            for k in range(KT):
                split_lo(dve, 2 * KT + k + 3, (k + 3) % KT)
                if k == 1:
                    evac_t1(2, rawq, 0)
                if k == 6:
                    dve.wait_ge(S["pre_v"], 8)
                    nc.vector.tensor_copy(quad_all[:, :, 0:8].rearrange("p q (t h) -> p q t h", t=T), by_quad(spc)).then_inc(S["pre_v"], 1)
                    dve.wait_ge(S["gc_p"], 1)
                    nc.vector.tensor_copy(quad_all[:, :, 8:16].rearrange("p q (t h) -> p q t h", t=T), by_quad(B[0][:, 0:32])).then_inc(S["pre_v"], 1)
                    dve.wait_ge(S["pre_v"], 10)
                    nc.vector.tensor_tensor(zz[:, 32:48].rearrange("p (q h) -> p q h", h=QH),
                                            B[1][:, 0:16].rearrange("p (q h) -> p q h", h=QH),
                                            quad_all[:, :, 8:12], ALU.subtract).then_inc(S["pre_v"], 1)
                    dve.wait_ge(S["pre_p"], 1)
                    nc.vector.tensor_copy(quad_all[:, :, 16:24].rearrange("p q (t h) -> p q t h", t=T), by_quad(spa)).then_inc(S["par_ok"], 1)
            dve.wait_ge(S["par_a"], 2)
            dve.wait_ge(S["par_ok"], 1)
            dve.wait_ge(S["cv_ok"], 12)

            def body(m, mixer):
                for s in range(BODY):
                    split_lo(dve, m * BODY + 3 * KT + s + 3, (s + 3) % KT)
                    mixer(m, s)

            with dve.Fori(0, QUADS) as m:
                body(m, dn)
            with dve.Fori(QUADS, 2 * QUADS - 1) as m:
                body(m, attn)

            last = 2 * QUADS - 1
            first_out = last * BODY + 4 * KT

            def m_lo(b):
                dve.wait_ge(S["m_hi"], b + 1)
                tiles = slice(M_AT[b], (M_AT + (KT,))[b + 1])
                nc.vector.tensor_tensor(u_lo[:, tiles], mixedT[:, tiles],
                                        u_hi[:, tiles].bitcast(F32), ALU.subtract).then_inc(S["m_lo"], 1)

            for s in range(2 * KT):
                split_lo(dve, last * BODY + 3 * KT + s + 3, (s + 3) % KT)
                attn(last, s)
                if s == KT:
                    m_lo(0)
                if KT <= s < KT + 7:
                    m_lo(s - KT + 1)
                if s == 44:
                    m_lo(8)

            def h_add(j, g, bank):
                dve.wait_ge(tile_used, KT * (g + 4 * last + 5))
                for t in range(T):
                    part = hbuf[:, bass.ds(j * GC + t * D, GC)]
                    nc.vector.tensor_tensor(part, proj[bank][t][:, :], part, ALU.add).then_inc(S["h_add"], 1)

            for k in range(KT):
                split_lo(dve, first_out + KT + k + 3, (k + 3) % KT)
                if k == 12:
                    dve.wait_ge(S["h_in"], 16)
                    h_add(0, 0, 1)

            def out_pair(j, final):
                for i in range(2):
                    for k in range(KT):
                        if not (final and i == 1 and k + AHEAD >= KT):
                            split_lo(dve, first_out + (j + i) * KT + k + AHEAD, (k + AHEAD) % KT)
                        if k == 12:
                            h_add(j + i - 1, j + i - 1, i)

            with dve.Fori(2, NG - 2, 2) as j:
                out_pair(j, False)
            out_pair(NG - 2, True)
            h_add(NG - 1, NG - 1, 0)
            dve.wait_ge(S["h_sq"], 2 * NG)
            nc.vector.tensor_reduce(stat[:, 0:2], hsum[:, :, :], AX.X, ALU.add).then_inc(S["h_red"], 1)
            dve.wait_ge(S["h_red"], 1)
            nc.vector.tensor_scalar(stat[:, 2:4], stat[:, 0:2], 1.0 / D, EPS, ALU.mult, ALU.add).then_inc(S["h_mean"], 1)
            dve.wait_ge(S["gf_in"], 16)
            for t in range(T):
                part = hbuf[:, t * D + D - GC:t * D + D]
                nc.vector.tensor_tensor(part, part, gfin[:, D - GC:D], ALU.mult).then_inc(S["h_gl"], 1)
            dve.wait_ge(S["h_rstd"], 1)
            dve.wait_ge(S["h_g"], 2 * (NG - 1))
            dve.wait_ge(S["h_gl"], 2)
            for t in range(T):
                for j in range(2, 4):
                    part = hbuf[:, t * D + 1024 * j:t * D + 1024 * j + 1024]
                    nc.vector.tensor_scalar(part, part, rstd[:, t:t + 1], None, ALU.mult).then_inc(S["h_fin_v"], 1)

        @block.gpsimd
        def _(pool):
            def over_h(ap, n=P):
                return ap.unsqueeze(2).to_broadcast([P, ap.shape[1], n])

            def each_h(ap, blocks=QH):
                return ap.unsqueeze(1).to_broadcast([P, blocks, ap.shape[1]])

            def square(src, done):
                nc.gpsimd.tensor_tensor(sq, src, src, ALU.mult).then_inc(done, 1)

            def dn(m):
                for i, tk in ((0, t_k), (1, t_q)):
                    pool.wait_ge(S["tok"], 4 * m + 2 * i + 2)
                    if i == 1:
                        pool.wait_ge(S["red"], 2 * m + 1)
                    square(tk, S["sqr"])
                    pool.wait_ge(S["red"], 2 * m + i + 1)
                    pool.sem_inc(S["pool_waits"])
                    st, fa = stat[:, 8 * i:8 * i + 8], fac[:, 8 * i:8 * i + 8]
                    mul = 1.0 if i == 0 else float(P)
                    nc.gpsimd.tensor_scalar(st, st, mul, mul * EPS, ALU.mult, ALU.add).then_inc(S["pow_in"], 1)
                    pool.wait_ge(S["pow_in"], 3 * m + i + 1)
                    if i == 0:
                        nc.gpsimd.tensor_tensor(fa, st, half[:, 0:8], ALU.pow).then_inc(S["pow_k"], 1)
                        pool.wait_ge(S["pow_k"], m + 1)
                        nc.gpsimd.tensor_tensor(fa, fa, qp[:, 16:24], ALU.mult).then_inc(S["fac_ok"], 1)
                    else:
                        nc.gpsimd.tensor_tensor(fa, st, half[:, 0:8], ALU.pow).then_inc(S["fac_ok"], 1)
                pool.wait_ge(S["scaled"], 2 * m + 1)
                nc.gpsimd.tensor_tensor(by_h(ktail), by_h(t_k[:, 0:GC]), over_h(qp[:, 28:32]), ALU.mult).then_inc(S["ktail_ok"], 1)
                for c in range(T):
                    dc = by_h(decay[:, c * GC:c * GC + GC])
                    pool.wait_ge(S["gsub"], 2 * m + c + 1)
                    nc.gpsimd.tensor_tensor(dc, dc, each_h(causal), ALU.add).then_inc(S["gmin"], 1)
                nc.gpsimd.tensor_copy(by_h(XX), each_h(ident, 2 * QH)).then_inc(S["x_id"], 1)
                pool.wait_ge(S["o0_ok"], m + 1)
                pool.wait_ge(S["o_ok"], m + 1)
                square(o_dn, S["osq"])
                pool.wait_ge(S["silu_g"], m + 1)
                nc.gpsimd.tensor_tensor(gate, gate, o_dn, ALU.mult).then_inc(S["gated"], 1)
                pool.wait_ge(S["ored"], m + 1)
                pool.sem_inc(S["pool_waits"])
                nc.gpsimd.tensor_scalar(stat[:, 0:8], stat[:, 0:8], 1.0 / P, EPS, ALU.mult, ALU.add).then_inc(S["pow_in"], 1)
                pool.wait_ge(S["pow_in"], 3 * m + 3)
                nc.gpsimd.tensor_tensor(fac[:, 0:8], stat[:, 0:8], half[:, 0:8], ALU.pow).then_inc(S["ofac"], 1)

            def attn(m):
                a = m - QUADS
                pool.wait_ge(S["akT"], 2 * a + 1)
                nc.gpsimd.tensor_copy(slope4[:, :], cst[:, bass.ds(C_SLOPE + a * QH, QH)]).then_inc(S["sl_ok"], 1)
                pool.wait_ge(S["sl_ok"], a + 1)
                pool.sem_inc(S["pool_waits"])
                for h in range(QH):
                    nc.gpsimd.tensor_scalar(bias[:, h * 384:h * 384 + 384], cst[:, C_DIST:C_DIST + 384], slope4[:, h:h + 1],
                                            None, ALU.mult).then_inc(S["bias1"], 1)
                for h in range(QH):
                    bh = bias[:, h * 384:h * 384 + 384]
                    pool.wait_ge(S["bias1"], QH * a + h + 1)
                    nc.gpsimd.tensor_tensor(bh, bh, cst[:, C_LOGN:C_LOGN + 384], ALU.add).then_inc(S["bias_ok"], 1)

            pool.wait_ge(S["xss"], 2)
            pool.wait_ge(S["half_ok"], 2)
            nc.gpsimd.tensor_tensor(rstd[:, :], stat[:, 2:4], half[:, 0:2], ALU.pow).then_inc(S["rstd_ok"], 1)
            pool.wait_ge(S["pre_v"], 8)
            nc.gpsimd.tensor_tensor(spa, zz[:, 0:32], half[:, :], ALU.pow).then_inc(S["pre_p"], 1)

            with pool.Fori(0, QUADS) as m:
                dn(m)
            with pool.Fori(QUADS, 2 * QUADS) as m:
                attn(m)

            pool.wait_ge(S["gf_in"], 16)
            with pool.Fori(0, NG - 1) as j:
                for t in range(T):
                    pool.wait_ge(S["h_sq"], 2 * j + t + 1)
                    part = hbuf[:, bass.ds(j * GC + t * D, GC)]
                    nc.gpsimd.tensor_tensor(part, part, gfin[:, bass.ds(j * GC, GC)], ALU.mult).then_inc(S["h_g"], 1)
            pool.wait_ge(S["h_mean"], 1)
            nc.gpsimd.tensor_tensor(rstd[:, :], stat[:, 2:4], half[:, 0:2], ALU.pow).then_inc(S["h_rstd"], 1)


_INS = ["x", "norm_g", "w_in", "conv_w", "a_log", "dt_bias", "dn_norm_g", "w_out", "final_norm_g"]


def kernel(**inputs):
    import concourse.bacc as bacc
    from concourse.bass_utils import run_bass_kernel_spmd

    nc = bacc.Bacc("TRN2", target_bir_lowering=False, num_devices=1)
    arrays, args = {}, []
    for name in _INS:
        a = np.ascontiguousarray(inputs[name])
        arrays[f"in_{name}"] = a
        args.append(nc.dram_tensor(f"in_{name}", a.shape, mybir.dt.from_np(a.dtype), kind="ExternalInput").ap())
    table = constant_table()
    arrays["constants"] = table
    args.append(nc.dram_tensor("constants", table.shape, F32, kind="ExternalInput").ap())
    shape = inputs["x"].shape
    args.append(nc.dram_tensor("out", shape, F32, kind="ExternalOutput").ap())
    hybrid_layer(nc, *args)
    r = run_bass_kernel_spmd(nc, [arrays], core_ids=[0])
    return r.results[0]["out"]
```

```python
from contextlib import ExitStack

import numpy as np

import concourse.bass as bass
from concourse import mybir

F32 = mybir.dt.float32
F32R = mybir.dt.float32r
ACT = mybir.ActivationFunctionType
ALU = mybir.AluOpType
AX = mybir.AxisListType

P = 128
SEQ = 256
T = SEQ // P
D = 4096
KT = D // P
HEADS = 16
WIDTH = HEADS * P
QH = 4
GC = QH * P
QUADS = HEADS // QH
COL = {"aq": 0, "ak": WIDTH, "av": 2 * WIDTH, "ag": 3 * WIDTH,
       "dq": 4 * WIDTH, "dk": 5 * WIDTH, "dv": 6 * WIDTH, "dg": 7 * WIDTH}
LOGITS = 8 * WIDTH
TAPS = 4
LEVELS = 7
SMALL = 5
EPS = 1e-6
NEG = -1.0e30
BODY = 4 * KT
RAW = 4
RING = 4
AHEAD = 3
NG = D // GC
LATE = 8
XCUT = (0, 2 * P) + tuple(range(4 * P, D + 1, 4 * P))
M_STEP = (19, 20, 24, 25, 26, 29, 30, 43)

C_ID, C_TRI, C_CAUSAL, C_YM = 0, 128, 256, 384
C_DIST = C_YM + LEVELS * 64
C_LOGN = C_DIST + 384
C_SLOPE = C_LOGN + 384
C_ALL = C_SLOPE + HEADS


def constant_table():
    c = np.zeros((P, C_ALL), np.float32)
    p = np.arange(P)[:, None]
    f = np.arange(P)[None, :]
    c[:, C_ID:C_ID + P] = p == f
    c[:, C_TRI:C_TRI + P] = p <= f
    c[:, C_CAUSAL:C_CAUSAL + P] = np.where(p <= f, 0.0, NEG)
    n = np.arange(64)[None, :]
    for lv in range(LEVELS):
        s = 1 << lv
        c[:, C_YM + 64 * lv:C_YM + 64 * lv + 64] = (p // (2 * s) == n // s) & (p % (2 * s) >= s)
    dist = np.concatenate([p - f, P + p - np.arange(SEQ)[None, :]], axis=1)
    count = np.zeros(dist.shape)
    for window, dilation in ((128, 1), (512, 4), (2048, 16)):
        count += (dist >= 0) & (dist <= window) & (dist % dilation == 0)
    c[:, C_DIST:C_DIST + 384] = -np.where(count > 0, dist, 0)
    c[:, C_LOGN:C_LOGN + 384] = np.where(count > 0, np.log(np.maximum(count, 1)), NEG)
    start = 2.0 ** (-8.0 / HEADS)
    c[:, C_SLOPE:] = np.array([start ** (i + 1) for i in range(HEADS)], np.float32)
    return c


def hybrid_layer(nc, x, norm_g, w_in, conv_w, a_log, dt_bias, dn_norm_g, w_out, final_norm_g,
                 consts, out):
    with ExitStack() as ctx:
        def sb(name, shape, dt=F32):
            return ctx.enter_context(nc.sbuf_tensor(name, shape, dt))

        def sem(name):
            return ctx.enter_context(nc.semaphore(name))

        u_hi = sb("u_hi", [P, KT, SEQ], F32R)
        u_lo = sb("u_lo", [P, KT, SEQ], F32R)
        mixedT = sb("mixedT", [P, KT, SEQ])
        w_raw = sb("w_raw", [P, RAW, 2, GC])
        w_hi = sb("w_hi", [P, RING, GC], F32R)
        w_lo = sb("w_lo", [P, RING, GC], F32R)
        cst = sb("cst", [P, C_ALL])
        mix = sb("mix", [P, 17920])
        quad_all = sb("quad_all", [P, QUADS, 32])
        conv_all = sb("conv_all", [P, QUADS, 48])
        qp = sb("qp", [P, 32])
        cw = sb("cw", [P, 48])
        ngT = sb("ngT", [P, KT + 1])
        rstd = sb("rstd", [P, 2])
        half = sb("half", [P, 32])
        stat = sb("stat", [P, 16])
        fac = sb("fac", [P, 16])
        negmax = sb("negmax", [P, 8])
        esum = sb("esum", [P, 8])
        rinv = sb("rinv", [P, 8])
        slope4 = sb("slope4", [P, QH])
        hsum = sb("hsum", [P, T, NG])

        ident = cst[:, C_ID:C_ID + P]
        tri = cst[:, C_TRI:C_TRI + P]
        causal = cst[:, C_CAUSAL:C_CAUSAL + P]

        def region(at, n):
            return mix[:, at:at + n]

        rawk, rawq, rawv, gate = (region(1024 * i, 1024) for i in range(4))
        f_k, f_q, f_v = (region(4096 + 1024 * i, 1024) for i in range(3))
        t_k, t_q, t_v = (region(7168 + 1024 * i, 1024) for i in range(3))
        XX = region(10240, 1024)
        XT = region(11264, 1024)
        decay = region(12288, 1024)
        Sst = region(13312, 512)
        Yb = region(13824, 512)
        yv = region(14336, 1024)
        Rb = region(15360, 512)
        QS = region(15872, 512)
        ktail = region(16384, 512)
        sq = region(16896, 1024)
        o_dn = t_q
        AT = f_v
        prob = region(10240, 1536)
        bias = region(7168, 1536)
        pT = region(12288, 1536)
        o_at = yv
        xin = region(0, 8192)
        wba = region(8192, 1024)
        junk = region(9216, 2048)
        cvr = region(11264, 256)
        ngr = region(11520, 128)
        lg = region(11648, 64)
        alog = region(11712, 16)
        dtb = region(11728, 16)
        zz = region(11744, 64)
        spa = region(11808, 32)
        spb = region(11840, 32)
        spc = region(11872, 32)
        ones = region(11904, 128)
        ssx = region(12032, 16)
        lgT = region(12288, SEQ)
        ba = [ring[:, slot].rearrange("p (k n) -> p k n", n=64) for slot in (2, 3) for ring in (w_hi, w_lo)]
        wba_r = wba.rearrange("p (b k n) -> p b k n", b=4, k=KT // 4)
        hbuf = region(0, 8192)
        gfin = region(8192, 4096)

        def by_h(ap, n=P):
            return ap.rearrange("p (h n) -> p h n", n=n)

        def pair(s):
            return lambda ap, half_: ap.rearrange("p h (b two s) -> p h b two s", two=2, s=s)[:, :, :, half_, :]

        proj = [[ctx.enter_context(nc.psum_tensor(f"proj{b}{t}", [P, GC], F32)) for t in range(T)]
                for b in range(2)]
        B = [ctx.enter_context(nc.psum_tensor(f"B{i}", [P, GC], F32)) for i in range(4)]

        ident_in, ng_in, consts_in, small_in, wba_in = (sem(n) for n in ("ident_in", "ng_in", "consts_in", "small_in", "wba_in"))
        x_in = [sem(f"x_in{i}") for i in range(len(XCUT) - 1)]
        w_in_ring = [sem(f"w_landed{i}") for i in range(RAW)]
        hi_ready, lo_ready, tile_used = sem("hi_ready"), sem("lo_ready"), sem("tile_used")
        chunks_asked = sem("chunks_asked")
        evac0, evac1 = sem("evac0"), sem("evac1")
        S = {n: sem(n) for n in (
            "pre_ng", "pre_ngc", "xT", "uhi", "ulo", "xsq", "xss", "rstd_ok", "half_ok", "cvT", "cv_ok",
            "ones_ok", "lg_p", "lg_hi", "ba_hi", "ba_lo", "lgT", "lg_t", "pre_v", "pre_a", "pre_p", "gc_p", "par_ok", "par_a",
            "fT", "bT", "kqT", "gcrow", "kk", "qk", "aT", "yp", "zp", "xtp", "y0p", "o0p", "ksp", "y1p", "o1p", "mT",
            "qp_ok", "tap3", "conv", "silu", "tok", "sqr", "red", "fac_ok", "scaled", "kq_ev", "v_ok",
            "ktail_ok", "gsub", "gmin", "gexp", "at_ok", "qkt_ok", "x_id", "y_ok", "x_ok", "xt_v", "xt_a", "y0_ok", "s_ok", "o0_ok",
            "r_mul", "r_ok", "qs_ok", "y1_ok", "o_ok", "silu_g", "gated", "osq", "ored", "ofac", "onorm", "mix_ok",
            "akT", "a_ev", "sl_ok", "bias_ok", "bias1", "sc", "logit", "amax", "aexp", "arin", "pTp", "pT_ok", "pv", "ao_ok",
            "a_silu", "agated", "amT", "amix_ok",
            "m_hi", "m_lo", "h_in", "gf_in", "h_asked", "rows_done", "h_add", "h_sq", "h_g", "h_fin_a", "h_fin_v", "y_out", "h_red", "h_mean", "h_rstd", "h_gl", "pow_in", "pow_k", "pool_waits")}

        tokens = x.rearrange("b (t p) d -> p (b t) d", p=P)
        out_tokens = out.rearrange("b (t p) d -> p (b t) d", p=P)
        w_in_r = w_in.rearrange("a (k p) n -> p (a k) n", p=P)
        w_out_r = w_out.rearrange("a (k p) n -> p (a k) n", p=P)

        def late_w(u, i):
            return u[:, 2 * i:2 * i + 2, :].rearrange("p a n -> p (a n)")

        block = ctx.enter_context(nc.Block())

        @block.sync
        def _(sp):
            def chunk(src, n, slot, first):
                if not first:
                    sp.wait_ge(lo_ready, 2 * n - 2 * RAW + 2)
                    sp.sem_inc(chunks_asked)
                sp.dma_start(w_raw[:, slot], src).then_inc(w_in_ring[slot], 16)

            def quad_groups(names, q, base):
                for i, name in enumerate(names):
                    col = COL[name] + q * GC if isinstance(q, int) else sp.snap(COL[name] + q * GC)
                    for c in range(KT // 2):
                        first_group = isinstance(q, int) and i == 0
                        if first_group and (c < 2 or c % 2 == 0):
                            part = c if c < 2 else c // 2 + 1
                            lo, hi = XCUT[part:part + 2]
                            sp.dma_start(xin.rearrange("p (t d) -> p t d", t=T)[:, :, lo:hi],
                                         tokens[:, :, lo:hi]).then_inc(x_in[part], 16)
                        if first_group and c == 9:
                            sp.dma_start(wba.rearrange("p (k n) -> p k n", k=KT), w_in_r[:, :, LOGITS:LOGITS + 32]).then_inc(wba_in, 16)
                        if first_group and c == 13:
                            sp.dma_start(cst[:, P:C_ALL], consts[:, P:C_ALL]).then_inc(consts_in, 16)
                            sp.dma_start(cvr.rearrange("p (i n) -> p i n", i=2)[0:96],
                                         conv_w.rearrange("a t (b n) -> (a t b) n", n=P).rearrange("(i r) n -> r i n", i=2)).then_inc(small_in, 16)
                            sp.dma_start(alog, a_log.to_broadcast([P, HEADS])).then_inc(small_in, 16)
                            sp.dma_start(dtb, dt_bias.to_broadcast([P, HEADS])).then_inc(small_in, 16)
                        src = w_in_r[:, 2 * c:2 * c + 2, bass.ds(col, GC)]
                        first = first_group and c < RAW
                        chunk(src, (q * 4 + i) * (KT // 2) + base + c, c % RAW, first)

            quad_groups(("dk", "dq", "dv", "dg"), 0, 0)
            with sp.Fori(1, QUADS) as q:
                quad_groups(("dk", "dq", "dv", "dg"), q, 0)
            with sp.Fori(0, QUADS) as q:
                quad_groups(("ak", "aq", "av", "ag"), q, QUADS * 4 * KT // 2)
            with sp.Fori(0, NG) as j:
                col = sp.snap(j * GC)
                for c in range(KT // 2):
                    if c == 12:
                        sp.wait_ge(S["amT"], QUADS)
                        sp.wait_ge(S["m_lo"], len(M_STEP))
                        sp.sem_inc(S["h_asked"])
                        sp.dma_start(hbuf.rearrange("p (t d) -> p t d", t=T)[:, :, bass.ds(col, GC)],
                                     tokens[:, :, bass.ds(col, GC)]).then_inc(S["h_in"], 16)
                        sp.dma_start(gfin[:, bass.ds(col, GC)],
                                     final_norm_g.rearrange("(a d) -> a d", a=1)[:, bass.ds(col, GC)].to_broadcast([P, GC])).then_inc(S["gf_in"], 16)
                    if c == 15:
                        sp.wait_ge(S["h_in"], 16 * j + 16)
                        sp.wait_ge(S["gf_in"], 16 * j + 16)
                    tile = 2 * c + KT // 2 if c < KT // 4 else 2 * c - KT // 2
                    src = w_out_r[:, tile:tile + 2, bass.ds(col, GC)]
                    chunk(src, j * (KT // 2) + 2 * QUADS * 4 * KT // 2 + c, c % RAW, False)
            for t in range(T):
                for j in (2, 0, 3, 1):
                    sp.wait_ge(S["h_fin_v" if j > 1 else "h_fin_a"], 2 * t + j % 2 + 1)
                    sp.dma_start(out_tokens[:, t, 1024 * j:1024 * j + 1024],
                                 hbuf[:, 4096 * t + 1024 * j:4096 * t + 1024 * j + 1024]).then_inc(S["y_out"], 16)
            sp.wait_ge(S["y_out"], 16 * 4 * T)

        @block.tensor
        def _(pe):
            def bank_free(group):
                pe.wait_ge(evac0, group - 2)
                pe.wait_ge(evac1, group - 2)

            def products(bank, t, k, hi, lo):
                tk = slice(t * P, t * P + P)
                o = proj[bank][t][:, :]
                nc.tensor.matmul(o, u_hi[:, k, tk], hi, start=(k == 0), stop=False)
                nc.tensor.matmul(o, u_hi[:, k, tk], lo, start=False, stop=False)
                return nc.tensor.matmul(o, u_lo[:, k, tk], hi, start=False, stop=(k == KT - 1))

            def run_step(n, k, bank):
                pe.wait_ge(lo_ready, n + 1)
                for t in range(T):
                    mm = products(bank, t, k, w_hi[:, k % RING], w_lo[:, k % RING])
                mm.then_inc(tile_used, 1)

            def turn(dst, src):
                for h in range(QH):
                    mm = nc.tensor.transpose(dst[:, h * P:h * P + P], src(h), ident)
                return mm

            def to_features(src, banks):
                for h in range(QH):
                    for t in range(T):
                        mm = nc.tensor.transpose(B[banks + h // 2][:, (h % 2) * SEQ + t * P:(h % 2) * SEQ + t * P + P],
                                                 src[:, t * GC + h * P:t * GC + h * P + P], ident)
                return mm

            def to_tokens(src, banks):
                for t in range(T):
                    for h in range(QH):
                        mm = nc.tensor.transpose(B[banks + t][:, h * P:h * P + P],
                                                 src[:, h * SEQ + t * P:h * SEQ + t * P + P], ident)
                return mm

            def mms(dst, lhs, rhs, n=P):
                for h in range(QH):
                    mm = nc.tensor.matmul(dst[:, h * n:h * n + n], lhs(h), rhs(h), start=True, stop=True)
                return mm

            def hs(ap, c=0, n=P):
                return lambda h: ap[:, c + h * n:c + h * n + n]

            def fs(ap, t):
                return lambda h: ap[:, h * SEQ + t * P:h * SEQ + t * P + P]

            def turned(m, lv, c):
                if lv < SMALL:
                    pe.wait_ge(S["xt_v"], 2 * SMALL * m + 2 * lv + c + 1)
                else:
                    pe.wait_ge(S["xt_a"], 2 * (LEVELS - SMALL) * m + 2 * (lv - SMALL) + c + 1)

            def dn(m, s):
                if s == 0:
                    pe.wait_ge(evac0, 4 * m + 1)
                    pe.wait_ge(evac1, 4 * m + 1)
                    to_features(rawk, 0).then_inc(S["fT"], 1)
                if s == 4:
                    pe.wait_ge(evac0, 4 * m + 2)
                    pe.wait_ge(evac1, 4 * m + 2)
                    to_features(rawq, 2).then_inc(S["fT"], 1)
                if s == 11:
                    pe.wait_ge(S["silu"], 3 * m + 1)
                    to_tokens(f_k, 0).then_inc(S["bT"], 1)
                if s == 16:
                    pe.wait_ge(S["silu"], 3 * m + 2)
                    to_tokens(f_q, 2).then_inc(S["bT"], 1)
                if s == 20:
                    pe.wait_ge(S["scaled"], 2 * m + 1)
                    to_features(t_k, 0).then_inc(S["kqT"], 1)
                if s == 23:
                    pe.wait_ge(S["kq_ev"], 4 * m + 2)
                    pe.wait_ge(evac0, 4 * m + 3)
                    pe.wait_ge(evac1, 4 * m + 3)
                    to_features(rawv, 0).then_inc(S["fT"], 1)
                if s == 25:
                    pe.wait_ge(S["scaled"], 2 * m + 2)
                    to_features(t_q, 2).then_inc(S["kqT"], 1)
                if s == 28:
                    pe.wait_ge(S["kq_ev"], 4 * m + 4)
                    for c in range(T):
                        for h in range(QH):
                            g = qp[:, c * QH + h:c * QH + h + 1].to_broadcast([P, P])
                            mm = nc.tensor.matmul(B[2 + c][:, h * P:h * P + P], g, tri, start=True, stop=True)
                    mm.then_inc(S["gcrow"], 1)
                if s == 34:
                    pe.wait_ge(S["silu"], 3 * m + 3)
                    to_tokens(f_v, 0).then_inc(S["bT"], 1)
                if s == 37:
                    pe.wait_ge(S["v_ok"], 2 * m + 2)
                    for c in range(T):
                        mms(B[c], fs(f_k, c), fs(f_k, c)).then_inc(S["kk"], 1)
                if s == 38:
                    pe.wait_ge(S["gsub"], 2 * m + 2)
                    for c in range(T):
                        mms(B[2 + c], fs(f_k, c), fs(f_q, c)).then_inc(S["qk"], 1)
                for c in range(T):
                    at, xx, xt, yb = (r[:, c * n:c * n + n] for r, n in ((AT, GC), (XX, GC), (XT, GC), (Yb, 256)))
                    e = s - 48 - c
                    if e >= 0 and e < 6 * (LEVELS - 1) and e % 6 == 0:
                        lv = e // 6 + 1
                        turned(m, lv - 1, c)
                        cols = pair(1 << lv)
                        xc = cols(by_h(xx), 0)
                        for h in range(QH):
                            mm = nc.tensor.matmul(B[c][:, h * 64:h * 64 + 64], at[:, h * P:h * P + P], xc[:, h],
                                                  start=True, stop=True)
                        mm.then_inc(S["yp"], 1)
                    if e >= 0 and e < 6 * (LEVELS - 1) and e % 6 == 2:
                        lv = e // 6 + 1
                        pe.wait_ge(S["qkt_ok"], 2 * m + c + 1)
                        pe.wait_ge(S["y_ok"], 2 * LEVELS * m + 2 * lv + c + 1)
                        mms(B[2 + c], hs(xt), hs(yb, 0, 64), 64).then_inc(S["zp"], 1)
                    if e < 6 * (LEVELS - 1) and e % 6 == 4 and (e + 2) // 6 >= SMALL:
                        lv = (e + 2) // 6
                        pe.wait_ge(S["x_ok"], 2 * LEVELS * m + 2 * lv + c + 1)
                        turn(B[c], hs(xx)).then_inc(S["xtp"], 1)
                if s == 85:
                    turned(m, LEVELS - 1, 0)
                    mms(B[0], hs(XT), hs(t_v)).then_inc(S["y0p"], 1)
                if s == 87:
                    pe.wait_ge(S["y0_ok"], m + 1)
                    mms(B[2], hs(decay), hs(yv)).then_inc(S["o0p"], 1)
                    pe.wait_ge(S["ktail_ok"], m + 1)
                    mms(B[0], hs(ktail), hs(yv)).then_inc(S["o0p"], 1)
                if s == 90:
                    pe.wait_ge(S["s_ok"], m + 1)
                    turned(m, LEVELS - 1, 1)
                    mms(B[1], fs(f_k, 1), hs(Sst)).then_inc(S["ksp"], 1)
                    mms(B[3], fs(f_q, 1), hs(Sst)).then_inc(S["ksp"], 1)
                if s == 94:
                    pe.wait_ge(S["r_ok"], m + 1)
                    mms(B[1], hs(XT, GC), hs(Rb)).then_inc(S["y1p"], 1)
                if s == 96:
                    pe.wait_ge(S["y1_ok"], m + 1)
                    pe.wait_ge(S["qs_ok"], m + 1)
                    mms(B[3], hs(decay, GC), hs(yv, GC)).then_inc(S["o1p"], 1)
                if s == 109:
                    pe.wait_ge(S["onorm"], m + 1)
                    pe.wait_ge(S["o0_ok"], m + 1)
                    to_features(gate, 0).then_inc(S["mT"], 1)
                if s == 126:
                    pe.wait_ge(S["mix_ok"], 2 * m + 2)

            def attn(m, s):
                a = m - QUADS
                if s == 0:
                    pe.wait_ge(evac0, 4 * m + 1)
                    pe.wait_ge(evac1, 4 * m + 1)
                    to_features(rawk, 0).then_inc(S["akT"], 1)
                if s == 2:
                    pe.wait_ge(evac0, 4 * m + 2)
                    pe.wait_ge(evac1, 4 * m + 2)
                    to_features(rawq, 2).then_inc(S["akT"], 1)
                if s == 6 or s == 7:
                    if s == 6:
                        pe.wait_ge(S["a_ev"], 4 * a + 4)
                    for h in range(2 * (s - 6), 2 * (s - 6) + 2):
                        nc.tensor.matmul(B[h][:, 0:P], f_q[:, h * SEQ:h * SEQ + P],
                                         f_k[:, h * SEQ:h * SEQ + P], start=True, stop=True)
                        nc.tensor.matmul(B[h][:, P:3 * P], f_q[:, h * SEQ + P:h * SEQ + SEQ],
                                         f_k[:, h * SEQ:h * SEQ + SEQ], start=True, stop=True).then_inc(S["sc"], 1)
                if s == 20:
                    pe.wait_ge(S["aexp"], 8 * a + 8)
                    for b in range(3):
                        turn(B[b], lambda h: prob[:, h * 384 + b * P:h * 384 + b * P + P]).then_inc(S["pTp"], 1)
                if s == 25:
                    pe.wait_ge(S["pT_ok"], 3 * a + 3)
                    pe.wait_ge(evac0, 4 * m + 3)
                    pe.wait_ge(evac1, 4 * m + 3)
                    mms(B[3], hs(pT), hs(rawv)).then_inc(S["pv"], 1)
                if s == 26:
                    for h in range(QH):
                        nc.tensor.matmul(B[0][:, h * P:h * P + P], pT[:, GC + h * P:GC + h * P + P],
                                         rawv[:, h * P:h * P + P], start=True, stop=False)
                        mm = nc.tensor.matmul(B[0][:, h * P:h * P + P], pT[:, 2 * GC + h * P:2 * GC + h * P + P],
                                              rawv[:, GC + h * P:GC + h * P + P], start=False, stop=True)
                    mm.then_inc(S["pv"], 1)
                if s == 40:
                    pe.wait_ge(S["agated"], a + 1)
                    to_features(gate, 1).then_inc(S["amT"], 1)
                if s == 44:
                    pe.wait_ge(S["amix_ok"], 2 * a + 2)

            pe.wait_ge(ident_in, 16)

            def x_tile(k):
                if k * P in XCUT:
                    pe.wait_ge(x_in[XCUT.index(k * P)], 16)
                if k >= 4:
                    pe.wait_ge(S["ulo"], k - 3)
                elif k == 3:
                    pe.wait_ge(S["pre_ngc"], 1)
                for t in range(T):
                    mm = nc.tensor.transpose(B[k % 4][:, t * P:t * P + P],
                                             xin[:, t * D + k * P:t * D + k * P + P], ident)
                mm.then_inc(S["xT"], 1)

            for k in range(3):
                x_tile(k)
            pe.wait_ge(ng_in, 32)
            nc.tensor.transpose(B[3][:, 0:KT + 1], ngr[0:KT + 1, :], ident[0:KT + 1, 0:KT + 1]).then_inc(S["pre_ng"], 1)
            for k in range(KT):
                if k + 3 < KT:
                    x_tile(k + 3)
                pe.wait_ge(S["ulo"], k + 1)
                run_step(k, k, 1)
            for k in range(KT):
                run_step(KT + k, k, 0)
                if k == 0:
                    for f in range(KT):
                        w = ba[f // 8][:, f % 8]
                        if f % 16 == 0:
                            pe.wait_ge(S["ba_lo"], f // 8 + 2)
                        nc.tensor.matmul(B[0][0:64, 0:SEQ], w, u_hi[:, f, :], start=(f == 0), stop=False)
                        mm = nc.tensor.matmul(B[0][0:64, 0:SEQ], w, u_lo[:, f, :], start=False, stop=(f == KT - 1))
                        if f % 16 == 15:
                            mm.then_inc(S["lg_p"], 1)
                if k == 11:
                    pe.wait_ge(S["lgT"], 1)
                    for t in range(T):
                        mm = nc.tensor.transpose(B[2][:, t * 64:t * 64 + 64], lgT[0:64, t * P:t * P + P], ident[0:64, 0:64])
                    mm.then_inc(S["lg_t"], 1)
                if k == 8:
                    pe.wait_ge(small_in, 16 * 3)
                    for i in range(2):
                        mm = nc.tensor.transpose(B[3][:, 96 * i:96 * i + 96], cvr[0:96, i * P:i * P + P], ident[0:96, 0:96])
                    mm.then_inc(S["cvT"], 1)
            bank_free(3)
            for k in range(KT):
                run_step(2 * KT + k, k, 1)
                if k == 4:
                    pe.wait_ge(S["pre_v"], 8)
                    pe.wait_ge(consts_in, 16)
                    pe.wait_ge(S["ones_ok"], 1)
                    nc.tensor.matmul(B[0][:, 0:32], tri, spc, start=True, stop=True)
                    nc.tensor.matmul(B[1][:, 0:32], ones, spc, start=True, stop=True).then_inc(S["gc_p"], 1)

            def body(m, mixer):
                for s in range(BODY):
                    g, k = s // KT, s % KT
                    if k == 0:
                        bank_free(4 * m + 4 + g)
                    run_step(m * BODY + 3 * KT + s, k, g % 2)
                    mixer(m, s)

            pe.wait_ge(S["par_ok"], 1)
            with pe.Fori(0, QUADS) as m:
                body(m, dn)
            with pe.Fori(QUADS, 2 * QUADS - 1) as m:
                body(m, attn)

            last = 2 * QUADS - 1
            first_out = last * BODY + 4 * KT
            bank_free(4 * last + 4)
            for s in range(2 * KT):
                if s == KT:
                    bank_free(4 * last + 5)
                if s >= KT and s % QH == 0:
                    pe.wait_ge(S["m_lo"], (s - KT) // QH + 1)
                run_step(last * BODY + 3 * KT + s, s % KT, s // KT % 2)
                attn(last, s)

            def out_bank_free(j):
                pe.wait_ge(S["h_add"], 2 * (j - 1))

            bank_free(4 * last + 6)
            for k in range(KT):
                run_step(first_out + KT + k, k, 0)
            def out_group(j, i, tiles):
                out_bank_free(j + i)
                for k in range(tiles):
                    run_step(first_out + (j + i) * KT + k, k, (1 + i) % 2)

            with pe.Fori(2, NG - 2, 2) as j:
                out_group(j, 0, KT)
                out_group(j, 1, KT)
            out_group(NG - 2, 0, KT)
            out_group(NG - 2, 1, KT - LATE)
            for t in range(T):
                for i in range(LATE):
                    k = KT - LATE + i
                    if t == 0:
                        pe.wait_ge(lo_ready, first_out + (NG - 1) * KT + k + 1)
                    mm = products(0, t, k, late_w(u_hi, i), late_w(u_lo, i))
                mm.then_inc(S["rows_done"], 1)

        def split_hi(act, n, k, first=False, late=None):
            to = w_hi[:, k % RING] if late is None else late_w(u_hi, late)
            if k % 2 == 0:
                act.wait_ge(w_in_ring[k // 2 % RAW], 16 * (n // (2 * RAW)) + 16 if isinstance(n, int) else n * 2 - (k % 8) * 2 + 16)
            if late is not None:
                act.wait_ge(tile_used, n - k + 2 * late + 2)
            elif not first:
                act.wait_ge(tile_used, n - RING + 1)
            nc.scalar.copy(to, w_raw[:, k // 2 % RAW, k % 2]).then_inc(hi_ready, 1)

        def split_lo(dve, n, k, late=None):
            hi, lo = (w_hi[:, k % RING], w_lo[:, k % RING]) if late is None else (late_w(u_hi, late), late_w(u_lo, late))
            dve.wait_ge(hi_ready, n + 1)
            nc.vector.tensor_tensor(lo, w_raw[:, k // 2 % RAW, k % 2], hi.bitcast(F32), ALU.subtract).then_inc(lo_ready, 1)

        @block.scalar
        def _(act):
            def evac_t0(group, dst, bank):
                act.wait_ge(tile_used, KT * group)
                nc.scalar.mul(dst[:, 0:GC], proj[bank][0][:, :], rstd[:, 0:1]).then_inc(evac0, 1)

            def tap3(m, i, dst, banks, hh):
                if hh == 0:
                    act.wait_ge(S["fT"], 3 * m + i + 1)
                for h in range(2 * hh, 2 * hh + 2):
                    nc.scalar.mul(dst[:, h * SEQ:h * SEQ + SEQ],
                                  B[banks + h // 2][:, (h % 2) * SEQ:(h % 2) * SEQ + SEQ],
                                  cw[:, (i * QH + h) * TAPS + 3:(i * QH + h) * TAPS + 4]).then_inc(S["tap3"], 1)

            def silu(m, i, f):
                act.wait_ge(S["conv"], 36 * m + 12 * i + 12)
                nc.scalar.activation(f, f, ACT.Silu).then_inc(S["silu"], 1)

            def dn(m, s):
                if s == 1:
                    evac_t0(4 * m + 3, rawv, 1)
                    act.wait_ge(S["qp_ok"], 2 * m + 2)
                if s in (2, 3):
                    tap3(m, 0, f_k, 0, s - 2)
                if s in (5, 6):
                    tap3(m, 1, f_q, 2, s - 5)
                if s == 9:
                    silu(m, 0, f_k)
                if s in (12, 13):
                    if s == 12:
                        act.wait_ge(S["bT"], 3 * m + 1)
                    nc.scalar.copy(t_k[:, (s - 12) * GC:(s - 11) * GC], B[s - 12][:, :]).then_inc(S["tok"], 1)
                if s == 15:
                    silu(m, 1, f_q)
                if s in (17, 18):
                    if s == 17:
                        act.wait_ge(S["bT"], 3 * m + 2)
                    nc.scalar.copy(t_q[:, (s - 17) * GC:(s - 16) * GC], B[2 + s - 17][:, :]).then_inc(S["tok"], 1)
                if s in (21, 22):
                    if s == 21:
                        act.wait_ge(S["kqT"], 2 * m + 1)
                    nc.scalar.copy(f_k[:, (s - 21) * GC:(s - 20) * GC], B[s - 21][:, :]).then_inc(S["kq_ev"], 1)
                if s in (24, 25):
                    tap3(m, 2, f_v, 0, s - 24)
                if s in (26, 27):
                    if s == 26:
                        act.wait_ge(S["kqT"], 2 * m + 2)
                    nc.scalar.copy(f_q[:, (s - 26) * GC:(s - 25) * GC], B[2 + s - 26][:, :]).then_inc(S["kq_ev"], 1)
                if s == 32:
                    silu(m, 2, f_v)
                if s == 33:
                    evac_t0(4 * m + 4, gate, 0)
                if s == 36:
                    act.wait_ge(evac0, 4 * m + 4)
                    act.wait_ge(evac1, 4 * m + 4)
                    nc.scalar.activation(gate, gate, ACT.Silu).then_inc(S["silu_g"], 1)
                if s == 38:
                    act.wait_ge(S["gmin"], 2 * m + 2)
                    nc.scalar.activation(decay, decay, ACT.Exp).then_inc(S["gexp"], 1)
                for c in range(T):
                    e = s - 47 - c
                    if 6 * SMALL <= e < 6 * LEVELS and e % 6 == 0:
                        act.wait_ge(S["xtp"], 2 * (LEVELS - SMALL) * m + 2 * (e // 6 - SMALL) + c + 1)
                        nc.scalar.copy(XT[:, c * GC:c * GC + GC], B[c][:, :]).then_inc(S["xt_a"], 1)
                if s == 65:
                    evac_t0(4 * m + 5, rawk, 1)
                if s == 86:
                    act.wait_ge(S["y0p"], m + 1)
                    nc.scalar.copy(yv[:, 0:GC], B[0][:, :]).then_inc(S["y0_ok"], 1)
                if s == 88:
                    act.wait_ge(S["o0p"], 2 * m + 2)
                    nc.scalar.copy(Sst, B[0][:, :]).then_inc(S["s_ok"], 1)
                if s == 89:
                    nc.scalar.copy(o_dn[:, 0:GC], B[2][:, :]).then_inc(S["o0_ok"], 1)
                if s == 95:
                    act.wait_ge(S["y1p"], m + 1)
                    nc.scalar.copy(yv[:, GC:2 * GC], B[1][:, :]).then_inc(S["y1_ok"], 1)
                if s == 97:
                    evac_t0(4 * m + 6, rawq, 0)
                if s in (110, 111):
                    b = s - 110
                    if b == 0:
                        act.wait_ge(S["mT"], m + 1)
                    nc.scalar.mul(mixedT[:, bass.ds(m * QH + 2 * b, 2), :],
                                  B[b][:, :].rearrange("p (h n) -> p h n", h=2), ngT[:, KT:KT + 1]).then_inc(S["mix_ok"], 1)

            def attn(m, s):
                a = m - QUADS
                if s == 1:
                    evac_t0(4 * m + 3, rawv, 1)
                if s in (2, 3):
                    if s == 2:
                        act.wait_ge(S["akT"], 2 * a + 1)
                    nc.scalar.copy(f_k[:, (s - 2) * GC:(s - 1) * GC], B[s - 2][:, :]).then_inc(S["a_ev"], 1)
                if s in (4, 5):
                    if s == 4:
                        act.wait_ge(S["akT"], 2 * a + 2)
                    nc.scalar.copy(f_q[:, (s - 4) * GC:(s - 3) * GC], B[2 + s - 4][:, :]).then_inc(S["a_ev"], 1)
                if s in (15, 16, 17, 18):
                    h = s - 15
                    if h == 0:
                        act.wait_ge(S["amax"], 2 * a + 2)
                    for t, (lo, n) in enumerate(((0, P), (P, SEQ))):
                        pr = prob[:, h * 384 + lo:h * 384 + lo + n]
                        nc.scalar.activation(pr, pr, ACT.Exp, bias=negmax[:, t * QH + h:t * QH + h + 1],
                                             accum_out=esum[:, t * QH + h:t * QH + h + 1]).then_inc(S["aexp"], 1)
                if s in (21, 22, 23):
                    b = s - 21
                    act.wait_ge(S["pTp"], 3 * a + b + 1)
                    nc.scalar.copy(pT[:, b * GC:b * GC + GC], B[b][:, :]).then_inc(S["pT_ok"], 1)
                if s == 33:
                    evac_t0(4 * m + 4, gate, 0)
                if s == 35:
                    act.wait_ge(evac0, 4 * m + 4)
                    act.wait_ge(evac1, 4 * m + 4)
                    nc.scalar.activation(gate, gate, ACT.Silu).then_inc(S["a_silu"], 1)
                if s in (41, 42):
                    b = s - 41
                    if b == 0:
                        act.wait_ge(S["amT"], a + 1)
                    nc.scalar.copy(mixedT[:, bass.ds(m * QH + 2 * b, 2), :],
                                   B[1 + b][:, :].rearrange("p (h n) -> p h n", h=2)).then_inc(S["amix_ok"], 1)
                if s == 65:
                    evac_t0(4 * m + 5, rawk, 1)
                if s == 97:
                    evac_t0(4 * m + 6, rawq, 0)

            act.dma_start(ident, consts[:, C_ID:C_ID + P]).then_inc(ident_in, 16)
            act.dma_start(ngr[0:KT, :], norm_g.rearrange("a (k p) -> (a k) p", p=P)).then_inc(ng_in, 16)
            act.dma_start(ngr[KT:KT + 1, :], dn_norm_g).then_inc(ng_in, 16)
            act.wait_ge(S["half_ok"], 1)
            nc.scalar.mul(ones, half[:, 0:1].to_broadcast([P, P]), -2.0).then_inc(S["ones_ok"], 1)

            def x_hi(k):
                act.wait_ge(S["xT"], k + 1)
                nc.scalar.mul(u_hi[:, k], B[k % 4][:, 0:SEQ], ngT[:, k:k + 1]).then_inc(S["uhi"], 1)

            split_hi(act, 0, 0, first=True)
            act.wait_ge(S["pre_ngc"], 1)
            x_hi(0)
            split_hi(act, 1, 1, first=True)
            split_hi(act, 2, 2, first=True)
            for k in range(KT):
                if k + 1 < KT:
                    x_hi(k + 1)
                if k == KT - 1:
                    act.wait_ge(wba_in, 16)
                    for b in range(4):
                        act.wait_ge(tile_used, KT - 1 + b // 2)
                        nc.scalar.copy(ba[b][:, :, 0:32], wba_r[:, b]).then_inc(S["ba_hi"], 1)
                    act.wait_ge(S["lg_p"], 1)
                split_hi(act, k + 3, (k + 3) % KT, first=(k < 1))
            for part in x_in:
                act.wait_ge(part, 16)
            act.wait_ge(S["lg_p"], 2)
            for k in range(KT):
                split_hi(act, KT + k + 3, (k + 3) % KT)
                if k == 1:
                    nc.scalar.copy(lgT[0:64, :], B[0][0:64, 0:SEQ]).then_inc(S["lgT"], 1)
                if k < 16:
                    if k >= 2:
                        act.wait_ge(S["xsq"], k - 1)
                    nc.scalar.activation(junk[:, (k % 2) * GC:(k % 2) * GC + GC], xin[:, GC * k:GC * k + GC], ACT.Square,
                                         accum_out=ssx[:, k:k + 1]).then_inc(S["xsq"], 1)
                if k == 20:
                    act.wait_ge(S["rstd_ok"], 1)
                    evac_t0(1, rawk, 1)
                if k == 23:
                    act.wait_ge(small_in, 16 * 3)
                    act.wait_ge(S["pre_v"], 5)
                    nc.scalar.activation(zz[:, 0:32], lg.rearrange("p (t n) -> p t n", t=T)[:, :, 0:HEADS], ACT.Exp,
                                         scale=-1.0).then_inc(S["pre_a"], 1)
                    nc.scalar.activation(spb, spb, ACT.Exp).then_inc(S["pre_a"], 1)
                if k == 24:
                    nc.scalar.activation(alog, alog, ACT.Exp).then_inc(S["pre_a"], 1)
                    act.wait_ge(S["pre_a"], 2)
                    nc.scalar.activation(spb, spb, ACT.Ln, bias=1.0).then_inc(S["pre_a"], 1)
            for k in range(KT):
                split_hi(act, 2 * KT + k + 3, (k + 3) % KT)
                if k == 1:
                    evac_t0(2, rawq, 0)
                if k == 8:
                    act.wait_ge(S["pre_v"], 11)
                    nc.scalar.activation(quad_all[:, :, 24:28], quad_all[:, :, 12:16], ACT.Exp).then_inc(S["par_a"], 1)
                    nc.scalar.activation(quad_all[:, :, 28:32], zz[:, 32:48].rearrange("p (q h) -> p q h", h=QH),
                                         ACT.Exp).then_inc(S["par_a"], 1)

            def body(m, mixer):
                for s in range(BODY):
                    split_hi(act, m * BODY + 3 * KT + s + 3, (s + 3) % KT)
                    mixer(m, s)

            with act.Fori(0, QUADS) as m:
                body(m, dn)
            with act.Fori(QUADS, 2 * QUADS - 1) as m:
                body(m, attn)

            last = 2 * QUADS - 1
            first_out = last * BODY + 4 * KT

            def m_hi(b):
                if b == 0:
                    act.wait_ge(S["mix_ok"], 2 * QUADS)
                    act.wait_ge(S["amix_ok"], 2 * QUADS - 2)
                if b == 2 * QUADS - 1:
                    act.wait_ge(S["amix_ok"], 2 * QUADS)
                act.wait_ge(tile_used, KT * (4 * last + 3) + QH * b + QH)
                tiles = slice(QH * b, QH * b + QH)
                nc.scalar.copy(u_hi[:, tiles], mixedT[:, tiles]).then_inc(S["m_hi"], 1)

            for s in range(2 * KT):
                split_hi(act, last * BODY + 3 * KT + s + 3, (s + 3) % KT)
                attn(last, s)
                if s in M_STEP:
                    m_hi(M_STEP.index(s))

            def h_square(j, g, rows=range(T)):
                for t in rows:
                    act.wait_ge(S["h_add"], 2 * g + t + 1)
                    nc.scalar.activation(w_sq, hbuf[:, bass.ds(j * GC + t * D, GC)], ACT.Square,
                                         accum_out=hsum[:, t, bass.ds(j, 1)]).then_inc(S["h_sq"], 1)
                    act.wait_ge(S["h_sq"], 2 * g + t + 1)

            w_sq = region(12288, GC)
            for i in range(1):
                for k in range(KT):
                    split_hi(act, first_out + KT + k + 3, (k + 3) % KT)
                    if k == 16:
                        h_square(0, 0)
            with act.Fori(2, NG - 1) as j:
                for k in range(KT):
                    split_hi(act, first_out + j * KT + k + 3, (k + 3) % KT)
                    if k == 16:
                        h_square(j - 1, j - 1)
            for k in range(KT):
                if k + 3 < KT:
                    split_hi(act, first_out + (NG - 1) * KT + k + 3, k + 3,
                             late=None if k + 3 < KT - LATE else k + 3 - KT + LATE)
                if k == 16:
                    h_square(NG - 2, NG - 2)
            act.wait_ge(S["h_g"], 2 * (NG - 1))
            for t in range(T):
                h_square(NG - 1, NG - 1, (t,))
                act.wait_ge(S["h_rstd"], t + 1)
                for j in range(2):
                    part = hbuf[:, t * D + 1024 * j:t * D + 1024 * j + 1024]
                    nc.scalar.mul(part, part, rstd[:, t:t + 1]).then_inc(S["h_fin_a"], 1)

        @block.vector
        def _(dve):
            def evac_t1(group, dst, bank):
                dve.wait_ge(tile_used, KT * group)
                nc.vector.tensor_scalar(dst[:, GC:2 * GC], proj[bank][1][:, :], rstd[:, 1:2], None,
                                        ALU.mult).then_inc(evac1, 1)

            def over_h(ap, n=P):
                return ap.unsqueeze(2).to_broadcast([P, ap.shape[1], n])

            def each_h(ap, blocks=QH):
                return ap.unsqueeze(1).to_broadcast([P, blocks, ap.shape[1]])

            def taps(m, i, f, banks, part):
                for n in (2 * part, 2 * part + 1):
                    shift, h = n // QH + 1, n % QH
                    if n < QH:
                        dve.wait_ge(S["tap3"], 12 * m + QH * i + h + 1)
                    else:
                        dve.wait_ge(S["conv"], 36 * m + 12 * i + n - 3)
                    to = f[:, h * SEQ + shift:h * SEQ + SEQ]
                    at = (h % 2) * SEQ
                    w = (i * QH + h) * TAPS + 3 - shift
                    nc.vector.scalar_tensor_tensor(out=to, in0=B[banks + h // 2][:, at:at + SEQ - shift],
                                                   scalar=cw[:, w:w + 1], in1=to,
                                                   op0=ALU.mult, op1=ALU.add).then_inc(S["conv"], 1)

            def dn(m, s):
                if s == 0:
                    nc.vector.tensor_copy(qp[:, :], quad_all[:, bass.ds(m, 1), :].rearrange("p q n -> p (q n)")).then_inc(S["qp_ok"], 1)
                    nc.vector.tensor_copy(cw[:, :], conv_all[:, bass.ds(m, 1), :].rearrange("p q n -> p (q n)")).then_inc(S["qp_ok"], 1)
                if s == 1:
                    evac_t1(4 * m + 3, rawv, 1)
                    dve.wait_ge(S["qp_ok"], 2 * m + 2)
                if 3 <= s < 9:
                    taps(m, 0, f_k, 0, s - 3)
                if 9 <= s < 15:
                    taps(m, 1, f_q, 2, s - 9)
                if 26 <= s < 32:
                    taps(m, 2, f_v, 0, s - 26)
                for i, at in ((0, 15), (1, 21)):
                    if s == at:
                        dve.wait_ge(S["sqr"], 2 * m + i + 1)
                        nc.vector.tensor_reduce(stat[:, 8 * i:8 * i + 8], by_h(sq), AX.X, ALU.add).then_inc(S["red"], 1)
                for i, at, tk in ((0, 18, t_k), (1, 24, t_q)):
                    if s == at:
                        dve.wait_ge(S["fac_ok"], 2 * m + i + 1)
                        nc.vector.tensor_tensor(by_h(tk), by_h(tk), over_h(fac[:, 8 * i:8 * i + 8]), ALU.mult).then_inc(S["scaled"], 1)
                if s in (30, 32):
                    c = (s - 30) // 2
                    if c == 0:
                        dve.wait_ge(S["gcrow"], m + 1)
                    nc.vector.tensor_tensor(by_h(decay[:, c * GC:c * GC + GC]), by_h(B[2 + c][:, :]),
                                            over_h(qp[:, 8 + QH * c:8 + QH * c + QH]), ALU.subtract).then_inc(S["gsub"], 1)
                if s == 33:
                    evac_t1(4 * m + 4, gate, 0)
                if s in (35, 36):
                    t = s - 35
                    if t == 0:
                        dve.wait_ge(S["bT"], 3 * m + 3)
                    nc.vector.tensor_tensor(by_h(t_v[:, t * GC:t * GC + GC]), by_h(B[t][:, :]),
                                            over_h(qp[:, 16 + QH * t:16 + QH * t + QH]), ALU.mult).then_inc(S["v_ok"], 1)
                if s in (39, 40):
                    c = s - 39
                    if c == 0:
                        dve.wait_ge(S["gexp"], m + 1)
                    dve.wait_ge(S["kk"], 2 * m + c + 1)
                    cc = slice(c * GC, c * GC + GC)
                    nc.vector.tensor_tensor(AT[:, cc], B[c][:, :], decay[:, cc], ALU.mult).then_inc(S["at_ok"], 1)
                if s in (41, 42):
                    c = s - 41
                    dve.wait_ge(S["qk"], 2 * m + c + 1)
                    cc = slice(c * GC, c * GC + GC)
                    nc.vector.tensor_tensor(decay[:, cc], B[2 + c][:, :], decay[:, cc], ALU.mult).then_inc(S["qkt_ok"], 1)
                for c in range(T):
                    yb = by_h(Yb[:, c * 256:c * 256 + 256], 64)
                    xx = by_h(XX[:, c * GC:c * GC + GC])
                    e = s - 43 - c
                    if e == 0:
                        dve.wait_ge(S["at_ok"], 2 * m + c + 1)
                        nc.vector.transpose(XT[:, c * GC:c * GC + GC], AT[:, c * GC:c * GC + GC]).then_inc(S["aT"], 1)
                    lv = e // 6
                    if 0 <= lv < LEVELS and e == (1 if lv == 0 else 6 * lv):
                        mask = each_h(cst[:, C_YM + 64 * lv:C_YM + 64 * lv + 64])
                        if lv == 0:
                            dve.wait_ge(S["aT"], 2 * m + c + 1)
                            nc.vector.tensor_tensor(yb, by_h(XT[:, c * GC:c * GC + GC])[:, :, 0:P:2], mask, ALU.mult).then_inc(S["y_ok"], 1)
                        else:
                            dve.wait_ge(S["yp"], 2 * (LEVELS - 1) * m + 2 * (lv - 1) + c + 1)
                            nc.vector.tensor_tensor(yb, by_h(B[c][:, 0:256], 64), mask, ALU.mult).then_inc(S["y_ok"], 1)
                    if 0 <= lv < LEVELS and e == 6 * lv + 2:
                        xc = pair(1 << lv)(xx, 0)
                        if lv == 0:
                            dve.wait_ge(S["y_ok"], 2 * LEVELS * m + c + 1)
                            dve.wait_ge(S["x_id"], m + 1)
                            z = yb
                        else:
                            dve.wait_ge(S["zp"], 2 * (LEVELS - 1) * m + 2 * (lv - 1) + c + 1)
                            z = by_h(B[2 + c][:, 0:256], 64)
                        z = z.rearrange("p h (b s) -> p h b s", s=1 << lv)
                        nc.vector.tensor_tensor(xc, xc, z, ALU.subtract).then_inc(S["x_ok"], 1)
                    if 0 <= lv < SMALL and e == 6 * lv + 3:
                        dve.wait_ge(S["x_ok"], 2 * LEVELS * m + 2 * lv + c + 1)
                        nc.vector.transpose(XT[:, c * GC:c * GC + GC], XX[:, c * GC:c * GC + GC]).then_inc(S["xt_v"], 1)
                if s == 65:
                    evac_t1(4 * m + 5, rawk, 1)
                if s == 91:
                    dve.wait_ge(S["ksp"], 2 * m + 2)
                    nc.vector.tensor_tensor(by_h(Rb), by_h(B[1][:, :]), over_h(qp[:, 24:28]), ALU.mult).then_inc(S["r_mul"], 1)
                if s == 92:
                    dve.wait_ge(S["r_mul"], m + 1)
                    nc.vector.tensor_tensor(Rb, t_v[:, GC:2 * GC], Rb, ALU.subtract).then_inc(S["r_ok"], 1)
                if s == 93:
                    nc.vector.tensor_tensor(by_h(QS), by_h(B[3][:, :]), over_h(qp[:, 24:28]), ALU.mult).then_inc(S["qs_ok"], 1)
                if s == 97:
                    evac_t1(4 * m + 6, rawq, 0)
                if s == 98:
                    dve.wait_ge(S["o1p"], m + 1)
                    dve.wait_ge(S["qs_ok"], m + 1)
                    nc.vector.tensor_tensor(o_dn[:, GC:2 * GC], B[3][:, :], QS, ALU.add).then_inc(S["o_ok"], 1)
                if s == 102:
                    dve.wait_ge(S["osq"], m + 1)
                    nc.vector.tensor_reduce(stat[:, 0:8], by_h(sq), AX.X, ALU.add).then_inc(S["ored"], 1)
                if s == 107:
                    dve.wait_ge(S["ofac"], m + 1)
                    dve.wait_ge(S["gated"], m + 1)
                    nc.vector.tensor_tensor(by_h(gate), by_h(gate), over_h(fac[:, 0:8]), ALU.mult).then_inc(S["onorm"], 1)

            def attn(m, s):
                a = m - QUADS
                if s == 1:
                    evac_t1(4 * m + 3, rawv, 1)
                if 8 <= s < 12:
                    h = s - 8
                    if h == 0:
                        dve.wait_ge(S["bias_ok"], QH * a + QH)
                    dve.wait_ge(S["sc"], QH * a + h + 1)
                    cc = slice(h * 384, h * 384 + 384)
                    nc.vector.scalar_tensor_tensor(out=prob[:, cc], in0=B[h][:, 0:384], scalar=float(P) ** -0.5,
                                                   in1=bias[:, cc], op0=ALU.mult, op1=ALU.add).then_inc(S["logit"], 1)
                if s in (12, 13):
                    t = s - 12
                    if t == 0:
                        dve.wait_ge(S["logit"], QH * a + QH)
                    lo, n = ((0, P), (P, SEQ))[t]
                    nc.vector.tensor_reduce(negmax[:, t * QH:t * QH + QH], by_h(prob, 384)[:, :, lo:lo + n], AX.X, ALU.max,
                                            negate=True).then_inc(S["amax"], 1)
                if s == 20:
                    dve.wait_ge(S["aexp"], 8 * a + 8)
                    nc.vector.reciprocal(rinv[:, :], esum[:, :]).then_inc(S["arin"], 1)
                if s in (27, 28):
                    t = s - 27
                    dve.wait_ge(S["arin"], a + 1)
                    dve.wait_ge(S["pv"], 2 * a + t + 1)
                    nc.vector.tensor_tensor(by_h(o_at[:, t * GC:t * GC + GC]), by_h(B[3 - 3 * t][:, :]),
                                            over_h(rinv[:, t * QH:t * QH + QH]), ALU.mult).then_inc(S["ao_ok"], 1)
                if s == 33:
                    evac_t1(4 * m + 4, gate, 0)
                if s == 37:
                    dve.wait_ge(S["a_silu"], a + 1)
                    dve.wait_ge(S["ao_ok"], 2 * a + 2)
                    nc.vector.tensor_tensor(gate, gate, o_at, ALU.mult).then_inc(S["agated"], 1)
                if s == 65:
                    evac_t1(4 * m + 5, rawk, 1)
                if s == 97:
                    evac_t1(4 * m + 6, rawq, 0)

            nc.vector.memset(half[:, :], -0.5).then_inc(S["half_ok"], 1)
            dve.wait_ge(S["pre_ng"], 1)
            nc.vector.tensor_copy(ngT[:, :], B[3][:, 0:KT + 1]).then_inc(S["pre_ngc"], 1)
            dve.wait_ge(S["pre_ngc"], 1)

            def x_lo(k):
                dve.wait_ge(S["uhi"], k + 1)
                nc.vector.scalar_tensor_tensor(out=u_lo[:, k], in0=B[k % 4][:, 0:SEQ], scalar=ngT[:, k:k + 1],
                                               in1=u_hi[:, k].bitcast(F32), op0=ALU.mult,
                                               op1=ALU.subtract).then_inc(S["ulo"], 1)

            split_lo(dve, 0, 0)
            x_lo(0)
            split_lo(dve, 1, 1)
            split_lo(dve, 2, 2)
            for k in range(KT):
                if k + 1 < KT:
                    x_lo(k + 1)
                if k == KT - 1:
                    for b in range(4):
                        dve.wait_ge(S["ba_hi"], b + 1)
                        nc.vector.tensor_tensor(ba[b][:, :, 32:64], wba_r[:, b],
                                                ba[b][:, :, 0:32].bitcast(F32), ALU.subtract).then_inc(S["ba_lo"], 1)
                split_lo(dve, k + 3, (k + 3) % KT)
            dve.wait_ge(small_in, 16 * 3)
            lgt = lg.rearrange("p (t n) -> p t n", t=T)
            s2 = lambda r: r.rearrange("p (t n) -> p t n", t=T)
            by_quad = lambda r: r.rearrange("p (t q h) -> p q t h", t=T, h=QH)
            for k in range(KT):
                split_lo(dve, KT + k + 3, (k + 3) % KT)
                if k == 17:
                    dve.wait_ge(S["xsq"], 16)
                    nc.vector.tensor_reduce(stat[:, 0:2], ssx.rearrange("p (t n) -> p t n", t=T), AX.X, ALU.add).then_inc(S["xss"], 1)
                    dve.wait_ge(S["xss"], 1)
                    nc.vector.tensor_scalar(stat[:, 2:4], stat[:, 0:2], 1.0 / D, EPS, ALU.mult, ALU.add).then_inc(S["xss"], 1)
                if k == 20:
                    dve.wait_ge(S["rstd_ok"], 1)
                    evac_t1(1, rawk, 1)
                if k == 21:
                    dve.wait_ge(S["lg_t"], 1)
                    for t in range(T):
                        nc.vector.tensor_scalar(lgt[:, t], B[2][:, t * 64:t * 64 + 32], rstd[:, t:t + 1], None, ALU.mult).then_inc(S["lg_hi"], 1)
                    dve.wait_ge(S["lg_hi"], 2)
                    for t in range(T):
                        nc.vector.scalar_tensor_tensor(out=lgt[:, t], in0=B[2][:, t * 64 + 32:t * 64 + 64], scalar=rstd[:, t:t + 1],
                                                       in1=lgt[:, t], op0=ALU.mult, op1=ALU.add).then_inc(S["pre_v"], 1)
                    dve.wait_ge(S["pre_v"], 2)
                    nc.vector.tensor_tensor(s2(spa), lgt[:, :, HEADS:2 * HEADS], each_h(dtb, T), ALU.add).then_inc(S["pre_v"], 1)
                    dve.wait_ge(S["pre_v"], 3)
                    nc.vector.tensor_scalar(zz[:, 32:64], spa, -1.0, None, ALU.mult).then_inc(S["pre_v"], 1)
                    dve.wait_ge(S["pre_v"], 4)
                    nc.vector.tensor_tensor(spb, spa, zz[:, 32:64], ALU.min).then_inc(S["pre_v"], 1)
                if k == 26:
                    dve.wait_ge(S["pre_a"], 4)
                    nc.vector.tensor_scalar(zz[:, 0:32], zz[:, 0:32], 1.0, None, ALU.add).then_inc(S["pre_v"], 1)
                    nc.vector.scalar_tensor_tensor(out=spc, in0=spa, scalar=0.0, in1=spb, op0=ALU.max, op1=ALU.add).then_inc(S["pre_v"], 1)
                    dve.wait_ge(S["pre_v"], 7)
                    nc.vector.scalar_tensor_tensor(out=s2(spc), in0=s2(spc), scalar=-1.0, in1=each_h(alog, T), op0=ALU.mult,
                                                   op1=ALU.mult).then_inc(S["pre_v"], 1)
                if k == 12:
                    dve.wait_ge(S["cvT"], 1)
                    for i in range(2):
                        for j, of in enumerate((1, 0, 2)):
                            to = conv_all[:, :, 16 * j:16 * j + 16].rearrange("p q (h c) -> p c q h", c=TAPS)[:, 2 * i:2 * i + 2]
                            fr = B[3][:, 96 * i:96 * i + 96].rearrange("p (c x q h) -> p x c q h", x=3, q=QUADS, h=QH)[:, of]
                            for c in range(2):
                                nc.vector.tensor_copy(to[:, c], fr[:, c]).then_inc(S["cv_ok"], 1)
            for k in range(KT):
                split_lo(dve, 2 * KT + k + 3, (k + 3) % KT)
                if k == 1:
                    evac_t1(2, rawq, 0)
                if k == 6:
                    dve.wait_ge(S["pre_v"], 8)
                    nc.vector.tensor_copy(quad_all[:, :, 0:8].rearrange("p q (t h) -> p q t h", t=T), by_quad(spc)).then_inc(S["pre_v"], 1)
                    dve.wait_ge(S["gc_p"], 1)
                    nc.vector.tensor_copy(quad_all[:, :, 8:16].rearrange("p q (t h) -> p q t h", t=T), by_quad(B[0][:, 0:32])).then_inc(S["pre_v"], 1)
                    dve.wait_ge(S["pre_v"], 10)
                    nc.vector.tensor_tensor(zz[:, 32:48].rearrange("p (q h) -> p q h", h=QH),
                                            B[1][:, 0:16].rearrange("p (q h) -> p q h", h=QH),
                                            quad_all[:, :, 8:12], ALU.subtract).then_inc(S["pre_v"], 1)
                    dve.wait_ge(S["pre_p"], 1)
                    nc.vector.tensor_copy(quad_all[:, :, 16:24].rearrange("p q (t h) -> p q t h", t=T), by_quad(spa)).then_inc(S["par_ok"], 1)
            dve.wait_ge(S["par_a"], 2)
            dve.wait_ge(S["par_ok"], 1)
            dve.wait_ge(S["cv_ok"], 12)

            def body(m, mixer):
                for s in range(BODY):
                    split_lo(dve, m * BODY + 3 * KT + s + 3, (s + 3) % KT)
                    mixer(m, s)

            with dve.Fori(0, QUADS) as m:
                body(m, dn)
            with dve.Fori(QUADS, 2 * QUADS - 1) as m:
                body(m, attn)

            last = 2 * QUADS - 1
            first_out = last * BODY + 4 * KT

            def m_lo(b):
                dve.wait_ge(S["m_hi"], b + 1)
                tiles = slice(QH * b, QH * b + QH)
                nc.vector.tensor_tensor(u_lo[:, tiles], mixedT[:, tiles],
                                        u_hi[:, tiles].bitcast(F32), ALU.subtract).then_inc(S["m_lo"], 1)

            for s in range(2 * KT):
                split_lo(dve, last * BODY + 3 * KT + s + 3, (s + 3) % KT)
                attn(last, s)
                if s in M_STEP:
                    m_lo(M_STEP.index(s))

            def h_add(j, g, bank, rows=range(T)):
                if rows == range(T):
                    dve.wait_ge(tile_used, KT * (g + 4 * last + 5))
                dve.wait_ge(S["h_in"], 16 * g + 16)
                for t in rows:
                    part = hbuf[:, bass.ds(j * GC + t * D, GC)]
                    nc.vector.tensor_tensor(part, proj[bank][t][:, :], part, ALU.add).then_inc(S["h_add"], 1)

            for k in range(KT):
                split_lo(dve, first_out + KT + k + 3, (k + 3) % KT)
                if k == 12:
                    h_add(0, 0, 1)

            def out_pair(j, final):
                for i in range(2):
                    for k in range(KT):
                        if not (final and i == 1 and k + AHEAD >= KT):
                            late = k + AHEAD - KT + LATE if final and i == 1 and k + AHEAD >= KT - LATE else None
                            split_lo(dve, first_out + (j + i) * KT + k + AHEAD, (k + AHEAD) % KT, late=late)
                        if k == 12:
                            h_add(j + i - 1, j + i - 1, i)

            with dve.Fori(2, NG - 2, 2) as j:
                out_pair(j, False)
            out_pair(NG - 2, True)
            dve.wait_ge(S["h_g"], 2 * (NG - 1))
            dve.wait_ge(S["gf_in"], 16 * NG)
            for t in range(T):
                dve.wait_ge(S["rows_done"], t + 1)
                h_add(NG - 1, NG - 1, 0, (t,))
                dve.wait_ge(S["h_sq"], 2 * NG - 1 + t)
                nc.vector.tensor_reduce(stat[:, t:t + 1], hsum[:, t, :], AX.X, ALU.add).then_inc(S["h_red"], 1)
                dve.wait_ge(S["h_red"], t + 1)
                nc.vector.tensor_scalar(stat[:, 2 + t:3 + t], stat[:, t:t + 1], 1.0 / D, EPS, ALU.mult, ALU.add).then_inc(S["h_mean"], 1)
                part = hbuf[:, t * D + D - GC:t * D + D]
                nc.vector.tensor_tensor(part, part, gfin[:, D - GC:D], ALU.mult).then_inc(S["h_gl"], 1)
                dve.wait_ge(S["h_rstd"], t + 1)
                dve.wait_ge(S["h_gl"], t + 1)
                for j in range(2, 4):
                    part = hbuf[:, t * D + 1024 * j:t * D + 1024 * j + 1024]
                    nc.vector.tensor_scalar(part, part, rstd[:, t:t + 1], None, ALU.mult).then_inc(S["h_fin_v"], 1)

        @block.gpsimd
        def _(pool):
            def over_h(ap, n=P):
                return ap.unsqueeze(2).to_broadcast([P, ap.shape[1], n])

            def each_h(ap, blocks=QH):
                return ap.unsqueeze(1).to_broadcast([P, blocks, ap.shape[1]])

            def square(src, done):
                nc.gpsimd.tensor_tensor(sq, src, src, ALU.mult).then_inc(done, 1)

            def dn(m):
                for i, tk in ((0, t_k), (1, t_q)):
                    pool.wait_ge(S["tok"], 4 * m + 2 * i + 2)
                    if i == 1:
                        pool.wait_ge(S["red"], 2 * m + 1)
                    square(tk, S["sqr"])
                    pool.wait_ge(S["red"], 2 * m + i + 1)
                    pool.sem_inc(S["pool_waits"])
                    st, fa = stat[:, 8 * i:8 * i + 8], fac[:, 8 * i:8 * i + 8]
                    mul = 1.0 if i == 0 else float(P)
                    nc.gpsimd.tensor_scalar(st, st, mul, mul * EPS, ALU.mult, ALU.add).then_inc(S["pow_in"], 1)
                    pool.wait_ge(S["pow_in"], 3 * m + i + 1)
                    if i == 0:
                        nc.gpsimd.tensor_tensor(fa, st, half[:, 0:8], ALU.pow).then_inc(S["pow_k"], 1)
                        pool.wait_ge(S["pow_k"], m + 1)
                        nc.gpsimd.tensor_tensor(fa, fa, qp[:, 16:24], ALU.mult).then_inc(S["fac_ok"], 1)
                    else:
                        nc.gpsimd.tensor_tensor(fa, st, half[:, 0:8], ALU.pow).then_inc(S["fac_ok"], 1)
                pool.wait_ge(S["scaled"], 2 * m + 1)
                nc.gpsimd.tensor_tensor(by_h(ktail), by_h(t_k[:, 0:GC]), over_h(qp[:, 28:32]), ALU.mult).then_inc(S["ktail_ok"], 1)
                for c in range(T):
                    dc = by_h(decay[:, c * GC:c * GC + GC])
                    pool.wait_ge(S["gsub"], 2 * m + c + 1)
                    nc.gpsimd.tensor_tensor(dc, dc, each_h(causal), ALU.add).then_inc(S["gmin"], 1)
                nc.gpsimd.tensor_copy(by_h(XX), each_h(ident, 2 * QH)).then_inc(S["x_id"], 1)
                pool.wait_ge(S["o0_ok"], m + 1)
                pool.wait_ge(S["o_ok"], m + 1)
                square(o_dn, S["osq"])
                pool.wait_ge(S["silu_g"], m + 1)
                nc.gpsimd.tensor_tensor(gate, gate, o_dn, ALU.mult).then_inc(S["gated"], 1)
                pool.wait_ge(S["ored"], m + 1)
                pool.sem_inc(S["pool_waits"])
                nc.gpsimd.tensor_scalar(stat[:, 0:8], stat[:, 0:8], 1.0 / P, EPS, ALU.mult, ALU.add).then_inc(S["pow_in"], 1)
                pool.wait_ge(S["pow_in"], 3 * m + 3)
                nc.gpsimd.tensor_tensor(fac[:, 0:8], stat[:, 0:8], half[:, 0:8], ALU.pow).then_inc(S["ofac"], 1)

            def attn(m):
                a = m - QUADS
                pool.wait_ge(S["akT"], 2 * a + 1)
                nc.gpsimd.tensor_copy(slope4[:, :], cst[:, bass.ds(C_SLOPE + a * QH, QH)]).then_inc(S["sl_ok"], 1)
                pool.wait_ge(S["sl_ok"], a + 1)
                pool.sem_inc(S["pool_waits"])
                for h in range(QH):
                    nc.gpsimd.tensor_scalar(bias[:, h * 384:h * 384 + 384], cst[:, C_DIST:C_DIST + 384], slope4[:, h:h + 1],
                                            None, ALU.mult).then_inc(S["bias1"], 1)
                for h in range(QH):
                    bh = bias[:, h * 384:h * 384 + 384]
                    pool.wait_ge(S["bias1"], QH * a + h + 1)
                    nc.gpsimd.tensor_tensor(bh, bh, cst[:, C_LOGN:C_LOGN + 384], ALU.add).then_inc(S["bias_ok"], 1)

            pool.wait_ge(S["xss"], 2)
            pool.wait_ge(S["half_ok"], 1)
            nc.gpsimd.tensor_tensor(rstd[:, :], stat[:, 2:4], half[:, 0:2], ALU.pow).then_inc(S["rstd_ok"], 1)
            pool.wait_ge(S["pre_v"], 8)
            nc.gpsimd.tensor_tensor(spa, zz[:, 0:32], half[:, :], ALU.pow).then_inc(S["pre_p"], 1)

            with pool.Fori(0, QUADS) as m:
                dn(m)
            with pool.Fori(QUADS, 2 * QUADS) as m:
                attn(m)

            with pool.Fori(0, NG - 1) as j:
                pool.wait_ge(S["gf_in"], 16 * j + 16)
                for t in range(T):
                    pool.wait_ge(S["h_sq"], 2 * j + t + 1)
                    part = hbuf[:, bass.ds(j * GC + t * D, GC)]
                    nc.gpsimd.tensor_tensor(part, part, gfin[:, bass.ds(j * GC, GC)], ALU.mult).then_inc(S["h_g"], 1)
            for t in range(T):
                pool.wait_ge(S["h_mean"], t + 1)
                nc.gpsimd.tensor_tensor(rstd[:, t:t + 1], stat[:, 2 + t:3 + t], half[:, 0:1], ALU.pow).then_inc(S["h_rstd"], 1)


_INS = ["x", "norm_g", "w_in", "conv_w", "a_log", "dt_bias", "dn_norm_g", "w_out", "final_norm_g"]


def kernel(**inputs):
    import concourse.bacc as bacc
    from concourse.bass_utils import run_bass_kernel_spmd

    nc = bacc.Bacc("TRN2", target_bir_lowering=False, num_devices=1)
    arrays, args = {}, []
    for name in _INS:
        a = np.ascontiguousarray(inputs[name])
        arrays[f"in_{name}"] = a
        args.append(nc.dram_tensor(f"in_{name}", a.shape, mybir.dt.from_np(a.dtype), kind="ExternalInput").ap())
    table = constant_table()
    arrays["constants"] = table
    args.append(nc.dram_tensor("constants", table.shape, F32, kind="ExternalInput").ap())
    shape = inputs["x"].shape
    args.append(nc.dram_tensor("out", shape, F32, kind="ExternalOutput").ap())
    hybrid_layer(nc, *args)
    r = run_bass_kernel_spmd(nc, [arrays], core_ids=[0])
    return r.results[0]["out"]
```

```python
from contextlib import ExitStack

import numpy as np

import concourse.bass as bass
from concourse import mybir

F32 = mybir.dt.float32
F32R = mybir.dt.float32r
ACT = mybir.ActivationFunctionType
ALU = mybir.AluOpType
AX = mybir.AxisListType

P = 128
SEQ = 256
T = SEQ // P
D = 4096
KT = D // P
HEADS = 16
WIDTH = HEADS * P
QH = 4
GC = QH * P
QUADS = HEADS // QH
COL = {"aq": 0, "ak": WIDTH, "av": 2 * WIDTH, "ag": 3 * WIDTH,
       "dq": 4 * WIDTH, "dk": 5 * WIDTH, "dv": 6 * WIDTH, "dg": 7 * WIDTH}
LOGITS = 8 * WIDTH
TAPS = 4
LEVELS = 7
SMALL = 5
EPS = 1e-6
NEG = -1.0e30
BODY = 4 * KT
RAW = 4
RING = 4
AHEAD = 3
NG = D // GC
LATE = 8
XCUT = (0, 2 * P) + tuple(range(4 * P, D + 1, 4 * P))
M_STEP = (19, 20, 24, 25, 26, 29, 30, 43)

C_ID, C_TRI, C_CAUSAL, C_YM = 0, 128, 256, 384
C_DIST = C_YM + LEVELS * 64
C_LOGN = C_DIST + 384
C_SLOPE = C_LOGN + 384
C_ALL = C_SLOPE + HEADS


def constant_table():
    c = np.zeros((P, C_ALL), np.float32)
    p = np.arange(P)[:, None]
    f = np.arange(P)[None, :]
    c[:, C_ID:C_ID + P] = p == f
    c[:, C_TRI:C_TRI + P] = p <= f
    c[:, C_CAUSAL:C_CAUSAL + P] = np.where(p <= f, 0.0, NEG)
    n = np.arange(64)[None, :]
    for lv in range(LEVELS):
        s = 1 << lv
        c[:, C_YM + 64 * lv:C_YM + 64 * lv + 64] = (p // (2 * s) == n // s) & (p % (2 * s) >= s)
    dist = np.concatenate([p - f, P + p - np.arange(SEQ)[None, :]], axis=1)
    count = np.zeros(dist.shape)
    for window, dilation in ((128, 1), (512, 4), (2048, 16)):
        count += (dist >= 0) & (dist <= window) & (dist % dilation == 0)
    c[:, C_DIST:C_DIST + 384] = -np.where(count > 0, dist, 0)
    c[:, C_LOGN:C_LOGN + 384] = np.where(count > 0, np.log(np.maximum(count, 1)), NEG)
    start = 2.0 ** (-8.0 / HEADS)
    c[:, C_SLOPE:] = np.array([start ** (i + 1) for i in range(HEADS)], np.float32)
    return c


def hybrid_layer(nc, x, norm_g, w_in, conv_w, a_log, dt_bias, dn_norm_g, w_out, final_norm_g,
                 consts, out):
    with ExitStack() as ctx:
        def sb(name, shape, dt=F32):
            return ctx.enter_context(nc.sbuf_tensor(name, shape, dt))

        def sem(name):
            return ctx.enter_context(nc.semaphore(name))

        u_hi = sb("u_hi", [P, KT, SEQ], F32R)
        u_lo = sb("u_lo", [P, KT, SEQ], F32R)
        mixedT = sb("mixedT", [P, KT, SEQ])
        w_raw = sb("w_raw", [P, RAW, 2, GC])
        w_hi = sb("w_hi", [P, RING, GC], F32R)
        w_lo = sb("w_lo", [P, RING, GC], F32R)
        tables = sb("tables", [P, C_ALL])
        mix = sb("mix", [P, 17920])
        quad_all = sb("quad_all", [P, QUADS, 32])
        conv_all = sb("conv_all", [P, QUADS, 48])
        quad = sb("quad", [P, 32])
        conv_w4 = sb("conv_w4", [P, 48])
        ngT = sb("ngT", [P, KT + 1])
        rstd = sb("rstd", [P, 2])
        half = sb("half", [P, 32])
        stat = sb("stat", [P, 16])
        fac = sb("fac", [P, 16])
        negmax = sb("negmax", [P, 8])
        esum = sb("esum", [P, 8])
        rinv = sb("rinv", [P, 8])
        slope4 = sb("slope4", [P, QH])
        hsum = sb("hsum", [P, T, NG])

        ident = tables[:, C_ID:C_ID + P]
        tri = tables[:, C_TRI:C_TRI + P]
        causal = tables[:, C_CAUSAL:C_CAUSAL + P]

        def region(at, n):
            return mix[:, at:at + n]

        rawk, rawq, rawv, gate = (region(1024 * i, 1024) for i in range(4))
        f_k, f_q, f_v = (region(4096 + 1024 * i, 1024) for i in range(3))
        t_k, t_q, t_v = (region(7168 + 1024 * i, 1024) for i in range(3))
        XX = region(10240, 1024)
        XT = region(11264, 1024)
        decay = region(12288, 1024)
        state = region(13312, 512)
        Yb = region(13824, 512)
        ysol = region(14336, 1024)
        resid = region(15360, 512)
        qS = region(15872, 512)
        ktail = region(16384, 512)
        sq = region(16896, 1024)
        o_dn = t_q
        AT = f_v
        prob = region(10240, 1536)
        bias = region(7168, 1536)
        pT = region(12288, 1536)
        o_at = ysol
        xin = region(0, 8192)
        wba = region(8192, 1024)
        scrap = region(9216, 2048)
        conv_rows = region(11264, 256)
        norm_rows = region(11520, 128)
        logits = region(11648, 64)
        exp_a = region(11712, 16)
        dt_all = region(11728, 16)
        scal64 = region(11744, 64)
        beta_a = region(11808, 32)
        soft = region(11840, 32)
        g_all = region(11872, 32)
        ones = region(11904, 128)
        ssx = region(12032, 16)
        lgT = region(12288, SEQ)
        ba = [ring[:, slot].rearrange("p (k n) -> p k n", n=64) for slot in (2, 3) for ring in (w_hi, w_lo)]
        wba_r = wba.rearrange("p (b k n) -> p b k n", b=4, k=KT // 4)
        hbuf = region(0, 8192)
        gfin = region(8192, 4096)

        def by_h(ap, n=P):
            return ap.rearrange("p (h n) -> p h n", n=n)

        def pair(s):
            return lambda ap, half_: ap.rearrange("p h (b two s) -> p h b two s", two=2, s=s)[:, :, :, half_, :]

        proj = [[ctx.enter_context(nc.psum_tensor(f"proj{b}{t}", [P, GC], F32)) for t in range(T)]
                for b in range(2)]
        B = [ctx.enter_context(nc.psum_tensor(f"B{i}", [P, GC], F32)) for i in range(4)]

        ident_in, ng_in, consts_in, small_in, wba_in = (sem(n) for n in ("ident_in", "ng_in", "consts_in", "small_in", "wba_in"))
        x_in = [sem(f"x_in{i}") for i in range(len(XCUT) - 1)]
        w_in_ring = [sem(f"w_landed{i}") for i in range(RAW)]
        hi_ready, lo_ready, tile_used = sem("hi_ready"), sem("lo_ready"), sem("tile_used")
        chunks_asked = sem("chunks_asked")
        evac0, evac1 = sem("evac0"), sem("evac1")
        S = {n: sem(n) for n in (
            "ng_turned",
            "ngT_ok",
            "half_ok",
            "ones_ok",
            "xT",
            "uhi",
            "ulo",
            "xsq",
            "xmean_ok",
            "rstd_ok",
            "ba_hi",
            "ba_lo",
            "logits_mm",
            "lgT",
            "logits_turned",
            "logits_hi",
            "scalars_v",
            "scalars_a",
            "beta_ok",
            "gc_mm",
            "par_v",
            "par_a",
            "conv_turned",
            "cv_ok",
            "qp_ok",
            "to_feat",
            "tap3",
            "conv",
            "silu",
            "to_tok",
            "tok",
            "sqr",
            "sumsq_ok",
            "pow_in",
            "pow_k",
            "fac_ok",
            "scaled",
            "kq_feat",
            "kq_ev",
            "v_ok",
            "ktail_ok",
            "gcrow",
            "gsub",
            "gmask_ok",
            "gexp",
            "kk_mm",
            "qk_mm",
            "at_ok",
            "qkt_ok",
            "a_turned",
            "x_id",
            "ax_mm",
            "y_ok",
            "xax_mm",
            "x_ok",
            "xt_v",
            "x_turned",
            "xt_a",
            "y0_mm",
            "y0_ok",
            "o0_mm",
            "o0_ok",
            "s_ok",
            "state_mm",
            "r_mul",
            "r_ok",
            "qs_ok",
            "y1_mm",
            "y1_ok",
            "o1_mm",
            "o_ok",
            "silu_g",
            "osq",
            "ored",
            "ofac",
            "gated",
            "onorm",
            "out_feat",
            "mix_ok",
            "akq_feat",
            "akq_ok",
            "sl_ok",
            "bias1",
            "bias_ok",
            "scores_mm",
            "logit",
            "amax",
            "aexp",
            "arin",
            "prob_turned",
            "pT_ok",
            "pv_mm",
            "ao_ok",
            "a_silu",
            "agated",
            "aout_feat",
            "amix_ok",
            "m_hi",
            "m_lo",
            "h_in",
            "gf_in",
            "rows_done",
            "h_add",
            "h_sq",
            "h_g",
            "h_g_last",
            "h_red",
            "h_mean",
            "h_rstd",
            "h_fin_a",
            "h_fin_v",
            "y_out",
            "h_asked",
            "pool_waits",
        )}

        tokens = x.rearrange("b (t p) d -> p (b t) d", p=P)
        out_tokens = out.rearrange("b (t p) d -> p (b t) d", p=P)
        w_in_r = w_in.rearrange("a (k p) n -> p (a k) n", p=P)
        w_out_r = w_out.rearrange("a (k p) n -> p (a k) n", p=P)

        def late_w(u, i):
            return u[:, 2 * i:2 * i + 2, :].rearrange("p a n -> p (a n)")

        block = ctx.enter_context(nc.Block())

        @block.sync
        def _(sp):
            def chunk(src, n, slot, first):
                if not first:
                    sp.wait_ge(lo_ready, 2 * n - 2 * RAW + 2)
                    sp.sem_inc(chunks_asked)
                sp.dma_start(w_raw[:, slot], src).then_inc(w_in_ring[slot], 16)

            def quad_groups(names, q, base):
                for i, name in enumerate(names):
                    col = COL[name] + q * GC if isinstance(q, int) else sp.snap(COL[name] + q * GC)
                    for c in range(KT // 2):
                        first_group = isinstance(q, int) and i == 0
                        if first_group and (c < 2 or c % 2 == 0):
                            part = c if c < 2 else c // 2 + 1
                            lo, hi = XCUT[part:part + 2]
                            sp.dma_start(xin.rearrange("p (t d) -> p t d", t=T)[:, :, lo:hi],
                                         tokens[:, :, lo:hi]).then_inc(x_in[part], 16)
                        if first_group and c == 9:
                            sp.dma_start(wba.rearrange("p (k n) -> p k n", k=KT), w_in_r[:, :, LOGITS:LOGITS + 32]).then_inc(wba_in, 16)
                        if first_group and c == 13:
                            sp.dma_start(tables[:, P:C_ALL], consts[:, P:C_ALL]).then_inc(consts_in, 16)
                            sp.dma_start(conv_rows.rearrange("p (i n) -> p i n", i=2)[0:96],
                                         conv_w.rearrange("a t (b n) -> (a t b) n", n=P).rearrange("(i r) n -> r i n", i=2)).then_inc(small_in, 16)
                            sp.dma_start(exp_a, a_log.to_broadcast([P, HEADS])).then_inc(small_in, 16)
                            sp.dma_start(dt_all, dt_bias.to_broadcast([P, HEADS])).then_inc(small_in, 16)
                        src = w_in_r[:, 2 * c:2 * c + 2, bass.ds(col, GC)]
                        first = first_group and c < RAW
                        chunk(src, (q * 4 + i) * (KT // 2) + base + c, c % RAW, first)

            sp.dma_start(ident, consts[:, C_ID:C_ID + P]).then_inc(ident_in, 16)
            quad_groups(("dk", "dq", "dv", "dg"), 0, 0)
            with sp.Fori(1, QUADS) as q:
                quad_groups(("dk", "dq", "dv", "dg"), q, 0)
            with sp.Fori(0, QUADS) as q:
                quad_groups(("ak", "aq", "av", "ag"), q, QUADS * 4 * KT // 2)
            with sp.Fori(0, NG) as j:
                col = sp.snap(j * GC)
                for c in range(KT // 2):
                    if c == 12:
                        sp.wait_ge(S["aout_feat"], QUADS)
                        sp.wait_ge(S["m_lo"], len(M_STEP))
                        sp.sem_inc(S["h_asked"])
                        sp.dma_start(hbuf.rearrange("p (t d) -> p t d", t=T)[:, :, bass.ds(col, GC)],
                                     tokens[:, :, bass.ds(col, GC)]).then_inc(S["h_in"], 16)
                        sp.dma_start(gfin[:, bass.ds(col, GC)],
                                     final_norm_g.rearrange("(a d) -> a d", a=1)[:, bass.ds(col, GC)].to_broadcast([P, GC])).then_inc(S["gf_in"], 16)
                    if c == 15:
                        sp.wait_ge(S["h_in"], 16 * j + 16)
                        sp.wait_ge(S["gf_in"], 16 * j + 16)
                    tile = 2 * c + KT // 2 if c < KT // 4 else 2 * c - KT // 2
                    src = w_out_r[:, tile:tile + 2, bass.ds(col, GC)]
                    chunk(src, j * (KT // 2) + 2 * QUADS * 4 * KT // 2 + c, c % RAW, False)
            for t in range(T):
                for j in (2, 0, 3, 1):
                    sp.wait_ge(S["h_fin_v" if j > 1 else "h_fin_a"], 2 * t + j % 2 + 1)
                    sp.dma_start(out_tokens[:, t, 1024 * j:1024 * j + 1024],
                                 hbuf[:, 4096 * t + 1024 * j:4096 * t + 1024 * j + 1024]).then_inc(S["y_out"], 16)
            sp.wait_ge(S["y_out"], 16 * 4 * T)

        @block.tensor
        def _(pe):
            def bank_free(group):
                pe.wait_ge(evac0, group - 2)
                pe.wait_ge(evac1, group - 2)

            def products(bank, t, k, hi, lo):
                tk = slice(t * P, t * P + P)
                o = proj[bank][t][:, :]
                nc.tensor.matmul(o, u_hi[:, k, tk], hi, start=(k == 0), stop=False)
                nc.tensor.matmul(o, u_hi[:, k, tk], lo, start=False, stop=False)
                return nc.tensor.matmul(o, u_lo[:, k, tk], hi, start=False, stop=(k == KT - 1))

            def run_step(n, k, bank):
                pe.wait_ge(lo_ready, n + 1)
                for t in range(T):
                    mm = products(bank, t, k, w_hi[:, k % RING], w_lo[:, k % RING])
                mm.then_inc(tile_used, 1)

            def turn(dst, src):
                for h in range(QH):
                    mm = nc.tensor.transpose(dst[:, h * P:h * P + P], src(h), ident)
                return mm

            def to_features(src, banks):
                for h in range(QH):
                    for t in range(T):
                        mm = nc.tensor.transpose(B[banks + h // 2][:, (h % 2) * SEQ + t * P:(h % 2) * SEQ + t * P + P],
                                                 src[:, t * GC + h * P:t * GC + h * P + P], ident)
                return mm

            def to_tokens(src, banks):
                for t in range(T):
                    for h in range(QH):
                        mm = nc.tensor.transpose(B[banks + t][:, h * P:h * P + P],
                                                 src[:, h * SEQ + t * P:h * SEQ + t * P + P], ident)
                return mm

            def mms(dst, lhs, rhs, n=P):
                for h in range(QH):
                    mm = nc.tensor.matmul(dst[:, h * n:h * n + n], lhs(h), rhs(h), start=True, stop=True)
                return mm

            def hs(ap, c=0, n=P):
                return lambda h: ap[:, c + h * n:c + h * n + n]

            def fs(ap, t):
                return lambda h: ap[:, h * SEQ + t * P:h * SEQ + t * P + P]

            def turned(m, lv, c):
                if lv < SMALL:
                    pe.wait_ge(S["xt_v"], 2 * SMALL * m + 2 * lv + c + 1)
                else:
                    pe.wait_ge(S["xt_a"], 2 * (LEVELS - SMALL) * m + 2 * (lv - SMALL) + c + 1)

            def dn(m, s):
                if s == 0:
                    pe.wait_ge(evac0, 4 * m + 1)
                    pe.wait_ge(evac1, 4 * m + 1)
                    to_features(rawk, 0).then_inc(S["to_feat"], 1)
                if s == 4:
                    pe.wait_ge(evac0, 4 * m + 2)
                    pe.wait_ge(evac1, 4 * m + 2)
                    to_features(rawq, 2).then_inc(S["to_feat"], 1)
                if s == 11:
                    pe.wait_ge(S["silu"], 3 * m + 1)
                    to_tokens(f_k, 0).then_inc(S["to_tok"], 1)
                if s == 17:
                    pe.wait_ge(S["silu"], 3 * m + 2)
                    to_tokens(f_q, 2).then_inc(S["to_tok"], 1)
                if s == 20:
                    pe.wait_ge(S["scaled"], 2 * m + 1)
                    to_features(t_k, 0).then_inc(S["kq_feat"], 1)
                if s == 23:
                    pe.wait_ge(S["kq_ev"], 4 * m + 2)
                    pe.wait_ge(evac0, 4 * m + 3)
                    pe.wait_ge(evac1, 4 * m + 3)
                    to_features(rawv, 0).then_inc(S["to_feat"], 1)
                if s == 26:
                    pe.wait_ge(S["scaled"], 2 * m + 2)
                    to_features(t_q, 2).then_inc(S["kq_feat"], 1)
                if s == 29:
                    pe.wait_ge(S["kq_ev"], 4 * m + 4)
                    for c in range(T):
                        for h in range(QH):
                            g = quad[:, c * QH + h:c * QH + h + 1].to_broadcast([P, P])
                            mm = nc.tensor.matmul(B[2 + c][:, h * P:h * P + P], g, tri, start=True, stop=True)
                    mm.then_inc(S["gcrow"], 1)
                if s == 34:
                    pe.wait_ge(S["silu"], 3 * m + 3)
                    to_tokens(f_v, 0).then_inc(S["to_tok"], 1)
                if s == 37:
                    pe.wait_ge(S["v_ok"], 2 * m + 2)
                    for c in range(T):
                        mms(B[c], fs(f_k, c), fs(f_k, c)).then_inc(S["kk_mm"], 1)
                if s == 38:
                    pe.wait_ge(S["gsub"], 2 * m + 2)
                    for c in range(T):
                        mms(B[2 + c], fs(f_k, c), fs(f_q, c)).then_inc(S["qk_mm"], 1)
                for c in range(T):
                    at, xx, xt, yb = (r[:, c * n:c * n + n] for r, n in ((AT, GC), (XX, GC), (XT, GC), (Yb, 256)))
                    e = s - 48 - c
                    if e >= 0 and e < 6 * (LEVELS - 1) and e % 6 == 0:
                        lv = e // 6 + 1
                        turned(m, lv - 1, c)
                        cols = pair(1 << lv)
                        xc = cols(by_h(xx), 0)
                        for h in range(QH):
                            mm = nc.tensor.matmul(B[c][:, h * 64:h * 64 + 64], at[:, h * P:h * P + P], xc[:, h],
                                                  start=True, stop=True)
                        mm.then_inc(S["ax_mm"], 1)
                    if e >= 0 and e < 6 * (LEVELS - 1) and e % 6 == 2:
                        lv = e // 6 + 1
                        pe.wait_ge(S["qkt_ok"], 2 * m + c + 1)
                        pe.wait_ge(S["y_ok"], 2 * LEVELS * m + 2 * lv + c + 1)
                        mms(B[2 + c], hs(xt), hs(yb, 0, 64), 64).then_inc(S["xax_mm"], 1)
                    if e < 6 * (LEVELS - 1) and e % 6 == 4 and (e + 2) // 6 >= SMALL:
                        lv = (e + 2) // 6
                        pe.wait_ge(S["x_ok"], 2 * LEVELS * m + 2 * lv + c + 1)
                        turn(B[c], hs(xx)).then_inc(S["x_turned"], 1)
                if s == 85:
                    turned(m, LEVELS - 1, 0)
                    mms(B[0], hs(XT), hs(t_v)).then_inc(S["y0_mm"], 1)
                if s == 87:
                    pe.wait_ge(S["y0_ok"], m + 1)
                    mms(B[2], hs(decay), hs(ysol)).then_inc(S["o0_mm"], 1)
                    pe.wait_ge(S["ktail_ok"], m + 1)
                    mms(B[0], hs(ktail), hs(ysol)).then_inc(S["o0_mm"], 1)
                if s == 90:
                    pe.wait_ge(S["s_ok"], m + 1)
                    turned(m, LEVELS - 1, 1)
                    mms(B[1], fs(f_k, 1), hs(state)).then_inc(S["state_mm"], 1)
                    mms(B[3], fs(f_q, 1), hs(state)).then_inc(S["state_mm"], 1)
                if s == 94:
                    pe.wait_ge(S["r_ok"], m + 1)
                    mms(B[1], hs(XT, GC), hs(resid)).then_inc(S["y1_mm"], 1)
                if s == 96:
                    pe.wait_ge(S["y1_ok"], m + 1)
                    pe.wait_ge(S["qs_ok"], m + 1)
                    mms(B[3], hs(decay, GC), hs(ysol, GC)).then_inc(S["o1_mm"], 1)
                if s == 109:
                    pe.wait_ge(S["onorm"], m + 1)
                    pe.wait_ge(S["o0_ok"], m + 1)
                    to_features(gate, 0).then_inc(S["out_feat"], 1)
                if s == 126:
                    pe.wait_ge(S["mix_ok"], 2 * m + 2)

            def attn(m, s):
                a = m - QUADS
                if s == 0:
                    pe.wait_ge(evac0, 4 * m + 1)
                    pe.wait_ge(evac1, 4 * m + 1)
                    to_features(rawk, 0).then_inc(S["akq_feat"], 1)
                if s == 2:
                    pe.wait_ge(evac0, 4 * m + 2)
                    pe.wait_ge(evac1, 4 * m + 2)
                    to_features(rawq, 2).then_inc(S["akq_feat"], 1)
                if s == 6 or s == 7:
                    if s == 6:
                        pe.wait_ge(S["akq_ok"], 4 * a + 4)
                    for h in range(2 * (s - 6), 2 * (s - 6) + 2):
                        nc.tensor.matmul(B[h][:, 0:P], f_q[:, h * SEQ:h * SEQ + P],
                                         f_k[:, h * SEQ:h * SEQ + P], start=True, stop=True)
                        nc.tensor.matmul(B[h][:, P:3 * P], f_q[:, h * SEQ + P:h * SEQ + SEQ],
                                         f_k[:, h * SEQ:h * SEQ + SEQ], start=True, stop=True).then_inc(S["scores_mm"], 1)
                if s == 20:
                    pe.wait_ge(S["aexp"], 8 * a + 8)
                    for b in range(3):
                        turn(B[b], lambda h: prob[:, h * 384 + b * P:h * 384 + b * P + P]).then_inc(S["prob_turned"], 1)
                if s == 25:
                    pe.wait_ge(S["pT_ok"], 3 * a + 3)
                    pe.wait_ge(evac0, 4 * m + 3)
                    pe.wait_ge(evac1, 4 * m + 3)
                    mms(B[3], hs(pT), hs(rawv)).then_inc(S["pv_mm"], 1)
                if s == 26:
                    for h in range(QH):
                        nc.tensor.matmul(B[0][:, h * P:h * P + P], pT[:, GC + h * P:GC + h * P + P],
                                         rawv[:, h * P:h * P + P], start=True, stop=False)
                        mm = nc.tensor.matmul(B[0][:, h * P:h * P + P], pT[:, 2 * GC + h * P:2 * GC + h * P + P],
                                              rawv[:, GC + h * P:GC + h * P + P], start=False, stop=True)
                    mm.then_inc(S["pv_mm"], 1)
                if s == 40:
                    pe.wait_ge(S["agated"], a + 1)
                    to_features(gate, 1).then_inc(S["aout_feat"], 1)
                if s == 44:
                    pe.wait_ge(S["amix_ok"], 2 * a + 2)

            pe.wait_ge(ident_in, 16)

            def x_tile(k):
                if k * P in XCUT:
                    pe.wait_ge(x_in[XCUT.index(k * P)], 16)
                if k >= 4:
                    pe.wait_ge(S["ulo"], k - 3)
                elif k == 3:
                    pe.wait_ge(S["ngT_ok"], 1)
                for t in range(T):
                    mm = nc.tensor.transpose(B[k % 4][:, t * P:t * P + P],
                                             xin[:, t * D + k * P:t * D + k * P + P], ident)
                mm.then_inc(S["xT"], 1)

            x_tile(0)
            pe.wait_ge(ng_in, 32)
            nc.tensor.transpose(B[3][:, 0:KT + 1], norm_rows[0:KT + 1, :], ident[0:KT + 1, 0:KT + 1]).then_inc(S["ng_turned"], 1)
            x_tile(1)
            x_tile(2)
            for k in range(KT):
                if k + 3 < KT:
                    x_tile(k + 3)
                pe.wait_ge(S["ulo"], k + 1)
                run_step(k, k, 1)
            for k in range(KT):
                run_step(KT + k, k, 0)
                if k == 0:
                    for f in range(KT):
                        w = ba[f // 8][:, f % 8]
                        if f % 16 == 0:
                            pe.wait_ge(S["ba_lo"], f // 8 + 2)
                        nc.tensor.matmul(B[0][0:64, 0:SEQ], w, u_hi[:, f, :], start=(f == 0), stop=False)
                        mm = nc.tensor.matmul(B[0][0:64, 0:SEQ], w, u_lo[:, f, :], start=False, stop=(f == KT - 1))
                        if f % 16 == 15:
                            mm.then_inc(S["logits_mm"], 1)
                if k == 11:
                    pe.wait_ge(S["lgT"], 1)
                    for t in range(T):
                        mm = nc.tensor.transpose(B[2][:, t * 64:t * 64 + 64], lgT[0:64, t * P:t * P + P], ident[0:64, 0:64])
                    mm.then_inc(S["logits_turned"], 1)
                if k == 8:
                    pe.wait_ge(small_in, 16 * 3)
                    for i in range(2):
                        mm = nc.tensor.transpose(B[3][:, 96 * i:96 * i + 96], conv_rows[0:96, i * P:i * P + P], ident[0:96, 0:96])
                    mm.then_inc(S["conv_turned"], 1)
            bank_free(3)
            for k in range(KT):
                run_step(2 * KT + k, k, 1)
                if k == 4:
                    pe.wait_ge(S["scalars_v"], 8)
                    pe.wait_ge(consts_in, 16)
                    pe.wait_ge(S["ones_ok"], 1)
                    nc.tensor.matmul(B[0][:, 0:32], tri, g_all, start=True, stop=True)
                    nc.tensor.matmul(B[1][:, 0:32], ones, g_all, start=True, stop=True).then_inc(S["gc_mm"], 1)

            def body(m, mixer):
                for s in range(BODY):
                    g, k = s // KT, s % KT
                    if k == 0:
                        bank_free(4 * m + 4 + g)
                    run_step(m * BODY + 3 * KT + s, k, g % 2)
                    mixer(m, s)

            pe.wait_ge(S["par_v"], 1)
            with pe.Fori(0, QUADS) as m:
                body(m, dn)
            with pe.Fori(QUADS, 2 * QUADS - 1) as m:
                body(m, attn)

            last = 2 * QUADS - 1
            first_out = last * BODY + 4 * KT
            bank_free(4 * last + 4)
            for s in range(2 * KT):
                if s == KT:
                    bank_free(4 * last + 5)
                if s >= KT and s % QH == 0:
                    pe.wait_ge(S["m_lo"], (s - KT) // QH + 1)
                run_step(last * BODY + 3 * KT + s, s % KT, s // KT % 2)
                attn(last, s)

            def out_bank_free(j):
                pe.wait_ge(S["h_add"], 2 * (j - 1))

            bank_free(4 * last + 6)
            for k in range(KT):
                run_step(first_out + KT + k, k, 0)
            def out_group(j, i, tiles):
                out_bank_free(j + i)
                for k in range(tiles):
                    run_step(first_out + (j + i) * KT + k, k, (1 + i) % 2)

            with pe.Fori(2, NG - 2, 2) as j:
                out_group(j, 0, KT)
                out_group(j, 1, KT)
            out_group(NG - 2, 0, KT)
            out_group(NG - 2, 1, KT - LATE)
            for t in range(T):
                for i in range(LATE):
                    k = KT - LATE + i
                    if t == 0:
                        pe.wait_ge(lo_ready, first_out + (NG - 1) * KT + k + 1)
                    mm = products(0, t, k, late_w(u_hi, i), late_w(u_lo, i))
                mm.then_inc(S["rows_done"], 1)

        def split_hi(act, n, k, first=False, late=None):
            to = w_hi[:, k % RING] if late is None else late_w(u_hi, late)
            if k % 2 == 0:
                rounds = (n - k % (2 * RAW)) * (16 // (2 * RAW))
                act.wait_ge(w_in_ring[k // 2 % RAW], rounds + 16)
            if late is not None:
                act.wait_ge(tile_used, n - k + 2 * late + 2)
            elif not first:
                act.wait_ge(tile_used, n - RING + 1)
            nc.scalar.copy(to, w_raw[:, k // 2 % RAW, k % 2]).then_inc(hi_ready, 1)

        def split_lo(dve, n, k, late=None):
            hi, lo = (w_hi[:, k % RING], w_lo[:, k % RING]) if late is None else (late_w(u_hi, late), late_w(u_lo, late))
            dve.wait_ge(hi_ready, n + 1)
            nc.vector.tensor_tensor(lo, w_raw[:, k // 2 % RAW, k % 2], hi.bitcast(F32), ALU.subtract).then_inc(lo_ready, 1)

        @block.scalar
        def _(act):
            def evac_t0(group, dst, bank):
                act.wait_ge(tile_used, KT * group)
                nc.scalar.mul(dst[:, 0:GC], proj[bank][0][:, :], rstd[:, 0:1]).then_inc(evac0, 1)

            def tap3(m, i, dst, banks, hh):
                if hh == 0:
                    act.wait_ge(S["to_feat"], 3 * m + i + 1)
                for h in range(2 * hh, 2 * hh + 2):
                    nc.scalar.mul(dst[:, h * SEQ:h * SEQ + SEQ],
                                  B[banks + h // 2][:, (h % 2) * SEQ:(h % 2) * SEQ + SEQ],
                                  conv_w4[:, (i * QH + h) * TAPS + 3:(i * QH + h) * TAPS + 4]).then_inc(S["tap3"], 1)

            def silu(m, i, f):
                act.wait_ge(S["conv"], 36 * m + 12 * i + 12)
                nc.scalar.activation(f, f, ACT.Silu).then_inc(S["silu"], 1)

            def dn(m, s):
                if s == 1:
                    evac_t0(4 * m + 3, rawv, 1)
                    act.wait_ge(S["qp_ok"], 2 * m + 2)
                if s in (2, 3):
                    tap3(m, 0, f_k, 0, s - 2)
                if s in (5, 6):
                    tap3(m, 1, f_q, 2, s - 5)
                if s == 9:
                    silu(m, 0, f_k)
                if s in (12, 13):
                    if s == 12:
                        act.wait_ge(S["to_tok"], 3 * m + 1)
                    nc.scalar.copy(t_k[:, (s - 12) * GC:(s - 11) * GC], B[s - 12][:, :]).then_inc(S["tok"], 1)
                if s == 15:
                    silu(m, 1, f_q)
                if s in (18, 19):
                    if s == 18:
                        act.wait_ge(S["to_tok"], 3 * m + 2)
                    nc.scalar.copy(t_q[:, (s - 18) * GC:(s - 17) * GC], B[2 + s - 18][:, :]).then_inc(S["tok"], 1)
                if s in (21, 22):
                    if s == 21:
                        act.wait_ge(S["kq_feat"], 2 * m + 1)
                    nc.scalar.copy(f_k[:, (s - 21) * GC:(s - 20) * GC], B[s - 21][:, :]).then_inc(S["kq_ev"], 1)
                if s in (24, 25):
                    tap3(m, 2, f_v, 0, s - 24)
                if s in (27, 28):
                    if s == 27:
                        act.wait_ge(S["kq_feat"], 2 * m + 2)
                    nc.scalar.copy(f_q[:, (s - 27) * GC:(s - 26) * GC], B[2 + s - 27][:, :]).then_inc(S["kq_ev"], 1)
                if s == 32:
                    silu(m, 2, f_v)
                if s == 33:
                    evac_t0(4 * m + 4, gate, 0)
                if s == 36:
                    act.wait_ge(evac0, 4 * m + 4)
                    act.wait_ge(evac1, 4 * m + 4)
                    nc.scalar.activation(gate, gate, ACT.Silu).then_inc(S["silu_g"], 1)
                if s == 38:
                    act.wait_ge(S["gmask_ok"], 2 * m + 2)
                    nc.scalar.activation(decay, decay, ACT.Exp).then_inc(S["gexp"], 1)
                for c in range(T):
                    e = s - 47 - c
                    if 6 * SMALL <= e < 6 * LEVELS and e % 6 == 0:
                        act.wait_ge(S["x_turned"], 2 * (LEVELS - SMALL) * m + 2 * (e // 6 - SMALL) + c + 1)
                        nc.scalar.copy(XT[:, c * GC:c * GC + GC], B[c][:, :]).then_inc(S["xt_a"], 1)
                if s == 65:
                    evac_t0(4 * m + 5, rawk, 1)
                if s == 86:
                    act.wait_ge(S["y0_mm"], m + 1)
                    nc.scalar.copy(ysol[:, 0:GC], B[0][:, :]).then_inc(S["y0_ok"], 1)
                if s == 88:
                    act.wait_ge(S["o0_mm"], 2 * m + 2)
                    nc.scalar.copy(state, B[0][:, :]).then_inc(S["s_ok"], 1)
                if s == 89:
                    nc.scalar.copy(o_dn[:, 0:GC], B[2][:, :]).then_inc(S["o0_ok"], 1)
                if s == 95:
                    act.wait_ge(S["y1_mm"], m + 1)
                    nc.scalar.copy(ysol[:, GC:2 * GC], B[1][:, :]).then_inc(S["y1_ok"], 1)
                if s == 97:
                    evac_t0(4 * m + 6, rawq, 0)
                if s in (110, 111):
                    b = s - 110
                    if b == 0:
                        act.wait_ge(S["out_feat"], m + 1)
                    nc.scalar.mul(mixedT[:, bass.ds(m * QH + 2 * b, 2), :],
                                  B[b][:, :].rearrange("p (h n) -> p h n", h=2), ngT[:, KT:KT + 1]).then_inc(S["mix_ok"], 1)

            def attn(m, s):
                a = m - QUADS
                if s == 1:
                    evac_t0(4 * m + 3, rawv, 1)
                if s in (2, 3):
                    if s == 2:
                        act.wait_ge(S["akq_feat"], 2 * a + 1)
                    nc.scalar.copy(f_k[:, (s - 2) * GC:(s - 1) * GC], B[s - 2][:, :]).then_inc(S["akq_ok"], 1)
                if s in (4, 5):
                    if s == 4:
                        act.wait_ge(S["akq_feat"], 2 * a + 2)
                    nc.scalar.copy(f_q[:, (s - 4) * GC:(s - 3) * GC], B[2 + s - 4][:, :]).then_inc(S["akq_ok"], 1)
                if s in (15, 16, 17, 18):
                    h = s - 15
                    if h == 0:
                        act.wait_ge(S["amax"], 2 * a + 2)
                    for t, (lo, n) in enumerate(((0, P), (P, SEQ))):
                        pr = prob[:, h * 384 + lo:h * 384 + lo + n]
                        nc.scalar.activation(pr, pr, ACT.Exp, bias=negmax[:, t * QH + h:t * QH + h + 1],
                                             accum_out=esum[:, t * QH + h:t * QH + h + 1]).then_inc(S["aexp"], 1)
                if s in (21, 22, 23):
                    b = s - 21
                    act.wait_ge(S["prob_turned"], 3 * a + b + 1)
                    nc.scalar.copy(pT[:, b * GC:b * GC + GC], B[b][:, :]).then_inc(S["pT_ok"], 1)
                if s == 33:
                    evac_t0(4 * m + 4, gate, 0)
                if s == 35:
                    act.wait_ge(evac0, 4 * m + 4)
                    act.wait_ge(evac1, 4 * m + 4)
                    nc.scalar.activation(gate, gate, ACT.Silu).then_inc(S["a_silu"], 1)
                if s in (41, 42):
                    b = s - 41
                    if b == 0:
                        act.wait_ge(S["aout_feat"], a + 1)
                    nc.scalar.copy(mixedT[:, bass.ds(m * QH + 2 * b, 2), :],
                                   B[1 + b][:, :].rearrange("p (h n) -> p h n", h=2)).then_inc(S["amix_ok"], 1)
                if s == 65:
                    evac_t0(4 * m + 5, rawk, 1)
                if s == 97:
                    evac_t0(4 * m + 6, rawq, 0)

            act.dma_start(norm_rows[0:KT, :], norm_g.rearrange("a (k p) -> (a k) p", p=P)).then_inc(ng_in, 16)
            act.dma_start(norm_rows[KT:KT + 1, :], dn_norm_g).then_inc(ng_in, 16)
            act.wait_ge(S["half_ok"], 1)
            nc.scalar.mul(ones, half[:, 0:1].to_broadcast([P, P]), -2.0).then_inc(S["ones_ok"], 1)

            def x_hi(k):
                act.wait_ge(S["xT"], k + 1)
                nc.scalar.mul(u_hi[:, k], B[k % 4][:, 0:SEQ], ngT[:, k:k + 1]).then_inc(S["uhi"], 1)

            act.wait_ge(S["ngT_ok"], 1)
            x_hi(0)
            split_hi(act, 0, 0, first=True)
            split_hi(act, 1, 1, first=True)
            split_hi(act, 2, 2, first=True)
            for k in range(KT):
                if k + 1 < KT:
                    x_hi(k + 1)
                if k == KT - 1:
                    act.wait_ge(wba_in, 16)
                    for b in range(4):
                        act.wait_ge(tile_used, KT - 1 + b // 2)
                        nc.scalar.copy(ba[b][:, :, 0:32], wba_r[:, b]).then_inc(S["ba_hi"], 1)
                    act.wait_ge(S["logits_mm"], 1)
                split_hi(act, k + AHEAD, (k + AHEAD) % KT, first=(k < 1))
            for part in x_in:
                act.wait_ge(part, 16)
            act.wait_ge(S["logits_mm"], 2)
            for k in range(KT):
                split_hi(act, KT + k + AHEAD, (k + AHEAD) % KT)
                if k == 1:
                    nc.scalar.copy(lgT[0:64, :], B[0][0:64, 0:SEQ]).then_inc(S["lgT"], 1)
                if k < 16:
                    if k >= 2:
                        act.wait_ge(S["xsq"], k - 1)
                    nc.scalar.activation(scrap[:, (k % 2) * GC:(k % 2) * GC + GC], xin[:, GC * k:GC * k + GC], ACT.Square,
                                         accum_out=ssx[:, k:k + 1]).then_inc(S["xsq"], 1)
                if k == 20:
                    act.wait_ge(S["rstd_ok"], 1)
                    evac_t0(1, rawk, 1)
                if k == 23:
                    act.wait_ge(small_in, 16 * 3)
                    act.wait_ge(S["scalars_v"], 5)
                    nc.scalar.activation(scal64[:, 0:32], logits.rearrange("p (t n) -> p t n", t=T)[:, :, 0:HEADS], ACT.Exp,
                                         scale=-1.0).then_inc(S["scalars_a"], 1)
                    nc.scalar.activation(soft, soft, ACT.Exp).then_inc(S["scalars_a"], 1)
                if k == 24:
                    nc.scalar.activation(exp_a, exp_a, ACT.Exp).then_inc(S["scalars_a"], 1)
                    act.wait_ge(S["scalars_a"], 2)
                    nc.scalar.activation(soft, soft, ACT.Ln, bias=1.0).then_inc(S["scalars_a"], 1)
            for k in range(KT):
                split_hi(act, 2 * KT + k + AHEAD, (k + AHEAD) % KT)
                if k == 1:
                    evac_t0(2, rawq, 0)
                if k == 8:
                    act.wait_ge(S["scalars_v"], 11)
                    nc.scalar.activation(quad_all[:, :, 24:28], quad_all[:, :, 12:16], ACT.Exp).then_inc(S["par_a"], 1)
                    nc.scalar.activation(quad_all[:, :, 28:32], scal64[:, 32:48].rearrange("p (q h) -> p q h", h=QH),
                                         ACT.Exp).then_inc(S["par_a"], 1)

            def body(m, mixer):
                for s in range(BODY):
                    split_hi(act, m * BODY + 3 * KT + s + AHEAD, (s + AHEAD) % KT)
                    mixer(m, s)

            with act.Fori(0, QUADS) as m:
                body(m, dn)
            with act.Fori(QUADS, 2 * QUADS - 1) as m:
                body(m, attn)

            last = 2 * QUADS - 1
            first_out = last * BODY + 4 * KT

            def m_hi(b):
                if b == 0:
                    act.wait_ge(S["mix_ok"], 2 * QUADS)
                    act.wait_ge(S["amix_ok"], 2 * QUADS - 2)
                if b == 2 * QUADS - 1:
                    act.wait_ge(S["amix_ok"], 2 * QUADS)
                act.wait_ge(tile_used, KT * (4 * last + 3) + QH * b + QH)
                tiles = slice(QH * b, QH * b + QH)
                nc.scalar.copy(u_hi[:, tiles], mixedT[:, tiles]).then_inc(S["m_hi"], 1)

            for s in range(2 * KT):
                split_hi(act, last * BODY + 3 * KT + s + AHEAD, (s + AHEAD) % KT)
                attn(last, s)
                if s in M_STEP:
                    m_hi(M_STEP.index(s))

            def h_square(j, g, rows=range(T)):
                for t in rows:
                    act.wait_ge(S["h_add"], 2 * g + t + 1)
                    nc.scalar.activation(w_sq, hbuf[:, bass.ds(j * GC + t * D, GC)], ACT.Square,
                                         accum_out=hsum[:, t, bass.ds(j, 1)]).then_inc(S["h_sq"], 1)
                    act.wait_ge(S["h_sq"], 2 * g + t + 1)

            w_sq = region(12288, GC)
            for k in range(KT):
                split_hi(act, first_out + KT + k + AHEAD, (k + AHEAD) % KT)
                if k == 16:
                    h_square(0, 0)
            with act.Fori(2, NG - 1) as j:
                for k in range(KT):
                    split_hi(act, first_out + j * KT + k + AHEAD, (k + AHEAD) % KT)
                    if k == 16:
                        h_square(j - 1, j - 1)
            for k in range(KT):
                if k + AHEAD < KT:
                    split_hi(act, first_out + (NG - 1) * KT + k + AHEAD, k + AHEAD,
                             late=None if k + AHEAD < KT - LATE else k + AHEAD - KT + LATE)
                if k == 16:
                    h_square(NG - 2, NG - 2)
            act.wait_ge(S["h_g"], 2 * (NG - 1))
            for t in range(T):
                h_square(NG - 1, NG - 1, (t,))
                act.wait_ge(S["h_rstd"], t + 1)
                for j in range(2):
                    part = hbuf[:, t * D + 1024 * j:t * D + 1024 * j + 1024]
                    nc.scalar.mul(part, part, rstd[:, t:t + 1]).then_inc(S["h_fin_a"], 1)

        @block.vector
        def _(dve):
            def evac_t1(group, dst, bank):
                dve.wait_ge(tile_used, KT * group)
                nc.vector.tensor_scalar(dst[:, GC:2 * GC], proj[bank][1][:, :], rstd[:, 1:2], None,
                                        ALU.mult).then_inc(evac1, 1)

            def over_h(ap, n=P):
                return ap.unsqueeze(2).to_broadcast([P, ap.shape[1], n])

            def each_h(ap, blocks=QH):
                return ap.unsqueeze(1).to_broadcast([P, blocks, ap.shape[1]])

            def taps(m, i, f, banks, part):
                for n in (2 * part, 2 * part + 1):
                    shift, h = n // QH + 1, n % QH
                    if n < QH:
                        dve.wait_ge(S["tap3"], 12 * m + QH * i + h + 1)
                    else:
                        dve.wait_ge(S["conv"], 36 * m + 12 * i + n - 3)
                    to = f[:, h * SEQ + shift:h * SEQ + SEQ]
                    at = (h % 2) * SEQ
                    w = (i * QH + h) * TAPS + 3 - shift
                    nc.vector.scalar_tensor_tensor(out=to, in0=B[banks + h // 2][:, at:at + SEQ - shift],
                                                   scalar=conv_w4[:, w:w + 1], in1=to,
                                                   op0=ALU.mult, op1=ALU.add).then_inc(S["conv"], 1)

            def dn(m, s):
                if s == 0:
                    nc.vector.tensor_copy(quad[:, :], quad_all[:, bass.ds(m, 1), :].rearrange("p q n -> p (q n)")).then_inc(S["qp_ok"], 1)
                    nc.vector.tensor_copy(conv_w4[:, :], conv_all[:, bass.ds(m, 1), :].rearrange("p q n -> p (q n)")).then_inc(S["qp_ok"], 1)
                if s == 1:
                    evac_t1(4 * m + 3, rawv, 1)
                    dve.wait_ge(S["qp_ok"], 2 * m + 2)
                if 3 <= s < 9:
                    taps(m, 0, f_k, 0, s - 3)
                if 9 <= s < 15:
                    taps(m, 1, f_q, 2, s - 9)
                if 26 <= s < 32:
                    taps(m, 2, f_v, 0, s - 26)
                for i, at in ((0, 15), (1, 22)):
                    if s == at:
                        dve.wait_ge(S["sqr"], 2 * m + i + 1)
                        nc.vector.tensor_reduce(stat[:, 8 * i:8 * i + 8], by_h(sq), AX.X, ALU.add).then_inc(S["sumsq_ok"], 1)
                for i, at, tk in ((0, 18, t_k), (1, 25, t_q)):
                    if s == at:
                        dve.wait_ge(S["fac_ok"], 2 * m + i + 1)
                        nc.vector.tensor_tensor(by_h(tk), by_h(tk), over_h(fac[:, 8 * i:8 * i + 8]), ALU.mult).then_inc(S["scaled"], 1)
                if s in (30, 32):
                    c = (s - 30) // 2
                    if c == 0:
                        dve.wait_ge(S["gcrow"], m + 1)
                    nc.vector.tensor_tensor(by_h(decay[:, c * GC:c * GC + GC]), by_h(B[2 + c][:, :]),
                                            over_h(quad[:, 8 + QH * c:8 + QH * c + QH]), ALU.subtract).then_inc(S["gsub"], 1)
                if s == 33:
                    evac_t1(4 * m + 4, gate, 0)
                if s in (35, 36):
                    t = s - 35
                    if t == 0:
                        dve.wait_ge(S["to_tok"], 3 * m + 3)
                    nc.vector.tensor_tensor(by_h(t_v[:, t * GC:t * GC + GC]), by_h(B[t][:, :]),
                                            over_h(quad[:, 16 + QH * t:16 + QH * t + QH]), ALU.mult).then_inc(S["v_ok"], 1)
                if s in (39, 40):
                    c = s - 39
                    if c == 0:
                        dve.wait_ge(S["gexp"], m + 1)
                    dve.wait_ge(S["kk_mm"], 2 * m + c + 1)
                    cc = slice(c * GC, c * GC + GC)
                    nc.vector.tensor_tensor(AT[:, cc], B[c][:, :], decay[:, cc], ALU.mult).then_inc(S["at_ok"], 1)
                if s in (41, 42):
                    c = s - 41
                    dve.wait_ge(S["qk_mm"], 2 * m + c + 1)
                    cc = slice(c * GC, c * GC + GC)
                    nc.vector.tensor_tensor(decay[:, cc], B[2 + c][:, :], decay[:, cc], ALU.mult).then_inc(S["qkt_ok"], 1)
                for c in range(T):
                    yb = by_h(Yb[:, c * 256:c * 256 + 256], 64)
                    xx = by_h(XX[:, c * GC:c * GC + GC])
                    e = s - 43 - c
                    if e == 0:
                        dve.wait_ge(S["at_ok"], 2 * m + c + 1)
                        nc.vector.transpose(XT[:, c * GC:c * GC + GC], AT[:, c * GC:c * GC + GC]).then_inc(S["a_turned"], 1)
                    lv = e // 6
                    if 0 <= lv < LEVELS and e == (1 if lv == 0 else 6 * lv):
                        mask = each_h(tables[:, C_YM + 64 * lv:C_YM + 64 * lv + 64])
                        if lv == 0:
                            dve.wait_ge(S["a_turned"], 2 * m + c + 1)
                            nc.vector.tensor_tensor(yb, by_h(XT[:, c * GC:c * GC + GC])[:, :, 0:P:2], mask, ALU.mult).then_inc(S["y_ok"], 1)
                        else:
                            dve.wait_ge(S["ax_mm"], 2 * (LEVELS - 1) * m + 2 * (lv - 1) + c + 1)
                            nc.vector.tensor_tensor(yb, by_h(B[c][:, 0:256], 64), mask, ALU.mult).then_inc(S["y_ok"], 1)
                    if 0 <= lv < LEVELS and e == 6 * lv + 2:
                        xc = pair(1 << lv)(xx, 0)
                        if lv == 0:
                            dve.wait_ge(S["y_ok"], 2 * LEVELS * m + c + 1)
                            dve.wait_ge(S["x_id"], m + 1)
                            z = yb
                        else:
                            dve.wait_ge(S["xax_mm"], 2 * (LEVELS - 1) * m + 2 * (lv - 1) + c + 1)
                            z = by_h(B[2 + c][:, 0:256], 64)
                        z = z.rearrange("p h (b s) -> p h b s", s=1 << lv)
                        nc.vector.tensor_tensor(xc, xc, z, ALU.subtract).then_inc(S["x_ok"], 1)
                    if 0 <= lv < SMALL and e == 6 * lv + 3:
                        dve.wait_ge(S["x_ok"], 2 * LEVELS * m + 2 * lv + c + 1)
                        nc.vector.transpose(XT[:, c * GC:c * GC + GC], XX[:, c * GC:c * GC + GC]).then_inc(S["xt_v"], 1)
                if s == 65:
                    evac_t1(4 * m + 5, rawk, 1)
                if s == 91:
                    dve.wait_ge(S["state_mm"], 2 * m + 2)
                    nc.vector.tensor_tensor(by_h(resid), by_h(B[1][:, :]), over_h(quad[:, 24:28]), ALU.mult).then_inc(S["r_mul"], 1)
                if s == 92:
                    dve.wait_ge(S["r_mul"], m + 1)
                    nc.vector.tensor_tensor(resid, t_v[:, GC:2 * GC], resid, ALU.subtract).then_inc(S["r_ok"], 1)
                if s == 93:
                    nc.vector.tensor_tensor(by_h(qS), by_h(B[3][:, :]), over_h(quad[:, 24:28]), ALU.mult).then_inc(S["qs_ok"], 1)
                if s == 97:
                    evac_t1(4 * m + 6, rawq, 0)
                if s == 98:
                    dve.wait_ge(S["o1_mm"], m + 1)
                    dve.wait_ge(S["qs_ok"], m + 1)
                    nc.vector.tensor_tensor(o_dn[:, GC:2 * GC], B[3][:, :], qS, ALU.add).then_inc(S["o_ok"], 1)
                if s == 102:
                    dve.wait_ge(S["osq"], m + 1)
                    nc.vector.tensor_reduce(stat[:, 0:8], by_h(sq), AX.X, ALU.add).then_inc(S["ored"], 1)
                if s == 107:
                    dve.wait_ge(S["ofac"], m + 1)
                    dve.wait_ge(S["gated"], m + 1)
                    nc.vector.tensor_tensor(by_h(gate), by_h(gate), over_h(fac[:, 0:8]), ALU.mult).then_inc(S["onorm"], 1)

            def attn(m, s):
                a = m - QUADS
                if s == 1:
                    evac_t1(4 * m + 3, rawv, 1)
                if 8 <= s < 12:
                    h = s - 8
                    if h == 0:
                        dve.wait_ge(S["bias_ok"], QH * a + QH)
                    dve.wait_ge(S["scores_mm"], QH * a + h + 1)
                    cc = slice(h * 384, h * 384 + 384)
                    nc.vector.scalar_tensor_tensor(out=prob[:, cc], in0=B[h][:, 0:384], scalar=float(P) ** -0.5,
                                                   in1=bias[:, cc], op0=ALU.mult, op1=ALU.add).then_inc(S["logit"], 1)
                if s in (12, 13):
                    t = s - 12
                    if t == 0:
                        dve.wait_ge(S["logit"], QH * a + QH)
                    lo, n = ((0, P), (P, SEQ))[t]
                    nc.vector.tensor_reduce(negmax[:, t * QH:t * QH + QH], by_h(prob, 384)[:, :, lo:lo + n], AX.X, ALU.max,
                                            negate=True).then_inc(S["amax"], 1)
                if s == 20:
                    dve.wait_ge(S["aexp"], 8 * a + 8)
                    nc.vector.reciprocal(rinv[:, :], esum[:, :]).then_inc(S["arin"], 1)
                if s in (27, 28):
                    t = s - 27
                    dve.wait_ge(S["arin"], a + 1)
                    dve.wait_ge(S["pv_mm"], 2 * a + t + 1)
                    nc.vector.tensor_tensor(by_h(o_at[:, t * GC:t * GC + GC]), by_h(B[3 - 3 * t][:, :]),
                                            over_h(rinv[:, t * QH:t * QH + QH]), ALU.mult).then_inc(S["ao_ok"], 1)
                if s == 33:
                    evac_t1(4 * m + 4, gate, 0)
                if s == 37:
                    dve.wait_ge(S["a_silu"], a + 1)
                    dve.wait_ge(S["ao_ok"], 2 * a + 2)
                    nc.vector.tensor_tensor(gate, gate, o_at, ALU.mult).then_inc(S["agated"], 1)
                if s == 65:
                    evac_t1(4 * m + 5, rawk, 1)
                if s == 97:
                    evac_t1(4 * m + 6, rawq, 0)

            nc.vector.memset(half[:, :], -0.5).then_inc(S["half_ok"], 1)
            dve.wait_ge(S["ng_turned"], 1)
            nc.vector.tensor_copy(ngT[:, :], B[3][:, 0:KT + 1]).then_inc(S["ngT_ok"], 1)
            dve.wait_ge(S["ngT_ok"], 1)

            def x_lo(k):
                dve.wait_ge(S["uhi"], k + 1)
                nc.vector.scalar_tensor_tensor(out=u_lo[:, k], in0=B[k % 4][:, 0:SEQ], scalar=ngT[:, k:k + 1],
                                               in1=u_hi[:, k].bitcast(F32), op0=ALU.mult,
                                               op1=ALU.subtract).then_inc(S["ulo"], 1)

            x_lo(0)
            split_lo(dve, 0, 0)
            split_lo(dve, 1, 1)
            split_lo(dve, 2, 2)
            for k in range(KT):
                if k + 1 < KT:
                    x_lo(k + 1)
                if k == KT - 1:
                    for b in range(4):
                        dve.wait_ge(S["ba_hi"], b + 1)
                        nc.vector.tensor_tensor(ba[b][:, :, 32:64], wba_r[:, b],
                                                ba[b][:, :, 0:32].bitcast(F32), ALU.subtract).then_inc(S["ba_lo"], 1)
                split_lo(dve, k + AHEAD, (k + AHEAD) % KT)
            dve.wait_ge(small_in, 16 * 3)
            lgt = logits.rearrange("p (t n) -> p t n", t=T)
            s2 = lambda r: r.rearrange("p (t n) -> p t n", t=T)
            by_quad = lambda r: r.rearrange("p (t q h) -> p q t h", t=T, h=QH)
            for k in range(KT):
                split_lo(dve, KT + k + AHEAD, (k + AHEAD) % KT)
                if k == 17:
                    dve.wait_ge(S["xsq"], 16)
                    nc.vector.tensor_reduce(stat[:, 0:2], ssx.rearrange("p (t n) -> p t n", t=T), AX.X, ALU.add).then_inc(S["xmean_ok"], 1)
                    dve.wait_ge(S["xmean_ok"], 1)
                    nc.vector.tensor_scalar(stat[:, 2:4], stat[:, 0:2], 1.0 / D, EPS, ALU.mult, ALU.add).then_inc(S["xmean_ok"], 1)
                if k == 20:
                    dve.wait_ge(S["rstd_ok"], 1)
                    evac_t1(1, rawk, 1)
                if k == 21:
                    dve.wait_ge(S["logits_turned"], 1)
                    for t in range(T):
                        nc.vector.tensor_scalar(lgt[:, t], B[2][:, t * 64:t * 64 + 32], rstd[:, t:t + 1], None, ALU.mult).then_inc(S["logits_hi"], 1)
                    dve.wait_ge(S["logits_hi"], 2)
                    for t in range(T):
                        nc.vector.scalar_tensor_tensor(out=lgt[:, t], in0=B[2][:, t * 64 + 32:t * 64 + 64], scalar=rstd[:, t:t + 1],
                                                       in1=lgt[:, t], op0=ALU.mult, op1=ALU.add).then_inc(S["scalars_v"], 1)
                    dve.wait_ge(S["scalars_v"], 2)
                    nc.vector.tensor_tensor(s2(beta_a), lgt[:, :, HEADS:2 * HEADS], each_h(dt_all, T), ALU.add).then_inc(S["scalars_v"], 1)
                    dve.wait_ge(S["scalars_v"], 3)
                    nc.vector.tensor_scalar(scal64[:, 32:64], beta_a, -1.0, None, ALU.mult).then_inc(S["scalars_v"], 1)
                    dve.wait_ge(S["scalars_v"], 4)
                    nc.vector.tensor_tensor(soft, beta_a, scal64[:, 32:64], ALU.min).then_inc(S["scalars_v"], 1)
                if k == 26:
                    dve.wait_ge(S["scalars_a"], 4)
                    nc.vector.tensor_scalar(scal64[:, 0:32], scal64[:, 0:32], 1.0, None, ALU.add).then_inc(S["scalars_v"], 1)
                    nc.vector.scalar_tensor_tensor(out=g_all, in0=beta_a, scalar=0.0, in1=soft, op0=ALU.max, op1=ALU.add).then_inc(S["scalars_v"], 1)
                    dve.wait_ge(S["scalars_v"], 7)
                    nc.vector.scalar_tensor_tensor(out=s2(g_all), in0=s2(g_all), scalar=-1.0, in1=each_h(exp_a, T), op0=ALU.mult,
                                                   op1=ALU.mult).then_inc(S["scalars_v"], 1)
                if k == 12:
                    dve.wait_ge(S["conv_turned"], 1)
                    for i in range(2):
                        for j, of in enumerate((1, 0, 2)):
                            to = conv_all[:, :, 16 * j:16 * j + 16].rearrange("p q (h c) -> p c q h", c=TAPS)[:, 2 * i:2 * i + 2]
                            fr = B[3][:, 96 * i:96 * i + 96].rearrange("p (c x q h) -> p x c q h", x=3, q=QUADS, h=QH)[:, of]
                            for c in range(2):
                                nc.vector.tensor_copy(to[:, c], fr[:, c]).then_inc(S["cv_ok"], 1)
            for k in range(KT):
                split_lo(dve, 2 * KT + k + AHEAD, (k + AHEAD) % KT)
                if k == 1:
                    evac_t1(2, rawq, 0)
                if k == 6:
                    dve.wait_ge(S["scalars_v"], 8)
                    nc.vector.tensor_copy(quad_all[:, :, 0:8].rearrange("p q (t h) -> p q t h", t=T), by_quad(g_all)).then_inc(S["scalars_v"], 1)
                    dve.wait_ge(S["gc_mm"], 1)
                    nc.vector.tensor_copy(quad_all[:, :, 8:16].rearrange("p q (t h) -> p q t h", t=T), by_quad(B[0][:, 0:32])).then_inc(S["scalars_v"], 1)
                    dve.wait_ge(S["scalars_v"], 10)
                    nc.vector.tensor_tensor(scal64[:, 32:48].rearrange("p (q h) -> p q h", h=QH),
                                            B[1][:, 0:16].rearrange("p (q h) -> p q h", h=QH),
                                            quad_all[:, :, 8:12], ALU.subtract).then_inc(S["scalars_v"], 1)
                    dve.wait_ge(S["beta_ok"], 1)
                    nc.vector.tensor_copy(quad_all[:, :, 16:24].rearrange("p q (t h) -> p q t h", t=T), by_quad(beta_a)).then_inc(S["par_v"], 1)
            dve.wait_ge(S["par_a"], 2)
            dve.wait_ge(S["par_v"], 1)
            dve.wait_ge(S["cv_ok"], 12)

            def body(m, mixer):
                for s in range(BODY):
                    split_lo(dve, m * BODY + 3 * KT + s + AHEAD, (s + AHEAD) % KT)
                    mixer(m, s)

            with dve.Fori(0, QUADS) as m:
                body(m, dn)
            with dve.Fori(QUADS, 2 * QUADS - 1) as m:
                body(m, attn)

            last = 2 * QUADS - 1
            first_out = last * BODY + 4 * KT

            def m_lo(b):
                dve.wait_ge(S["m_hi"], b + 1)
                tiles = slice(QH * b, QH * b + QH)
                nc.vector.tensor_tensor(u_lo[:, tiles], mixedT[:, tiles],
                                        u_hi[:, tiles].bitcast(F32), ALU.subtract).then_inc(S["m_lo"], 1)

            for s in range(2 * KT):
                split_lo(dve, last * BODY + 3 * KT + s + AHEAD, (s + AHEAD) % KT)
                attn(last, s)
                if s in M_STEP:
                    m_lo(M_STEP.index(s))

            def h_add(j, g, bank, rows=range(T)):
                if rows == range(T):
                    dve.wait_ge(tile_used, KT * (g + 4 * last + 5))
                dve.wait_ge(S["h_in"], 16 * g + 16)
                for t in rows:
                    part = hbuf[:, bass.ds(j * GC + t * D, GC)]
                    nc.vector.tensor_tensor(part, proj[bank][t][:, :], part, ALU.add).then_inc(S["h_add"], 1)

            for k in range(KT):
                split_lo(dve, first_out + KT + k + AHEAD, (k + AHEAD) % KT)
                if k == 12:
                    h_add(0, 0, 1)

            def out_pair(j, final):
                for i in range(2):
                    for k in range(KT):
                        if not (final and i == 1 and k + AHEAD >= KT):
                            late = k + AHEAD - KT + LATE if final and i == 1 and k + AHEAD >= KT - LATE else None
                            split_lo(dve, first_out + (j + i) * KT + k + AHEAD, (k + AHEAD) % KT, late=late)
                        if k == 12:
                            h_add(j + i - 1, j + i - 1, i)

            with dve.Fori(2, NG - 2, 2) as j:
                out_pair(j, False)
            out_pair(NG - 2, True)
            dve.wait_ge(S["h_g"], 2 * (NG - 1))
            dve.wait_ge(S["gf_in"], 16 * NG)
            for t in range(T):
                dve.wait_ge(S["rows_done"], t + 1)
                h_add(NG - 1, NG - 1, 0, (t,))
                dve.wait_ge(S["h_sq"], 2 * NG - 1 + t)
                nc.vector.tensor_reduce(stat[:, t:t + 1], hsum[:, t, :], AX.X, ALU.add).then_inc(S["h_red"], 1)
                dve.wait_ge(S["h_red"], t + 1)
                nc.vector.tensor_scalar(stat[:, 2 + t:3 + t], stat[:, t:t + 1], 1.0 / D, EPS, ALU.mult, ALU.add).then_inc(S["h_mean"], 1)
                part = hbuf[:, t * D + D - GC:t * D + D]
                nc.vector.tensor_tensor(part, part, gfin[:, D - GC:D], ALU.mult).then_inc(S["h_g_last"], 1)
                dve.wait_ge(S["h_rstd"], t + 1)
                dve.wait_ge(S["h_g_last"], t + 1)
                for j in range(2, 4):
                    part = hbuf[:, t * D + 1024 * j:t * D + 1024 * j + 1024]
                    nc.vector.tensor_scalar(part, part, rstd[:, t:t + 1], None, ALU.mult).then_inc(S["h_fin_v"], 1)

        @block.gpsimd
        def _(pool):
            def over_h(ap, n=P):
                return ap.unsqueeze(2).to_broadcast([P, ap.shape[1], n])

            def each_h(ap, blocks=QH):
                return ap.unsqueeze(1).to_broadcast([P, blocks, ap.shape[1]])

            def square(src, done):
                nc.gpsimd.tensor_tensor(sq, src, src, ALU.mult).then_inc(done, 1)

            def dn(m):
                for i, tk in ((0, t_k), (1, t_q)):
                    pool.wait_ge(S["tok"], 4 * m + 2 * i + 2)
                    if i == 1:
                        pool.wait_ge(S["sumsq_ok"], 2 * m + 1)
                    square(tk, S["sqr"])
                    pool.wait_ge(S["sumsq_ok"], 2 * m + i + 1)
                    pool.sem_inc(S["pool_waits"])
                    st, fa = stat[:, 8 * i:8 * i + 8], fac[:, 8 * i:8 * i + 8]
                    mul = 1.0 if i == 0 else float(P)
                    nc.gpsimd.tensor_scalar(st, st, mul, mul * EPS, ALU.mult, ALU.add).then_inc(S["pow_in"], 1)
                    pool.wait_ge(S["pow_in"], 3 * m + i + 1)
                    if i == 0:
                        nc.gpsimd.tensor_tensor(fa, st, half[:, 0:8], ALU.pow).then_inc(S["pow_k"], 1)
                        pool.wait_ge(S["pow_k"], m + 1)
                        nc.gpsimd.tensor_tensor(fa, fa, quad[:, 16:24], ALU.mult).then_inc(S["fac_ok"], 1)
                    else:
                        nc.gpsimd.tensor_tensor(fa, st, half[:, 0:8], ALU.pow).then_inc(S["fac_ok"], 1)
                pool.wait_ge(S["scaled"], 2 * m + 1)
                nc.gpsimd.tensor_tensor(by_h(ktail), by_h(t_k[:, 0:GC]), over_h(quad[:, 28:32]), ALU.mult).then_inc(S["ktail_ok"], 1)
                for c in range(T):
                    dc = by_h(decay[:, c * GC:c * GC + GC])
                    pool.wait_ge(S["gsub"], 2 * m + c + 1)
                    nc.gpsimd.tensor_tensor(dc, dc, each_h(causal), ALU.add).then_inc(S["gmask_ok"], 1)
                nc.gpsimd.tensor_copy(by_h(XX), each_h(ident, 2 * QH)).then_inc(S["x_id"], 1)
                pool.wait_ge(S["o0_ok"], m + 1)
                pool.wait_ge(S["o_ok"], m + 1)
                square(o_dn, S["osq"])
                pool.wait_ge(S["silu_g"], m + 1)
                nc.gpsimd.tensor_tensor(gate, gate, o_dn, ALU.mult).then_inc(S["gated"], 1)
                pool.wait_ge(S["ored"], m + 1)
                pool.sem_inc(S["pool_waits"])
                nc.gpsimd.tensor_scalar(stat[:, 0:8], stat[:, 0:8], 1.0 / P, EPS, ALU.mult, ALU.add).then_inc(S["pow_in"], 1)
                pool.wait_ge(S["pow_in"], 3 * m + 3)
                nc.gpsimd.tensor_tensor(fac[:, 0:8], stat[:, 0:8], half[:, 0:8], ALU.pow).then_inc(S["ofac"], 1)

            def attn(m):
                a = m - QUADS
                pool.wait_ge(S["akq_feat"], 2 * a + 1)
                nc.gpsimd.tensor_copy(slope4[:, :], tables[:, bass.ds(C_SLOPE + a * QH, QH)]).then_inc(S["sl_ok"], 1)
                pool.wait_ge(S["sl_ok"], a + 1)
                pool.sem_inc(S["pool_waits"])
                for h in range(QH):
                    nc.gpsimd.tensor_scalar(bias[:, h * 384:h * 384 + 384], tables[:, C_DIST:C_DIST + 384], slope4[:, h:h + 1],
                                            None, ALU.mult).then_inc(S["bias1"], 1)
                for h in range(QH):
                    bh = bias[:, h * 384:h * 384 + 384]
                    pool.wait_ge(S["bias1"], QH * a + h + 1)
                    nc.gpsimd.tensor_tensor(bh, bh, tables[:, C_LOGN:C_LOGN + 384], ALU.add).then_inc(S["bias_ok"], 1)

            pool.wait_ge(S["xmean_ok"], 2)
            pool.wait_ge(S["half_ok"], 1)
            nc.gpsimd.tensor_tensor(rstd[:, :], stat[:, 2:4], half[:, 0:2], ALU.pow).then_inc(S["rstd_ok"], 1)
            pool.wait_ge(S["scalars_v"], 8)
            nc.gpsimd.tensor_tensor(beta_a, scal64[:, 0:32], half[:, :], ALU.pow).then_inc(S["beta_ok"], 1)

            with pool.Fori(0, QUADS) as m:
                dn(m)
            with pool.Fori(QUADS, 2 * QUADS) as m:
                attn(m)

            with pool.Fori(0, NG - 1) as j:
                pool.wait_ge(S["gf_in"], 16 * j + 16)
                for t in range(T):
                    pool.wait_ge(S["h_sq"], 2 * j + t + 1)
                    part = hbuf[:, bass.ds(j * GC + t * D, GC)]
                    nc.gpsimd.tensor_tensor(part, part, gfin[:, bass.ds(j * GC, GC)], ALU.mult).then_inc(S["h_g"], 1)
            for t in range(T):
                pool.wait_ge(S["h_mean"], t + 1)
                nc.gpsimd.tensor_tensor(rstd[:, t:t + 1], stat[:, 2 + t:3 + t], half[:, 0:1], ALU.pow).then_inc(S["h_rstd"], 1)


_INS = ["x", "norm_g", "w_in", "conv_w", "a_log", "dt_bias", "dn_norm_g", "w_out", "final_norm_g"]


def kernel(**inputs):
    import concourse.bacc as bacc
    from concourse.bass_utils import run_bass_kernel_spmd

    nc = bacc.Bacc("TRN2", target_bir_lowering=False, num_devices=1)
    arrays, args = {}, []
    for name in _INS:
        a = np.ascontiguousarray(inputs[name])
        arrays[f"in_{name}"] = a
        args.append(nc.dram_tensor(f"in_{name}", a.shape, mybir.dt.from_np(a.dtype), kind="ExternalInput").ap())
    table = constant_table()
    arrays["constants"] = table
    args.append(nc.dram_tensor("constants", table.shape, F32, kind="ExternalInput").ap())
    shape = inputs["x"].shape
    args.append(nc.dram_tensor("out", shape, F32, kind="ExternalOutput").ap())
    hybrid_layer(nc, *args)
    r = run_bass_kernel_spmd(nc, [arrays], core_ids=[0])
    return r.results[0]["out"]
```
